# Optimizing a Trainium2 kernel written in Bass

```python
import math
import jax, jax.numpy as jnp
from jax import lax
import numpy as np

D_MODEL = 1024
BATCH = 1
SEQ = 256
DEPTH = 2

HEAD_DIM = 64
N_HEAD_SLOTS = D_MODEL // HEAD_DIM
MIX_WIDTH = N_HEAD_SLOTS * HEAD_DIM
HEADS_PER_MIXER = N_HEAD_SLOTS // 2
KV_HEADS = 2
GROUP = HEADS_PER_MIXER // KV_HEADS
HQ = HEADS_PER_MIXER * HEAD_DIM
KVW = KV_HEADS * HEAD_DIM
Q_BLOCK = 128
NSA_CMP_LEN = 32
NSA_CMP_STRIDE = 16
NSA_SEL_LEN = 64
NSA_SEL_TOP = 8
NSA_WINDOW = 512
NSA_FORCE = 1e4
SWA_WINDOW = 128
MOBA_BLOCK = 256
MOBA_TOP = 3
MOBA_Q_CHUNK = 32
REL_BUCKETS = 32
REL_MAX_DIST = 128
D_FF = ((8 * D_MODEL // 3 + 255) // 256) * 256
RMS_EPS = 1e-6
NEG = -1e30
AB_WIDTH = HQ + 6 * KVW + 3 * HEADS_PER_MIXER + HQ + 2 * KVW
CD_WIDTH = HQ + 2 * KVW + 3 * HQ
N_EVEN = (DEPTH + 1) // 2
N_ODD = DEPTH // 2


def rms_norm(x, w):
    xf = x.astype(jnp.float32)
    y = xf * lax.rsqrt(jnp.mean(xf * xf, axis=-1, keepdims=True) + RMS_EPS)
    return (y * w.astype(jnp.float32)).astype(x.dtype)

def rel_bucket(dist):
    n = jnp.maximum(dist, 0)
    max_exact = REL_BUCKETS // 2
    nf = jnp.maximum(n, 1).astype(jnp.float32)
    large = max_exact + (jnp.log(nf / max_exact) / math.log(REL_MAX_DIST / max_exact)
                         * (REL_BUCKETS - max_exact)).astype(jnp.int32)
    large = jnp.minimum(large, REL_BUCKETS - 1)
    return jnp.where(n < max_exact, n, large)

def masked_softmax(s, valid):
    s = jnp.where(valid, s.astype(jnp.float32), NEG)
    p = jax.nn.softmax(s, axis=-1)
    return jnp.where(valid, p, 0.0)

def nsa_attention(q, k_cmp, v_cmp, k_sel, v_sel, k_win, v_win, gates, cmp_wk, cmp_wv, cmp_pe, rel_tab):
    B, S, H, dh = q.shape
    G, R = KV_HEADS, GROUP
    dt = q.dtype
    scale = HEAD_DIM ** -0.5
    n_cmp = (S - NSA_CMP_LEN) // NSA_CMP_STRIDE + 1
    cmp_start = jnp.arange(n_cmp) * NSA_CMP_STRIDE
    gidx = cmp_start[:, None] + jnp.arange(NSA_CMP_LEN)[None, :]
    kc = jnp.einsum('bnlgd,lde->bnge', k_cmp[:, gidx] + cmp_pe[:, None, :], cmp_wk)
    vc = jnp.einsum('bnlgd,lde->bnge', v_cmp[:, gidx] + cmp_pe[:, None, :], cmp_wv)
    cmp_end = cmp_start + NSA_CMP_LEN - 1
    n_sel = S // NSA_SEL_LEN
    sel_start = jnp.arange(n_sel) * NSA_SEL_LEN
    overlap = jnp.maximum(jnp.minimum(cmp_end[:, None] + 1, sel_start[None, :] + NSA_SEL_LEN)
                          - jnp.maximum(cmp_start[:, None], sel_start[None, :]), 0)
    overlap_w = overlap.astype(jnp.float32) / NSA_CMP_LEN
    top = min(NSA_SEL_TOP, n_sel)
    ksb = k_sel.reshape(B, n_sel, NSA_SEL_LEN, G, dh).transpose(0, 3, 1, 2, 4)
    vsb = v_sel.reshape(B, n_sel, NSA_SEL_LEN, G, dh).transpose(0, 3, 1, 2, 4)
    kw = jnp.pad(k_win, ((0, 0), (NSA_WINDOW, 0), (0, 0), (0, 0)))
    vw = jnp.pad(v_win, ((0, 0), (NSA_WINDOW, 0), (0, 0), (0, 0)))
    bi = jnp.arange(B)[:, None, None, None]
    gi = jnp.arange(G)[None, :, None, None]
    sb = jnp.arange(n_sel)

    def block(n):
        t0 = n * Q_BLOCK
        tq = t0 + jnp.arange(Q_BLOCK)
        qb = lax.dynamic_slice_in_dim(q, t0, Q_BLOCK, axis=1).reshape(B, Q_BLOCK, G, R, dh)
        gb = lax.dynamic_slice_in_dim(gates, t0, Q_BLOCK, axis=1).reshape(B, Q_BLOCK, G, R, 1, 3)
        dist = tq[:, None] - cmp_end[None, :]
        s = jnp.einsum('bqgrd,bngd->bgrqn', qb, kc) * scale
        s = s + rel_tab[rel_bucket(dist)].transpose(2, 3, 0, 1)
        p_cmp = masked_softmax(s, dist >= 0)
        o_cmp = jnp.einsum('bgrqn,bngd->bqgrd', p_cmp.astype(dt), vc)
        imp = jnp.einsum('bgrqn,ns->bgqs', p_cmp, overlap_w)
        own = tq // NSA_SEL_LEN
        forced = (sb[None, :] == 0) | (sb[None, :] == own[:, None]) | (sb[None, :] == own[:, None] - 1)
        causal_blk = sb[None, :] <= own[:, None]
        imp = jnp.where(causal_blk, imp + jnp.where(forced, NSA_FORCE, 0.0), NEG)
        _, sel = lax.top_k(imp, top)
        ks = ksb[bi, gi, sel].reshape(B, G, Q_BLOCK, top * NSA_SEL_LEN, dh)
        vs = vsb[bi, gi, sel].reshape(B, G, Q_BLOCK, top * NSA_SEL_LEN, dh)
        pos = (sel[..., None] * NSA_SEL_LEN + jnp.arange(NSA_SEL_LEN)).reshape(B, G, Q_BLOCK, top * NSA_SEL_LEN)
        dist = tq[None, None, :, None] - pos
        s = jnp.einsum('bqgrd,bgqkd->bgrqk', qb, ks) * scale
        s = s + rel_tab[rel_bucket(dist), gi].transpose(0, 1, 4, 2, 3)
        p = masked_softmax(s, (dist >= 0)[:, :, None])
        o_sel = jnp.einsum('bgrqk,bgqkd->bqgrd', p.astype(dt), vs)
        kwb = lax.dynamic_slice_in_dim(kw, t0, NSA_WINDOW + Q_BLOCK, axis=1)
        vwb = lax.dynamic_slice_in_dim(vw, t0, NSA_WINDOW + Q_BLOCK, axis=1)
        kpos = t0 - NSA_WINDOW + jnp.arange(NSA_WINDOW + Q_BLOCK)
        dist = tq[:, None] - kpos[None, :]
        valid = (dist >= 0) & (dist < NSA_WINDOW) & (kpos[None, :] >= 0)
        s = jnp.einsum('bqgrd,bkgd->bgrqk', qb, kwb) * scale
        s = s + rel_tab[rel_bucket(dist)].transpose(2, 3, 0, 1)
        p = masked_softmax(s, valid)
        o_win = jnp.einsum('bgrqk,bkgd->bqgrd', p.astype(dt), vwb)
        o = jnp.stack([o_cmp, o_sel, o_win], axis=-1)
        return jnp.sum(o * gb, axis=-1).reshape(B, Q_BLOCK, H * dh)

    out = lax.map(block, jnp.arange(S // Q_BLOCK))
    return out.transpose(1, 0, 2, 3).reshape(B, S, H * dh)

def swa_sink_attention(q, k, v, sinks, rel_tab):
    B, S, H, dh = q.shape
    G, R = KV_HEADS, GROUP
    dt = q.dtype
    scale = HEAD_DIM ** -0.5
    kp = jnp.pad(k, ((0, 0), (SWA_WINDOW, 0), (0, 0), (0, 0)))
    vp = jnp.pad(v, ((0, 0), (SWA_WINDOW, 0), (0, 0), (0, 0)))
    sink = jnp.broadcast_to(sinks.astype(jnp.float32).reshape(G, R)[None, :, :, None, None],
                            (B, G, R, Q_BLOCK, 1))

    def block(n):
        t0 = n * Q_BLOCK
        tq = t0 + jnp.arange(Q_BLOCK)
        qb = lax.dynamic_slice_in_dim(q, t0, Q_BLOCK, axis=1).reshape(B, Q_BLOCK, G, R, dh)
        kb = lax.dynamic_slice_in_dim(kp, t0, SWA_WINDOW + Q_BLOCK, axis=1)
        vb = lax.dynamic_slice_in_dim(vp, t0, SWA_WINDOW + Q_BLOCK, axis=1)
        kpos = t0 - SWA_WINDOW + jnp.arange(SWA_WINDOW + Q_BLOCK)
        dist = tq[:, None] - kpos[None, :]
        valid = (dist >= 0) & (dist < SWA_WINDOW) & (kpos[None, :] >= 0)
        s = jnp.einsum('bqgrd,bkgd->bgrqk', qb, kb) * scale
        s = s + rel_tab[rel_bucket(dist)].transpose(2, 3, 0, 1)
        s = jnp.where(valid, s.astype(jnp.float32), NEG)
        p = jax.nn.softmax(jnp.concatenate([s, sink], axis=-1), axis=-1)[..., :-1]
        o = jnp.einsum('bgrqk,bkgd->bqgrd', p.astype(dt), vb)
        return o.reshape(B, Q_BLOCK, H * dh)

    out = lax.map(block, jnp.arange(S // Q_BLOCK))
    return out.transpose(1, 0, 2, 3).reshape(B, S, H * dh)

def moba_attention(q, k, v, rel_tab_h):
    B, S, H, dh = q.shape
    G, R = KV_HEADS, GROUP
    L = MOBA_BLOCK
    dt = q.dtype
    scale = HEAD_DIM ** -0.5
    nb = max(-(-S // L), 2)
    pad = nb * L - S
    kp = jnp.pad(k, ((0, 0), (0, pad), (0, 0), (0, 0)))
    vp = jnp.pad(v, ((0, 0), (0, pad), (0, 0), (0, 0)))
    head_grp = jnp.arange(H) // R
    kb = kp.reshape(B, nb, L, G, dh)
    k_mean = jnp.mean(kb.astype(jnp.float32), axis=2).astype(dt)[:, :, head_grp]
    kbh = kb[:, :, :, head_grp].transpose(0, 3, 1, 2, 4)
    vbh = vp.reshape(B, nb, L, G, dh)[:, :, :, head_grp].transpose(0, 3, 1, 2, 4)
    top = min(MOBA_TOP, nb - 1)
    bi = jnp.arange(B)[:, None, None, None]
    hi = jnp.arange(H)[None, None, :, None]
    Qc = MOBA_Q_CHUNK

    def chunk(n):
        t0 = n * Qc
        tq = t0 + jnp.arange(Qc)
        qc = lax.dynamic_slice_in_dim(q, t0, Qc, axis=1)
        own = t0 // L
        gs = jnp.einsum('bqhd,bnhd->bqhn', qc, k_mean).astype(jnp.float32)
        gs = jnp.where(jnp.arange(nb) < own, gs, NEG)
        _, sel = lax.top_k(gs, top)
        sel_ok = sel < own
        ks = kbh[bi, hi, sel]
        vs = vbh[bi, hi, sel]
        pos = sel[..., None] * L + jnp.arange(L)
        s_past = jnp.einsum('bqhd,bqhnld->bqhnl', qc, ks) * scale
        s_past = s_past + rel_tab_h[rel_bucket(tq[None, :, None, None, None] - pos), hi[..., None]]
        k_own = lax.dynamic_slice_in_dim(kp, own * L, L, axis=1)[:, :, head_grp]
        v_own = lax.dynamic_slice_in_dim(vp, own * L, L, axis=1)[:, :, head_grp]
        dist_own = tq[:, None] - (own * L + jnp.arange(L))[None, :]
        s_own = jnp.einsum('bqhd,blhd->bqhl', qc, k_own) * scale
        s_own = s_own + rel_tab_h[rel_bucket(dist_own)].transpose(0, 2, 1)
        s = jnp.concatenate([s_past.reshape(B, Qc, H, top * L), s_own], axis=-1)
        valid = jnp.concatenate([
            jnp.broadcast_to(sel_ok[..., None], (B, Qc, H, top, L)).reshape(B, Qc, H, top * L),
            jnp.broadcast_to((dist_own >= 0)[:, None, :], (B, Qc, H, L))], axis=-1)
        p = masked_softmax(s, valid).astype(dt)
        o = (jnp.einsum('bqhk,bqhkd->bqhd', p[..., :top * L], vs.reshape(B, Qc, H, top * L, dh))
             + jnp.einsum('bqhl,blhd->bqhd', p[..., top * L:], v_own))
        return o.reshape(B, Qc, H * dh)

    out = lax.map(chunk, jnp.arange(S // Qc))
    return out.transpose(1, 0, 2, 3).reshape(B, S, H * dh)

def stick_breaking_attention(q, k, v):
    B, S, H, dh = q.shape
    dt = q.dtype
    scale = HEAD_DIM ** -0.5
    kpos = jnp.arange(S)

    def block(n):
        t0 = n * Q_BLOCK
        tq = t0 + jnp.arange(Q_BLOCK)
        qb = lax.dynamic_slice_in_dim(q, t0, Q_BLOCK, axis=1)
        z = jnp.einsum('bqhd,bkhd->bhqk', qb, k).astype(jnp.float32) * scale
        strict = kpos[None, :] < tq[:, None]
        log_1m = jnp.where(strict, jax.nn.log_sigmoid(-z), 0.0)
        after = lax.cumsum(log_1m, axis=3, reverse=True) - log_1m
        w = jnp.where(strict, jnp.exp(jax.nn.log_sigmoid(z) + after), 0.0)
        o = jnp.einsum('bhqk,bkhd->bqhd', w.astype(dt), v)
        return o.reshape(B, Q_BLOCK, H * dh)

    out = lax.map(block, jnp.arange(S // Q_BLOCK))
    return out.transpose(1, 0, 2, 3).reshape(B, S, H * dh)

def mixer_ab(h, w_in, w_out, cmp_wk, cmp_wv, cmp_pe, sinks, rel_table):
    B, S, _ = h.shape
    H, G, dh = HEADS_PER_MIXER, KV_HEADS, HEAD_DIM
    proj = h @ w_in
    sizes = [HQ, KVW, KVW, KVW, KVW, KVW, KVW, 3 * H, HQ, KVW, KVW]
    qa, kca, vca, ksa, vsa, kwa, vwa, ga, qb, kb, vb = jnp.split(proj, np.cumsum(sizes)[:-1].tolist(), axis=-1)
    kv = lambda t: t.reshape(B, S, G, dh)
    gates = jax.nn.sigmoid(ga.astype(jnp.float32)).astype(h.dtype).reshape(B, S, H, 3)
    tab_a = rel_table[:, :H].reshape(REL_BUCKETS, G, GROUP)
    tab_b = rel_table[:, H:2 * H].reshape(REL_BUCKETS, G, GROUP)
    o_a = nsa_attention(qa.reshape(B, S, H, dh), kv(kca), kv(vca), kv(ksa), kv(vsa), kv(kwa), kv(vwa),
                        gates, cmp_wk, cmp_wv, cmp_pe, tab_a)
    o_b = swa_sink_attention(qb.reshape(B, S, H, dh), kv(kb), kv(vb), sinks, tab_b)
    return jnp.concatenate([o_a, o_b], axis=-1) @ w_out

def mixer_cd(h, w_in, w_out, rel_table):
    B, S, _ = h.shape
    H, G, dh = HEADS_PER_MIXER, KV_HEADS, HEAD_DIM
    proj = h @ w_in
    sizes = [HQ, KVW, KVW, HQ, HQ, HQ]
    qc, kc, vc, qd, kd, vd = jnp.split(proj, np.cumsum(sizes)[:-1].tolist(), axis=-1)
    o_c = moba_attention(qc.reshape(B, S, H, dh), kc.reshape(B, S, G, dh), vc.reshape(B, S, G, dh),
                         rel_table[:, :H])
    o_d = stick_breaking_attention(qd.reshape(B, S, H, dh), kd.reshape(B, S, H, dh), vd.reshape(B, S, H, dh))
    return jnp.concatenate([o_c, o_d], axis=-1) @ w_out

def swiglu(h, w_in, w_out):
    gate, up = jnp.split(h @ w_in, 2, axis=-1)
    return (jax.nn.silu(gate) * up) @ w_out

def first_inputs(seed: int = 0) -> dict:
    key = jax.random.key(seed)
    ks = jax.random.split(key, 16)
    f32 = jnp.float32

    def nrm(k, shape, s):
        return jax.random.normal(k, shape, f32) * s

    return {
        "x": nrm(ks[0], (BATCH, SEQ, D_MODEL), 1.0),
        "c": nrm(ks[1], (BATCH, D_MODEL), 1.0),
        "rel_table": nrm(ks[2], (REL_BUCKETS, N_HEAD_SLOTS), 0.5),
        "mod_w": nrm(ks[3], (DEPTH, 2, D_MODEL, 3 * D_MODEL), 0.5 * D_MODEL ** -0.5),
        "mod_b": nrm(ks[4], (DEPTH, 2, 3 * D_MODEL), 0.02),
        "norm_w": 1.0 + nrm(ks[5], (DEPTH, 2, 2, D_MODEL), 0.02),
        "w_in_ab": nrm(ks[6], (N_EVEN, D_MODEL, AB_WIDTH), D_MODEL ** -0.5),
        "w_out_ab": nrm(ks[7], (N_EVEN, MIX_WIDTH, D_MODEL), MIX_WIDTH ** -0.5),
        "nsa_cmp_wk": nrm(ks[8], (N_EVEN, NSA_CMP_LEN, HEAD_DIM, HEAD_DIM), (NSA_CMP_LEN * HEAD_DIM) ** -0.5),
        "nsa_cmp_wv": nrm(ks[9], (N_EVEN, NSA_CMP_LEN, HEAD_DIM, HEAD_DIM), (NSA_CMP_LEN * HEAD_DIM) ** -0.5),
        "nsa_cmp_pe": nrm(ks[10], (N_EVEN, NSA_CMP_LEN, HEAD_DIM), 0.1),
        "swa_sinks": nrm(ks[11], (N_EVEN, HEADS_PER_MIXER), 0.5),
        "w_in_cd": nrm(ks[12], (N_ODD, D_MODEL, CD_WIDTH), D_MODEL ** -0.5),
        "w_out_cd": nrm(ks[13], (N_ODD, MIX_WIDTH, D_MODEL), MIX_WIDTH ** -0.5),
        "ffn_w_in": nrm(ks[14], (DEPTH, D_MODEL, 2 * D_FF), D_MODEL ** -0.5),
        "ffn_w_out": nrm(ks[15], (DEPTH, D_FF, D_MODEL), D_FF ** -0.5),
    }

def first_block(x, c, rel_table, mod_w, mod_b, norm_w, w_in_ab, w_out_ab, nsa_cmp_wk, nsa_cmp_wv,
              nsa_cmp_pe, swa_sinks, w_in_cd, w_out_cd, ffn_w_in, ffn_w_out):
    for layer in range(DEPTH):
        shift, scale, gate = jnp.split((c @ mod_w[layer, 0] + mod_b[layer, 0])[:, None, :], 3, axis=-1)
        h = rms_norm(x, norm_w[layer, 0, 0]) * (1.0 + scale) + shift
        i = layer // 2
        if layer % 2 == 0:
            y = mixer_ab(h, w_in_ab[i], w_out_ab[i], nsa_cmp_wk[i], nsa_cmp_wv[i], nsa_cmp_pe[i],
                         swa_sinks[i], rel_table)
        else:
            y = mixer_cd(h, w_in_cd[i], w_out_cd[i], rel_table)
        x = x + gate * rms_norm(y, norm_w[layer, 0, 1])
        shift, scale, gate = jnp.split((c @ mod_w[layer, 1] + mod_b[layer, 1])[:, None, :], 3, axis=-1)
        h = rms_norm(x, norm_w[layer, 1, 0]) * (1.0 + scale) + shift
        y = swiglu(h, ffn_w_in[layer], ffn_w_out[layer])
        x = x + gate * rms_norm(y, norm_w[layer, 1, 1])
    return x


DEPTH_2 = 1

MIX_WIDTH_2 = D_MODEL
ATTN_WIDTH = MIX_WIDTH_2 // 2
N_Q_HEADS = ATTN_WIDTH // HEAD_DIM
N_KV_HEADS = 2
KV_WIDTH = N_KV_HEADS * HEAD_DIM
TOK_WIDTH = MIX_WIDTH_2 - ATTN_WIDTH
N_TOK_HEADS = TOK_WIDTH // HEAD_DIM
N_IN = ATTN_WIDTH + 2 * KV_WIDTH + 2 * TOK_WIDTH
CHUNK = 128
GRID_W = 64
ROPE_THETA = 10000.0
D_FF_2 = 2816
CONV_W = 3
N_MOD = 6
EPS = 1e-6


def rmsnorm(x, g):
    xf = x.astype(jnp.float32)
    y = xf * lax.rsqrt(jnp.mean(xf * xf, axis=-1, keepdims=True) + EPS)
    return (y * g.astype(jnp.float32)).astype(x.dtype)

def axial_rope_tables(seq_len):
    rows = seq_len // GRID_W
    row_id = jnp.broadcast_to(jnp.arange(rows)[:, None], (rows, GRID_W)).reshape(-1).astype(jnp.float32)
    col_id = jnp.broadcast_to(jnp.arange(GRID_W)[None, :], (rows, GRID_W)).reshape(-1).astype(jnp.float32)
    axis_dim = HEAD_DIM // 2
    inv_freq = jnp.power(jnp.float32(ROPE_THETA), -jnp.arange(0, axis_dim, 2, dtype=jnp.float32) / axis_dim)
    ang_r = row_id[:, None] * inv_freq[None, :]
    ang_c = col_id[:, None] * inv_freq[None, :]
    ang = jnp.concatenate([ang_r, ang_r, ang_c, ang_c], axis=-1)
    return jnp.cos(ang), jnp.sin(ang)

def rotate_half(a):
    a1, a2 = jnp.split(a, 2, axis=-1)
    return jnp.concatenate([-a2, a1], axis=-1)

def apply_axial_rope(x, cos, sin):
    xr, xc = jnp.split(x, 2, axis=-1)
    rot = jnp.concatenate([rotate_half(xr), rotate_half(xc)], axis=-1)
    return x * cos + rot * sin

def block_attention(q, k, v):
    B, S = q.shape[0], q.shape[1]
    groups = N_Q_HEADS // N_KV_HEADS
    nb = S // Q_BLOCK
    qb = q.reshape(B, nb, Q_BLOCK, N_KV_HEADS, groups, HEAD_DIM).transpose(1, 0, 2, 3, 4, 5)
    scale = jnp.float32(HEAD_DIM ** -0.5)

    def one_block(qi):
        s = jnp.einsum('bqkgd,bskd->bkgqs', qi, k, preferred_element_type=jnp.float32) * scale
        p = jax.nn.softmax(s, axis=-1)
        return jnp.einsum('bkgqs,bskd->bqkgd', p.astype(v.dtype), v)

    ob = lax.map(one_block, qb)
    return ob.transpose(1, 0, 2, 3, 4, 5).reshape(B, S, ATTN_WIDTH)

def chunked_token_mlp(z, g_v, w_s, b_s):
    B, S = z.shape[0], z.shape[1]
    nc = S // CHUNK
    z = jax.nn.gelu(z)
    u, v = jnp.split(z, 2, axis=-1)
    v = rmsnorm(v.reshape(B, S, N_TOK_HEADS, HEAD_DIM), g_v)
    v = v.reshape(B, nc, CHUNK, N_TOK_HEADS, HEAD_DIM)
    mixed = jnp.einsum('hpq,bcqhd->bcphd', w_s, v) + b_s.T[None, None, :, :, None]
    out = u.reshape(B, nc, CHUNK, N_TOK_HEADS, HEAD_DIM) * mixed
    return out.reshape(B, S, TOK_WIDTH)

def conv_glu_ffn(h, w_up, w_conv, b_conv, w_down):
    z = h @ w_up
    zp = jnp.pad(z, ((0, 0), (1, 1), (0, 0)))
    z = zp[:, :-2] * w_conv[0] + zp[:, 1:-1] * w_conv[1] + zp[:, 2:] * w_conv[2] + b_conv
    a, b = jnp.split(z, 2, axis=-1)
    return (jax.nn.silu(a) * b) @ w_down

def second_inputs(seed: int = 0) -> dict:
    key = jax.random.key(seed)
    ks = jax.random.split(key, 24)
    f32 = jnp.float32
    L, D = DEPTH_2, D_MODEL

    def nrm(k, shape, scale):
        return jax.random.normal(k, shape, f32) * scale

    def gain(k, shape):
        return 1.0 + 0.05 * jax.random.normal(k, shape, f32)

    return {
        "x": nrm(ks[0], (BATCH, SEQ, D), 1.0),
        "c": nrm(ks[1], (BATCH, D), 1.0),
        "w_ada": nrm(ks[2], (L, D, N_MOD * D), 0.5 * D ** -0.5),
        "b_ada": nrm(ks[3], (L, N_MOD * D), 0.01),
        "g_norm1": gain(ks[4], (L, D)),
        "w_in": nrm(ks[5], (L, D, N_IN), D ** -0.5),
        "g_q": gain(ks[6], (L, HEAD_DIM)),
        "g_k": gain(ks[7], (L, HEAD_DIM)),
        "g_tok_v": gain(ks[8], (L, HEAD_DIM)),
        "w_s": nrm(ks[9], (L, N_TOK_HEADS, CHUNK, CHUNK), CHUNK ** -0.5),
        "b_s": 1.0 + nrm(ks[10], (L, N_TOK_HEADS, CHUNK), 0.01),
        "g_attn_out": gain(ks[11], (L, ATTN_WIDTH)),
        "g_tok_out": gain(ks[12], (L, TOK_WIDTH)),
        "w_out": nrm(ks[13], (L, MIX_WIDTH_2, D), MIX_WIDTH_2 ** -0.5),
        "g_norm2": gain(ks[14], (L, D)),
        "w_up": nrm(ks[15], (L, D, 2 * D_FF_2), D ** -0.5),
        "w_conv": nrm(ks[16], (L, CONV_W, 2 * D_FF_2), CONV_W ** -0.5),
        "b_conv": nrm(ks[17], (L, 2 * D_FF_2), 0.01),
        "w_down": nrm(ks[18], (L, D_FF_2, D), D_FF_2 ** -0.5),
        "g_final": gain(ks[19], (D,)),
    }

def second_block(x, c, w_ada, b_ada, g_norm1, w_in, g_q, g_k, g_tok_v, w_s, b_s,
              g_attn_out, g_tok_out, w_out, g_norm2, w_up, w_conv, b_conv, w_down, g_final):
    B, S, _ = x.shape
    cos, sin = axial_rope_tables(S)
    cos = cos.astype(x.dtype)[None, :, None, :]
    sin = sin.astype(x.dtype)[None, :, None, :]
    mod_all = jnp.einsum('bd,ldm->lbm', jax.nn.silu(c), w_ada) + b_ada[:, None, :]

    for l in range(DEPTH_2):
        sh1, sc1, gt1, sh2, sc2, gt2 = jnp.split(mod_all[l][:, None, :], N_MOD, axis=-1)

        h = rmsnorm(x, g_norm1[l]) * (1.0 + sc1) + sh1
        proj = h @ w_in[l]
        q, k, v, z = jnp.split(
            proj, [ATTN_WIDTH, ATTN_WIDTH + KV_WIDTH, ATTN_WIDTH + 2 * KV_WIDTH], axis=-1)
        q = rmsnorm(q.reshape(B, S, N_Q_HEADS, HEAD_DIM), g_q[l])
        k = rmsnorm(k.reshape(B, S, N_KV_HEADS, HEAD_DIM), g_k[l])
        q = apply_axial_rope(q, cos, sin)
        k = apply_axial_rope(k, cos, sin)
        v = v.reshape(B, S, N_KV_HEADS, HEAD_DIM)
        attn = block_attention(q, k, v)
        tok = chunked_token_mlp(z, g_tok_v[l], w_s[l], b_s[l])
        mixed = jnp.concatenate(
            [rmsnorm(attn, g_attn_out[l]), rmsnorm(tok, g_tok_out[l])], axis=-1)
        x = x + gt1 * (mixed @ w_out[l])

        h = rmsnorm(x, g_norm2[l]) * (1.0 + sc2) + sh2
        x = x + gt2 * conv_glu_ffn(h, w_up[l], w_conv[l], b_conv[l], w_down[l])

    return rmsnorm(x, g_final)


def setup_inputs(seed=0):
    out = dict(first_inputs(seed))
    for name, value in second_inputs(seed + 1).items():
        if name != "x":
            out[name + "_2"] = value
    return out


def reference(
    x, c, rel_table, mod_w, mod_b, norm_w, w_in_ab, w_out_ab, nsa_cmp_wk, nsa_cmp_wv,
    nsa_cmp_pe, swa_sinks, w_in_cd, w_out_cd, ffn_w_in, ffn_w_out, c_2, w_ada_2, b_ada_2,
    g_norm1_2, w_in_2, g_q_2, g_k_2, g_tok_v_2, w_s_2, b_s_2, g_attn_out_2, g_tok_out_2,
    w_out_2, g_norm2_2, w_up_2, w_conv_2, b_conv_2, w_down_2, g_final_2,
):
    x = first_block(
        x, c, rel_table, mod_w, mod_b, norm_w, w_in_ab, w_out_ab, nsa_cmp_wk, nsa_cmp_wv,
        nsa_cmp_pe, swa_sinks, w_in_cd, w_out_cd, ffn_w_in, ffn_w_out,
    )
    return second_block(
        x, c_2, w_ada_2, b_ada_2, g_norm1_2, w_in_2, g_q_2, g_k_2, g_tok_v_2, w_s_2, b_s_2,
        g_attn_out_2, g_tok_out_2, w_out_2, g_norm2_2, w_up_2, w_conv_2, b_conv_2, w_down_2,
        g_final_2,
    )


_drawn_inputs = setup_inputs


def setup_inputs(seed=0):
    import zlib

    import numpy as np

    out = dict(_drawn_inputs(seed))
    spreads = {}
    factors = {'swa_sinks': 8.0,
     'b_ada_2': 5.744,
     'g_norm1_2': 5.083,
     'g_q_2': 8.0,
     'g_k_2': 8.0,
     'g_tok_v_2': 8.0,
     'b_s_2': 8.0,
     'g_attn_out_2': 7.397,
     'g_tok_out_2': 7.247,
     'g_norm2_2': 5.274,
     'b_conv_2': 8.0}
    for name, (base, spread) in spreads.items():
        noise = np.random.default_rng([zlib.crc32(name.encode()), seed]).standard_normal(out[name].shape)
        drawn = base * np.exp(spread * noise) if base else spread * noise
        out[name] = __import__('jax').numpy.asarray(drawn.astype(out[name].dtype))
    for name, factor in factors.items():
        out[name] = (out[name] * factor).astype(out[name].dtype)
    return out
```

```python
import math
from contextlib import ExitStack

import numpy as np

import concourse.bass as bass
from concourse import mybir

F32 = mybir.dt.float32
F32R = mybir.dt.float32r
ALU = mybir.AluOpType
ACT = mybir.ActivationFunctionType
AX = mybir.AxisListType.X

P = 128
D = 1024
KT = D // P
S = 256
QT = S // P
HD = 64
H = 8
G = 2
FF = 2816
FT = FF // P
REL = 32
NCMP, CLEN, CSTR = 15, 32, 16
EPS = 1e-6
BIG = 1e30
UW = 1024
COPIES = 16
RING = 6
MW = 3 * D
MC = MW // 2

AB_UNITS, CD_UNITS, SB_UNITS = 24, 27, 24
FFN_UNITS = 3 * FT
BASE = {}
_p = 0
for _name, _n in (("ab", AB_UNITS), ("f0", FFN_UNITS), ("cd", CD_UNITS), ("f1", FFN_UNITS),
                  ("sb", SB_UNITS), ("f2", FFN_UNITS)):
    BASE[_name] = _p
    _p += _n
N_UNITS = _p

CONST = {}
_c = 0
for _name, _n in (("ident", P), ("ones", P), ("blockones", P), ("rot", P), ("tri", P), ("neg1", P),
                  ("cos", S), ("sin", S), ("stickmask", 3 * P), ("cmpmask", QT * 16),
                  ("rowvalid", QT), ("select", P), ("headmask", H)):
    CONST[_name] = (_c, _n)
    _c += _n
CONST_COLS = _c
EARLY = {}
_c = 0
for _name, _n in (("onehot_cmp", 4 * S), ("onehot_rel", 512), ("negmask", 512)):
    EARLY[_name] = (_c, _n)
    _c += _n
EARLY_COLS = _c
PARAM = {}
_c = 0
for _name, _n in (("c", 2 * KT), ("modb", 6 * 24), ("normw", 11 * KT), ("gout", 8), ("gqk", 2),
                  ("gtokv", HD), ("sinks", H), ("pe", CLEN), ("wga", KT * 24), ("conv", FT * 8),
                  ("bs", 4 * P), ("reltab", 16), ("relblock", 32)):
    PARAM[_name] = (_c, _n)
    _c += _n
PARAM_COLS = _c


def rel_bucket(dist):
    n = np.maximum(dist, 0)
    nf = np.maximum(n, 1).astype(np.float32)
    large = 16 + (np.log(nf / np.float32(16)) / np.float32(math.log(8.0)) * np.float32(16)).astype(np.int32)
    return np.where(n < 16, n, np.minimum(large, 31))


def shape_constants():
    c = np.zeros((P, CONST_COLS), np.float32)
    e = np.zeros((P, EARLY_COLS), np.float32)

    def put(name, a, to=c, where=CONST):
        at, n = where[name]
        a = np.asarray(a, np.float32).reshape(a.shape[0], -1)
        assert a.shape[1] == n, name
        to[:a.shape[0], at:at + n] = a

    i = np.arange(P)
    put("ident", np.eye(P))
    put("ones", np.ones((P, P)))
    put("blockones", (i[:, None] // HD == i[None, :] // HD).astype(np.float32))
    rot = np.zeros((P, P), np.float32)
    for m in range(P):
        if m % 32 < 16:
            rot[m + 16, m] = -1.0
        else:
            rot[m - 16, m] = 1.0
    put("rot", rot)
    put("tri", -(i[:, None] >= i[None, :]).astype(np.float32))
    put("neg1", -np.ones((P, P)))
    t = np.arange(S)
    inv = np.power(np.float32(10000.0), -np.arange(0, 32, 2, dtype=np.float32) / np.float32(32))
    ang_r = (t // 64).astype(np.float32)[:, None] * inv[None]
    ang_c = (t % 64).astype(np.float32)[:, None] * inv[None]
    ang = np.concatenate([ang_r, ang_r, ang_c, ang_c] * 2, -1).T
    put("cos", np.cos(ang))
    put("sin", np.sin(ang))
    tri = np.where(i[:, None] < i[None, :], 0.0, -BIG)
    put("stickmask", np.concatenate([tri, np.zeros((P, P)), tri], 1))
    q = np.arange(S)
    n = np.arange(16)
    dist = q[:, None] - (CSTR * n + CLEN - 1)[None]
    ok = (dist >= 0) & (n < NCMP)[None]
    put("cmpmask", np.where(ok, 0.0, BIG).reshape(QT, P, 16).transpose(1, 0, 2))
    put("rowvalid", ok.any(1).astype(np.float32).reshape(QT, P).T)
    sel = np.zeros((NCMP, P), np.float32)
    for h in range(H):
        for m in range(NCMP):
            sel[m, h * 16 + m] = 1.0
    put("select", sel)
    put("headmask", (i[:, None] // 16 == np.arange(H)[None]).astype(np.float32))
    hot = np.zeros((4, REL, 4, S), np.float32)
    for m in range(NCMP):
        hot[m % 4, rel_bucket(dist[:, m]), m // 4, q] = 1.0
    put("onehot_cmp", hot.reshape(P, 4 * S), e, EARLY)
    far = 255 - np.arange(512)
    hot = np.zeros((REL, 512), np.float32)
    hot[rel_bucket(far), np.arange(512)] = 1.0
    put("onehot_rel", hot, e, EARLY)
    neg = np.zeros((16, 512), np.float32)
    neg[:, far < 0] = BIG
    neg[8:, far >= 128] = BIG
    put("negmask", neg, e, EARLY)
    return c, e


class Count:

    def __init__(self, sem):
        self.sem, self.n, self.i, self.per = sem, 0, None, 0

    def inc(self, ins):
        ins.then_inc(self.sem, 1)
        self.n += 1
        return ins

    def now(self):
        return self.n if self.i is None else self.i * self.per + self.n

    def enter(self, i, per):
        self.i, self.per, self.first = i, per, self.n

    def leave(self, turns):
        assert self.n - self.first == self.per, (self.n - self.first, self.per)
        self.n = self.first + turns * self.per
        self.i = None


def build_program(nc, A):
    with ExitStack() as ctx:
        def sb(name, shape, dt=F32):
            return ctx.enter_context(nc.sbuf_tensor(name, shape, dt))

        def sem(name):
            return ctx.enter_context(nc.semaphore(name))

        x = sb("x", [P, KT, S])
        hH = sb("hH", [P, KT, S], F32R)
        hL = sb("hL", [P, KT, S], F32R)
        raw = sb("raw", [P, RING, UW])
        wH = sb("wH", [P, RING, UW], F32R)
        wL = sb("wL", [P, RING, UW], F32R)
        modbuf = sb("modbuf", [P, 2, MC])
        acc0 = sb("acc0", [P, MW])
        proj = sb("proj", [P, 13, S])
        acc1 = proj[:, :, :].rearrange("p a b -> p (a b)")[:, 0:MW]
        early = proj[:, :, :].rearrange("p a b -> p (a b)")[:, 0:EARLY_COLS]
        vt = sb("vt", [P, QT, 5, P])
        strips = sb("strips", [P, 16, S])
        cw = strips[:, :, :].rearrange("p (g a) b -> p g (a b)", g=G).rearrange(
            "p g (l e) -> p g l e", e=HD)
        wst = strips[:, 0:4, :].rearrange("p a (b c) -> p (a b) c", b=2)
        bc = sb("bc", [P, QT, 16, H])
        otok = sb("otok", [P, QT, D])
        tt = otok[:, :, :].rearrange("p q (k s) -> p (q k) s", s=S)
        sn = sb("sn", [P, 2, 512])
        pr = sb("pr", [P, 2, 512])
        pt = sb("pt", [P, 2, 512])
        sq = sb("sq", [P, 2, 512])
        lnms = sb("lnms", [P, S])
        rstd = sb("rstd", [P, S])
        aH = sb("aH", [P, 2, S], F32R)
        aL = sb("aL", [P, 2, S], F32R)
        gwH = sb("gwH", [P, KT, 24], F32R)
        gwL = sb("gwL", [P, KT, 24], F32R)
        con = sb("con", [P, CONST_COLS])
        par = sb("par", [P, PARAM_COLS])
        mv = sb("mv", [P, 6, 24])
        sc1 = sb("sc1", [P, 6, KT])
        gw1 = sb("gw1", [P, 6, KT])
        csil = sb("csil", [P, KT])
        epst = sb("epst", [P, 1])
        nm = sb("nm", [P, 48, QT])
        sm = sb("sm", [P, 48, QT])
        rg = sb("rg", [P, H, QT])
        gt = sb("gt", [P, QT, 24])
        nsink = sb("nsink", [P, H])
        qgain = sb("qgain", [P, 1])
        sinkx = sb("sinkx", [P, H, QT])
        kc = sb("kc", [P, 16])
        kcs = sb("kcs", [16, P])
        vcs = sb("vcs", [16, P])
        cm = sb("cm", [P, 3, 16])
        small = sb("small", [P, 64])

        bank = [ctx.enter_context(nc.psum_tensor(f"bank{i}", [P, 512], F32)) for i in range(8)]

        def const(name, rows=P):
            at, n = CONST[name]
            return con[0:rows, at:at + n]

        def param(name, rows=P):
            at, n = PARAM[name]
            return par[0:rows, at:at + n]

        def early_const(name, rows=P):
            at, n = EARLY[name]
            return early[0:rows, at:at + n]

        ident, ones = const("ident"), const("ones")
        normw = param("normw").rearrange("p (n k) -> p n k", k=KT)
        modb = param("modb").rearrange("p (m j) -> p m j", j=24)
        cvec = param("c").rearrange("p (n k) -> p n k", k=KT)
        conv = param("conv").rearrange("p (t c) -> p t c", c=8)
        xfl = x[:, :, :].rearrange("p k s -> p (k s)")
        hHf = hH[:, :, :].rearrange("p k s -> p (k s)")
        hLf = hL[:, :, :].rearrange("p k s -> p (k s)")
        ttf = tt.rearrange("p k s -> p (k s)")

        small_landed = sem("small_landed")
        x_landed = sem("x_landed")
        early_landed = sem("early_landed")
        raw_full = [sem(f"raw_full{i}") for i in range(RING)]
        hi_ready = [sem(f"hi_ready{i}") for i in range(3)]
        lo_ready = [sem(f"lo_ready{i}") for i in range(3)]
        unit_used = [sem(f"unit_used{i}") for i in range(3)]
        mod_full = [sem(f"mod_full{i}") for i in range(2)]
        start_full = [sem(f"start_full{i}") for i in range(6)]
        mod_used = sem("mod_used")
        acc_zero = sem("acc_zero")
        cw_zero = sem("cw_zero")
        cw_landed = sem("cw_landed")
        table_out = sem("table_out")
        strips_landed = sem("strips_landed")
        wst_landed = sem("wst_landed")
        misc_psum = sem("misc_psum")
        misc_taken = sem("misc_taken")
        sq_ready = sem("sq_ready")
        sq_used = sem("sq_used")
        pair_ready = sem("pair_ready")
        rstd_ready = sem("rstd_ready")
        x_ready = sem("x_ready")
        y_ready = sem("y_ready")
        hf_ready = sem("hf_ready")
        hH_ready = sem("hH_ready")
        h_ready = sem("h_ready")
        proj_done = sem("proj_done")
        v_turned = sem("v_turned")
        v_ready = sem("v_ready")
        gw_ready = sem("gw_ready")
        gate_exp = sem("gate_exp")
        cmp_sub = sem("cmp_sub")
        cmp_exp = sem("cmp_exp")
        kpe_ready = sem("kpe_ready")
        scores_psum = sem("scores_psum")
        neg_ready = sem("neg_ready")
        prob_ready = sem("prob_ready")
        pt_psum = sem("pt_psum")
        pt_ready = sem("pt_ready")
        pv_done = sem("pv_done")
        o_taken = sem("o_taken")
        sink_in = sem("sink_in")
        sink_exp = sem("sink_exp")
        otok_ready = sem("otok_ready")
        oT_psum = sem("oT_psum")
        oT_ready = sem("oT_ready")
        oTH_ready = sem("oTH_ready")
        z_psum = sem("z_psum")
        zabs_ready = sem("zabs_ready")
        zlog_ready = sem("zlog_ready")
        sp_ready = sem("sp_ready")
        suf_psum = sem("suf_psum")
        fw_ready = sem("fw_ready")
        w_ready = sem("w_ready")
        stick_pv = sem("stick_pv")
        silu_ready = sem("silu_ready")
        af_ready = sem("af_ready")
        aH_ready = sem("aH_ready")
        aL_ready = sem("aL_ready")
        zc_ready = sem("zc_ready")
        conv_ready = sem("conv_ready")
        csil_ready = sem("csil_ready")
        eps_ready = sem("eps_ready")
        dve_done = sem("dve_done")
        act_done = sem("act_done")
        qk_sq = sem("qk_sq")
        qk_ms = sem("qk_ms")
        qk_rstd = sem("qk_rstd")
        qk_n = sem("qk_n")
        qk_rot = sem("qk_rot")
        qk_done = sem("qk_done")
        tokv_sq = sem("tokv_sq")
        tokv_ms = sem("tokv_ms")
        tokv_rstd = sem("tokv_rstd")
        tokv_ready = sem("tokv_ready")
        tok_psum = sem("tok_psum")
        tok_ready = sem("tok_ready")
        tokms = sem("tokms")
        tokrstd = sem("tokrstd")
        an_in = sem("an_in")
        an_out = sem("an_out")
        mixf_ready = sem("mixf_ready")
        mixH_ready = sem("mixH_ready")
        out_ready = sem("out_ready")
        out_stored = sem("out_stored")

        NORMS = ["A0", "B0", "A1", "B1", "A2", "B2", "A3", "B3", "A4", "A5", "A6"]
        MISC = ["table", "bc", "mod0a", "cmpk", "kcT", "cmpv", "vrep", "mod0g", "cscore", "gates", "cpt0",
                "cpt1", "cpv0", "cpv1", "mod1a", "mod1g", "mod2a", "mod2g", "mod3a", "mod3g", "mod4a", "mod4g",
                "mod5a", "mod5g"]
        misc = {name: i for i, name in enumerate(MISC)}
        PROJ0 = {"ab": 0, "cd": 16, "sb": 34}
        NPROJ = {"ab": 16, "cd": 18, "sb": 14}
        VALUES = {"ab": (range(13, 16), 0), "cd": (range(13, 18), 3), "sb": (range(5, 10), 8)}
        ATT = {"ab": [(0, 5, 2, 0, 0), (8, 5, 3, 1, 0), (16, 9, 4, 2, 8)], "cd": [(24, 0, 4, 0, 0)],
               "sb": [(32, 0, 4, 0, None)]}
        MIX_ORDER = (2, 3, 0, 1)

        def mix_src(b):
            if b < 2:
                return sn[:, b, :]
            return proj[:, 5 + 2 * (b - 2):7 + 2 * (b - 2), :].rearrange("p a s -> p (a s)")

        qk_rs = (sn[:, 0, :], sn[:, 1, :], pt[:, 0, 0:S])
        qk_tiles = (proj[:, 0:2, :], proj[:, 2:4, :], proj[:, 4:5, :])
        TILE0 = {"f0": 0, "f1": FT, "f2": 2 * FT}
        JOBS = ([(0, k, n * D, D) for n in range(2) for k in range(KT)]
                + [(0, k, 2 * D, D) for k in range(KT)]
                + [(1, k, n * MC, MC) for k in range(KT) for n in range(2)])
        N_JOBS = len(JOBS)
        JOBS_AT_START = 2 * KT
        start_slots = ([modbuf[:, :, :].rearrange("p a b -> p (a b)")[:, n * D:(n + 1) * D] for n in range(3)]
                       + [otok[:, q, :] for q in range(QT)]
                       + [vt[:, :, :, :].rearrange("p q a b -> p (q a b)")[:, 0:D]])
        SLOTS = len(start_slots)

        def job_value(q):
            return 16 * ((q - JOBS_AT_START) // 2 + 1)

        def job_buffer(q):
            width = JOBS[q][3]
            if q < JOBS_AT_START:
                return start_slots[q % SLOTS], start_full[q % SLOTS], 16 * (q // SLOTS + 1)
            return modbuf[:, q % 2, 0:width], mod_full[q % 2], job_value(q)
        JOBS_AB = [JOBS_AT_START + (min(KT, e + 1) if e < 10 else KT + -((9 - e) * 8 // 7)) for e in range(24)]
        assert JOBS_AB[-1] == N_JOBS

        mod_src = [A["mod_w"][m] for m in range(4)] + [A["w_ada"][:, 0:MW], A["w_ada"][:, MW:2 * MW]]

        def cls(p):
            return p % 3, p // 3 + 1

        def wait_unit(eng, p):
            c, n = cls(p)
            eng.wait_ge(unit_used[c], n)

        Y_UNIT = {"ab": BASE["ab"] + 16, "cd": BASE["cd"] + 18, "sb": BASE["sb"] + 14}
        FIDX = {"f0": 0, "f1": 1, "f2": 2}

        def wait_y(eng, phase, b):
            if phase in Y_UNIT:
                wait_unit(eng, Y_UNIT[phase] + 2 * b + 1)
            elif b < 3:
                eng.wait_ge(y_ready, 3 * FIDX[phase] + b + 1)
            else:
                wait_unit(eng, BASE[phase] + 3 * FT - 1)

        def bcast(ap, shape):
            return ap.broadcast_to(shape)

        def add_pairs(eng, tensor_tensor, norm):
            n = NORMS.index(norm)
            for b in range(4):
                eng.wait_ge(sq_ready, 4 * n + b + 1)
                tensor_tensor(sq[:, b % 2, 0:S], sq[:, b % 2, 0:S], sq[:, b % 2, S:2 * S],
                              ALU.add).then_inc(pair_ready, 1)

        block = ctx.enter_context(nc.Block())

        @block.sync
        def _(sp):
            def load_unit(p, b=None, i=None):
                if p >= N_UNITS and i is None:
                    return
                c, n = cls(p)
                slot = p % RING
                if i is None:
                    if p >= RING:
                        sp.wait_ge(lo_ready[c], n - 2)
                    src = A["weights"][p]
                else:
                    sp.wait_ge(lo_ready[c], i * 2 + (n - 2))
                    src = A["weights"][bass.ds(i * RING + p, 1)].rearrange("o p n -> (o p) n")
                sp.dma_start(raw[:, slot, :], src).then_inc(raw_full[slot], 16)

            def load_job(q):
                m, k, col, width = JOBS[q]
                depth = SLOTS if q < JOBS_AT_START else 2
                if q >= depth:
                    sp.wait_ge(mod_used, q - depth + 1)
                dst, landed, _ = job_buffer(q)
                sp.dma_start(dst, mod_src[m][k * P:(k + 1) * P, col:col + width]).then_inc(landed, 16)

            sp.dma_start(par[:, :], A["params"]).then_inc(small_landed, 16)
            sp.dma_start(con[:, :], A["consts"]).then_inc(small_landed, 16)
            sp.dma_start(x[:, :, :], A["xT"]).then_inc(x_landed, 16)
            for q in range(SLOTS):
                load_job(q)
            sp.dma_start(early, A["early"]).then_inc(early_landed, 16)
            for q in range(SLOTS, JOBS_AT_START):
                load_job(q)
            sp.wait_ge(misc_taken, misc["table"] + 1)
            sp.dma_start(A["table"].rearrange("b h n -> h b n"),
                         pt[0:16, 1:2, :].broadcast_to((16, COPIES, 512))).then_inc(table_out, 16)
            for p in range(2):
                load_unit(p)
            sp.wait_ge(cw_zero, 1)
            for g in range(G):
                sp.dma_start(cw[g * HD:(g + 1) * HD, g], A["cmp_w"][0]).then_inc(cw_landed, 16)
            for p in range(2, RING):
                load_unit(p)
            done = JOBS_AT_START
            for e in range(24):
                load_unit(e + RING)
                for q in range(done, JOBS_AB[e]):
                    load_job(q)
                done = JOBS_AB[e]
                if e == 4:
                    sp.wait_ge(misc_psum, misc["cmpk"] + 1)
                    for g in range(G):
                        sp.dma_start(cw[g * HD:(g + 1) * HD, g], A["cmp_w"][1]).then_inc(cw_landed, 16)
                if e == 9:
                    sp.wait_ge(misc_psum, misc["cmpv"] + 1)
                    sp.wait_ge(table_out, 16)
                    for a in range(P // COPIES):
                        diag = bass.AP(A["table"].tensor, P - 1 - COPIES * a,
                                       [[16 * 512 - 1, COPIES], [512, 16], [1, S]])
                        sp.dma_start(strips[COPIES * a:COPIES * (a + 1), :, :],
                                     diag).then_inc(strips_landed, 16)

            def ffn(base, job0, mods):
                def step(t, i=None, jobs=False):
                    for c in range(3):
                        p = base + 3 * (t + 2) + c
                        if i is None:
                            load_unit(p)
                        else:
                            load_unit(p, i=i)
                    if jobs:
                        par_ = t % 2
                        for n in range(2):
                            q = job0 + 2 * par_ + n
                            sp.wait_ge(mod_used, i * 4 + (q - 1))
                            src = mods[par_][bass.ds(i * P, P), n * MC:(n + 1) * MC]
                            sp.dma_start(modbuf[:, q % 2, :], src).then_inc(mod_full[q % 2], 16)

                step(0)
                step(1)
                if mods:
                    with sp.Fori(0, 8) as i:
                        step(2, i, True)
                        step(3, i, True)
                    done_turns = 8
                else:
                    with sp.Fori(0, 8) as i:
                        step(2, i)
                        step(3, i)
                    done_turns = 8
                for t in range(2 + 2 * done_turns, FT):
                    step(t)

            ffn(BASE["f0"], N_JOBS, (mod_src[2], mod_src[3]))
            for e in range(CD_UNITS):
                load_unit(BASE["cd"] + e + RING)
            ffn(BASE["f1"], N_JOBS + 32, (mod_src[4], mod_src[5]))
            for e in range(SB_UNITS):
                load_unit(BASE["sb"] + e + RING)
                if e == 0:
                    sp.dma_start(wst, A["w_s"]).then_inc(wst_landed, 16)
            ffn(BASE["f2"], 0, None)
            for b in range(4):
                sp.wait_ge(out_ready, b + 1)
                sp.dma_start(A["out"][:, 2 * b:2 * b + 2, :], tt[:, 2 * b:2 * b + 2, :]).then_inc(out_stored, 16)
            sp.wait_ge(out_stored, 64)

        @block.gpsimd
        def _(pool):
            def split_low(b, par_=None, i=None):
                slot = 3 * (b % 2) + 2
                n = b + 1
                pool.wait_ge(hi_ready[2], n if i is None else i * 2 + n)
                nc.gpsimd.tensor_tensor(wL[:, slot, :], raw[:, slot, :], wH[:, slot, :].bitcast(F32),
                                        ALU.subtract).then_inc(lo_ready[2], 1)

            nc.gpsimd.memset(strips[:, :, :], 0.0).then_inc(cw_zero, 1)
            nc.gpsimd.memset(epst[:, :], EPS).then_inc(eps_ready, 1)

            def plain(first, last):
                for b in range(first, last):
                    split_low(b)

            def looped(b0):
                with pool.Fori(0, 8) as i:
                    split_low(b0, i=i)
                    split_low(b0 + 1, i=i)

            def zero_accs(seen):
                pool.wait_ge(misc_psum, misc[seen] + 1)
                nc.gpsimd.memset(acc0[:, :], 0.0).then_inc(acc_zero, 1)
                nc.gpsimd.memset(acc1, 0.0).then_inc(acc_zero, 1)

            def pairs(norm):
                add_pairs(pool, nc.gpsimd.tensor_tensor, norm)

            f0, cd, f1, sb0, f2 = (BASE[f] // 3 for f in ("f0", "cd", "f1", "sb", "f2"))
            pairs("A0")
            plain(0, f0 + 1)
            pairs("A1")
            wait_y(pool, "ab", 3)
            zero_accs("mod1g")
            plain(f0 + 1, f0 + 3)
            looped(f0 + 3)
            plain(f0 + 19, cd + 1)
            pairs("A2")
            plain(cd + 1, f1 + 1)
            pairs("A3")
            wait_y(pool, "cd", 3)
            zero_accs("mod3g")
            plain(f1 + 1, f1 + 3)
            looped(f1 + 3)
            plain(f1 + 19, sb0 + 1)
            pairs("A4")
            plain(sb0 + 1, f2 + 1)
            pairs("A5")
            plain(f2 + 1, f2 + 3)
            looped(f2 + 3)
            plain(f2 + 19, N_UNITS // 3)
            pairs("A6")

        @block.scalar
        def _(act):
            chain = Count(act_done)

            def link(ins):
                chain.inc(ins)
                act.wait_ge(chain.sem, chain.now())

            class Cursor:
                at = 0
            hi = Cursor()

            def split_high(p, i=None):
                c, n = cls(p)
                slot = p % RING
                if i is None:
                    act.wait_ge(raw_full[slot], 16 * (p // RING + 1))
                    if p >= RING:
                        act.wait_ge(unit_used[c], n - 2)
                else:
                    act.wait_ge(raw_full[slot], i * 16 + 16 * (p // RING + 1))
                    act.wait_ge(unit_used[c], i * 2 + (n - 2))
                nc.scalar.activation(wH[:, slot, :], raw[:, slot, :], ACT.Copy).then_inc(hi_ready[c], 1)

            def split_upto(n):
                while hi.at < min(n, N_UNITS):
                    split_high(hi.at)
                    hi.at += 1

            def norm_rstd(n):
                act.wait_ge(sq_used, 4 * n + 4)
                link(nc.scalar.activation(lnms[:, :], bank[6][:, 0:S], ACT.Ln, bias=epst[:, 0:1], scale=1.0 / D))
                nc.scalar.activation(rstd[:, :], lnms[:, :], ACT.Exp, scale=-0.5).then_inc(rstd_ready, 1)

            def squares(n, ready, src):
                for b in range(4):
                    ready(b)
                    if 4 * n + b >= 2:
                        act.wait_ge(sq_used, 4 * n + b - 1)
                    nc.scalar.activation(sq[:, b % 2, :], src(b), ACT.Square).then_inc(sq_ready, 1)

            def norm_a(a):
                n = NORMS.index(f"A{a}")
                squares(n, lambda b: act.wait_ge(x_landed, 16) if a == 0 else act.wait_ge(x_ready, 4 * a - 4 + b + 1),
                        lambda b: xfl[:, b * 512:(b + 1) * 512])
                norm_rstd(n)
                if a < 6:
                    for b in range(4):
                        act.wait_ge(hf_ready, 4 * a + b + 1)
                        if b == 0:
                            act.wait_ge(misc_taken, misc[f"mod{a}a"] + 1)
                        for k in range(2 * b, 2 * b + 2):
                            last = nc.scalar.activation(hH[:, k, :], tt[:, k, :], ACT.Identity,
                                                        bias=mv[:, a, k:k + 1])
                        last.then_inc(hH_ready, 1)

            def norm_b(i, phase):
                n = NORMS.index(f"B{i}")
                squares(n, lambda b: wait_y(act, phase, b), lambda b: bank[b][:, :])
                norm_rstd(n)

            def take_proj(phase, e, dst, scale=1.0, func=ACT.Copy):
                wait_unit(act, BASE[phase] + e)
                nc.scalar.activation(dst, bank[4 + e % 2][:, 0:S], func, scale=scale).then_inc(proj_done, 1)

            def take_value(phase, e, func=ACT.Copy):
                tiles, first = VALUES[phase]
                n = first + e - tiles[0]
                if e - tiles[0] >= 2:
                    act.wait_ge(v_turned, n - 1)
                take_proj(phase, e, sq[:, n % 2, 0:S], func=func)

            def exp_rows(a, buf, src_banks=None):
                act.wait_ge(neg_ready, a + 1)
                if src_banks is None:
                    cuts = ((0, P), (P, 3 * P))
                else:
                    cuts = ((0, S), (S, 2 * S))
                for q, (lo, up) in enumerate(cuts):
                    src = sn[:, buf, lo:up] if src_banks is None else src_banks[:, lo:up]
                    last = nc.scalar.activation(pr[:, buf, lo:up], src, ACT.Exp, bias=nm[:, a, q:q + 1],
                                                scale=-1.0, accum_out=sm[:, a, q:q + 1])
                last.then_inc(prob_ready, 1)

            def oT_high(o0, n=4):
                for b in range(n):
                    act.wait_ge(oT_psum, o0 + b + 1)
                    nc.scalar.activation(hHf[:, b * 512:(b + 1) * 512], bank[4 + b % 2][:, :],
                                         ACT.Copy).then_inc(oTH_ready, 1)

            def ffn(phase, norm):
                base = BASE[phase]
                g0 = TILE0[phase]

                def step(t, i=None):
                    def at(n, per):
                        return n if i is None else i * per + n

                    b = base + 3 * (t + 1)
                    split = t < FT - 1 or base + 3 * FT < N_UNITS
                    for c in range(2):
                        if split:
                            split_high(b + c, i)
                    act.wait_ge(unit_used[1], at((base + 3 * t + 1) // 3 + 1, 2))
                    bk = bank[4 + t % 2]
                    if phase != "f2":
                        nc.scalar.activation(sn[:, t % 2, 0:S], bk[:, 0:S], ACT.Silu).then_inc(silu_ready, 1)
                    else:
                        row = conv[:, t] if i is None else conv[:, bass.ds(i * 2 + t, 1)].rearrange("p o c -> p (o c)")
                        for n in range(2):
                            last = nc.scalar.activation(pr[:, t % 2, n * S:(n + 1) * S], bk[:, n * S:(n + 1) * S],
                                                        ACT.Identity, bias=row[:, 4 * n + 3:4 * n + 4],
                                                        scale=row[:, 4 * n + 1:4 * n + 2])
                        last.then_inc(zc_ready, 1)
                        act.wait_ge(conv_ready, at(t + 1, 2))
                        nc.scalar.activation(sn[:, t % 2, 0:S], pr[:, t % 2, 0:S], ACT.Silu).then_inc(silu_ready, 1)
                    if split:
                        split_high(b + 2, i)
                    act.wait_ge(af_ready, at(g0 + t + 1, 2))
                    if t >= 2:
                        act.wait_ge(unit_used[2], at((base + 3 * (t - 2) + 2) // 3 + 1, 2))
                    nc.scalar.activation(aH[:, t % 2, :], sn[:, t % 2, S:2 * S], ACT.Copy).then_inc(aH_ready, 1)

                step(0)
                step(1)
                with act.Fori(0, 8) as i:
                    step(2, i)
                    step(3, i)
                for t in range(18, FT):
                    step(t)
                hi.at = base + 3 * FT + 3
                nc.scalar.preload_act_table_set("natural_log_exp_and_others")
                if norm is not None:
                    norm_b(norm, phase)

            act.wait_ge(small_landed, 32)
            nc.scalar.activation(csil[:, :], cvec[:, 1, :], ACT.Silu).then_inc(csil_ready, 1)
            nc.scalar.preload_act_table_set("natural_log_exp_and_others")
            nc.scalar.activation(gwH[:, :, :].rearrange("p k n -> p (k n)"), param("wga"), ACT.Copy).then_inc(gw_ready, 1)
            act.wait_ge(eps_ready, 1)

            norm_a(0)
            split_upto(3)
            act.wait_ge(misc_taken, misc["bc"] + 1)
            for e in range(16):
                split_upto(min(e + 5, 27))
                if e < 13:
                    scale = -0.125 if e >= 5 else 1.0
                    take_proj("ab", e, proj[:, e, :], scale)
                else:
                    take_value("ab", e)
                if e == 13:
                    act.wait_ge(cmp_sub, 1)
                    nc.scalar.activation(pr[:, 0, 0:S], sn[:, 0, 0:S], ACT.Exp, scale=-1.0).then_inc(cmp_exp, 1)
                if e == 14:
                    act.wait_ge(misc_taken, misc["gates"] + 1)
                    nc.scalar.activation(small[:, 0:48], gt[:, :, :].rearrange("p q n -> p (q n)"), ACT.Exp,
                                         scale=-1.0).then_inc(gate_exp, 1)
            for a in range(24):
                if a >= 2:
                    act.wait_ge(pt_psum, a - 1)
                else:
                    act.wait_ge(misc_psum, misc["cpv1"] + 1)
                exp_rows(a, a % 2)
            act.wait_ge(sink_in, 1)
            nc.scalar.activation(sinkx[:, :, :], sinkx[:, :, :], ACT.Exp).then_inc(sink_exp, 1)
            oT_high(0)
            for e in range(16, 24):
                split_upto(min(e + 5, 27))
            norm_b(0, "ab")
            norm_a(1)
            ffn("f0", 1)
            norm_a(2)

            act.wait_ge(misc_psum, misc["mod2g"] + 1)
            base = BASE["cd"]
            end = base + CD_UNITS
            for e in range(18):
                split_upto(min(base + e + 5, end + 3))
                if e < 13:
                    scale = -0.125 if e < 4 else (0.125 if 5 <= e < 9 else 1.0)
                    take_proj("cd", e, proj[:, e, :], scale)
                else:
                    take_value("cd", e)
            for a in range(24, 32):
                act.wait_ge(pt_psum, a - 1)
                exp_rows(a, a % 2)
            for h in range(H + 1):
                if h < H:
                    act.wait_ge(zabs_ready, h + 1)
                    link(nc.scalar.activation(pt[:, h % 2, 0:384], pt[:, h % 2, 0:384], ACT.Exp, scale=-1.0))
                    nc.scalar.activation(pt[:, h % 2, 0:384], pt[:, h % 2, 0:384], ACT.Ln,
                                         bias=ones[:, 0:1]).then_inc(zlog_ready, 1)
                if h >= 1:
                    act.wait_ge(fw_ready, h)
                    nc.scalar.activation(pr[:, (h - 1) % 2, 0:384], pr[:, (h - 1) % 2, 0:384],
                                         ACT.Exp).then_inc(w_ready, 1)
            oT_high(4)
            for e in range(18, 27):
                split_upto(min(base + e + 5, end + 3))
            norm_b(2, "cd")
            norm_a(3)
            ffn("f1", 3)
            norm_a(4)

            act.wait_ge(misc_psum, misc["mod4g"] + 1)
            base = BASE["sb"]
            end = base + SB_UNITS
            for e in range(14):
                split_upto(min(base + e + 5, end + 3))
                if e < 5:
                    take_proj("sb", e, proj[:, e, :])
                    act.wait_ge(proj_done, PROJ0["sb"] + e + 1)
                    nc.scalar.activation(tt[:, e, :], proj[:, e, :], ACT.Square).then_inc(qk_sq, 1)
                elif e == 5:
                    take_value("sb", e)
                    act.wait_ge(qk_ms, 5)
                    for n, src in enumerate((bank[2][:, :], bank[3][:, :], bank[6][:, 0:S])):
                        dst = qk_rs[n]
                        link(nc.scalar.activation(dst, src, ACT.Ln, bias=epst[:, 0:1], scale=1.0 / HD))
                        nc.scalar.activation(dst, dst, ACT.Exp, scale=-0.5).then_inc(qk_rstd, 1)
                elif e < 10:
                    take_value("sb", e, func=ACT.Gelu_apprx_tanh)
                else:
                    take_proj("sb", e, proj[:, e - 5, :], func=ACT.Gelu_apprx_tanh)
            nc.scalar.preload_act_table_set("natural_log_exp_and_others")
            act.wait_ge(tokv_ms, 1)
            link(nc.scalar.activation(small[:, 16:32], small[:, 0:16], ACT.Ln, bias=epst[:, 0:1], scale=1.0 / HD))
            nc.scalar.activation(small[:, 32:48], small[:, 16:32], ACT.Exp, scale=-0.5).then_inc(tokv_rstd, 1)
            for a in range(32, 40):
                if a >= 34:
                    act.wait_ge(pt_psum, a - 1)
                exp_rows(a, a % 2, bank[4 + a % 2])
            act.wait_ge(tokms, 1)
            link(nc.scalar.activation(lnms[:, :], bank[2][:, 0:S], ACT.Ln, bias=epst[:, 0:1], scale=1.0 / 512))
            nc.scalar.activation(rstd[:, :], lnms[:, :], ACT.Exp, scale=-0.5).then_inc(tokrstd, 1)
            act.wait_ge(otok_ready, 3)
            for q in range(QT):
                link(nc.scalar.activation(sn[:, q, :], otok[:, q, 0:512], ACT.Square,
                                          accum_out=small[:, 48 + q:49 + q]))
            link(nc.scalar.activation(small[:, 50:52], small[:, 48:50], ACT.Ln, bias=epst[:, 0:1], scale=1.0 / 512))
            nc.scalar.activation(small[:, 52:54], small[:, 50:52], ACT.Exp, scale=-0.5).then_inc(an_in, 1)
            for n, b in enumerate(MIX_ORDER):
                act.wait_ge(mixf_ready, n + 1)
                nc.scalar.activation(hHf[:, b * 512:(b + 1) * 512], mix_src(b), ACT.Copy).then_inc(mixH_ready, 1)
            for e in range(14, 24):
                split_upto(min(base + e + 5, end + 3))
            norm_a(5)
            ffn("f2", None)
            norm_a(6)

        @block.vector
        def _(dve):
            chain = Count(dve_done)

            def link(ins):
                chain.inc(ins)
                dve.wait_ge(chain.sem, chain.now())

            class Cursor:
                at = 0
                job = 0
            lo = Cursor()
            V = nc.vector

            def split_low(p, i=None):
                c, n = cls(p)
                slot = p % RING
                dve.wait_ge(hi_ready[c], n if i is None else i * 2 + n)
                V.tensor_tensor(wL[:, slot, :], raw[:, slot, :], wH[:, slot, :].bitcast(F32),
                                ALU.subtract).then_inc(lo_ready[c], 1)

            def split_upto(n):
                while lo.at < min(n, N_UNITS):
                    if lo.at % 3 != 2:
                        split_low(lo.at)
                    lo.at += 1

            def job(q):
                m, k, col, width = JOBS[q]
                src, landed, value = job_buffer(q)
                dve.wait_ge(landed, value)
                dst = acc0[:, col:col + width]
                if q >= 1:
                    dve.wait_ge(mod_used, q)
                if k == 0:
                    V.tensor_scalar(dst, src, cvec[:, 0, 0:1], None, ALU.mult).then_inc(mod_used, 1)
                else:
                    V.scalar_tensor_tensor(out=dst, in0=src, scalar=cvec[:, 0, k:k + 1], in1=dst,
                                           op0=ALU.mult, op1=ALU.add).then_inc(mod_used, 1)

            def jobs_upto(n):
                while lo.job < n:
                    job(lo.job)
                    lo.job += 1

            def take(name):
                dve.wait_ge(misc_psum, misc[name] + 1)

            def taken(ins):
                ins.then_inc(misc_taken, 1)

            def mod_vector(m, name, lo_=0, up=24):
                take(name)
                taken(V.tensor_tensor(mv[:, m, lo_:up], bank[7][:, lo_:up], modb[:, m, lo_:up], ALU.add))
                dve.wait_ge(misc_taken, misc[name] + 1)
                if lo_ == 0:
                    w = normw[:, 2 * m if m < 4 else 8 + (m - 4), :]
                    link(V.scalar_tensor_tensor(out=sc1[:, m, :], in0=mv[:, m, KT:2 * KT], scalar=1.0, in1=w,
                                                op0=ALU.add, op1=ALU.mult))
                if up == 24:
                    if m < 4:
                        link(V.tensor_tensor(gw1[:, m, :], mv[:, m, 2 * KT:24], normw[:, 2 * m + 1, :], ALU.mult))
                    else:
                        link(V.tensor_copy(gw1[:, m, :], mv[:, m, 2 * KT:24]))

            def norm_a(a):
                n = NORMS.index(f"A{a}")
                scale = sc1[:, a, :] if a < 6 else normw[:, 10, :]
                if 1 <= a < 6:
                    mod_vector(a, f"mod{a}a", 0, 16)
                dve.wait_ge(rstd_ready, n + 1)

                def lower(b):
                    dve.wait_ge(hH_ready, 4 * a + b + 1)
                    for k in range(2 * b, 2 * b + 2):
                        last = V.scalar_tensor_tensor(out=hL[:, k, :], in0=tt[:, k, :], scalar=mv[:, a, k:k + 1],
                                                      in1=hH[:, k, :].bitcast(F32), op0=ALU.add, op1=ALU.subtract)
                    last.then_inc(h_ready, 1)

                for b in range(4):
                    for k in range(2 * b, 2 * b + 2):
                        last = V.scalar_tensor_tensor(out=tt[:, k, :], in0=x[:, k, :], scalar=scale[:, k:k + 1],
                                                      in1=rstd[:, :], op0=ALU.mult, op1=ALU.mult)
                    last.then_inc(hf_ready if a < 6 else out_ready, 1)
                    if a < 6 and b >= 1:
                        lower(b - 1)
                if a < 6:
                    lower(3)
                if 1 <= a < 6:
                    mod_vector(a, f"mod{a}g", 16, 24)

            def norm_b(i, m):
                add_pairs(dve, V.tensor_tensor, f"B{i}")
                dve.wait_ge(rstd_ready, NORMS.index(f"B{i}") + 1)
                for b in range(4):
                    link(V.tensor_tensor(tt[:, 2 * b:2 * b + 2, :],
                                         bank[b][:, :].rearrange("p (k s) -> p k s", k=2),
                                         bcast(rstd[:, :].unsqueeze(1), [P, 2, S]), ALU.mult))
                    for k in range(2 * b, 2 * b + 2):
                        last = V.scalar_tensor_tensor(out=x[:, k, :], in0=tt[:, k, :], scalar=gw1[:, m, k:k + 1],
                                                      in1=x[:, k, :], op0=ALU.mult, op1=ALU.add)
                    last.then_inc(x_ready, 1)

            def residual(phase, m):
                for b in range(4):
                    wait_y(dve, phase, b)
                    for k in range(2 * b, 2 * b + 2):
                        last = V.scalar_tensor_tensor(out=x[:, k, :], in0=bank[b][:, (k % 2) * S:(k % 2 + 1) * S],
                                                      scalar=gw1[:, m, k:k + 1], in1=x[:, k, :],
                                                      op0=ALU.mult, op1=ALU.add)
                    last.then_inc(x_ready, 1)

            def values(phase, e):
                tiles, first = VALUES[phase]
                if e - 1 in tiles:
                    col = e - 1 - tiles[0]
                    n = first + col
                    dve.wait_ge(v_turned, n + 1)
                    V.tensor_copy(vt[:, :, col, :], bank[n % 2][:, 0:S].rearrange("p (q n) -> p q n", q=QT)
                                  ).then_inc(v_ready, 1)

            def neg_scores(a, strip, first=3e38):
                dve.wait_ge(scores_psum, a + 1)
                if a >= 2:
                    dve.wait_ge(prob_ready, a - 1)
                bk = bank[4 + a % 2]
                V.tensor_tensor_reduce(sn[:, a % 2, 0:P], bk[:, 0:P], strips[:, strip, P:S], 1.0, first,
                                       ALU.add, ALU.min, nm[:, a, 0:1])
                V.tensor_tensor_reduce(sn[:, a % 2, P:3 * P], bk[:, P:3 * P], strips[:, strip, :], 1.0, first,
                                       ALU.add, ALU.min, nm[:, a, 1:2]).then_inc(neg_ready, 1)

            def take_pt(a, width=384):
                dve.wait_ge(pt_psum, a + 1)
                if a >= 2:
                    dve.wait_ge(pv_done, a - 1)
                V.tensor_copy(pt[:, a % 2, 0:width], bank[6 + a % 2][:, 0:width]).then_inc(pt_ready, 1)

            def row_factor(a0, gate):
                link(V.reciprocal(rg[:, :, :], sm[:, a0:a0 + H, :]))
                if gate is not None:
                    gates = gt[:, :, :].rearrange("p q (h j) -> p j h q", j=3)[:, gate]
                    link(V.tensor_tensor(rg[:, :, :], rg[:, :, :], gates, ALU.mult))

            def take_o(j, a0, col, add, signal=None):
                dve.wait_ge(pv_done, a0 + H)
                for q in range(QT):
                    dst = otok[:, q, col:col + 512].rearrange("p (h d) -> p h d", d=HD)
                    src = bank[2 * (j % 2) + q][:, :].rearrange("p (h d) -> p h d", d=HD)
                    f = bcast(rg[:, :, q:q + 1], [P, H, HD])
                    if add:
                        tmp = sq[:, q, :].rearrange("p (h d) -> p h d", d=HD)
                        link(V.tensor_tensor(tmp, src, f, ALU.mult))
                        ins = V.tensor_tensor(dst, dst, tmp, ALU.add)
                    else:
                        ins = V.tensor_tensor(dst, src, f, ALU.mult)
                    if q == QT - 1 and signal is not None:
                        ins.then_inc(signal, 1)
                    else:
                        link(ins)

            def oT_low(o0):
                for b in range(4):
                    dve.wait_ge(oTH_ready, o0 + b + 1)
                    V.tensor_tensor(hLf[:, b * 512:(b + 1) * 512], bank[4 + b % 2][:, :],
                                    hHf[:, b * 512:(b + 1) * 512].bitcast(F32), ALU.subtract).then_inc(oT_ready, 1)

            def ffn(phase, job0, mods):
                base = BASE[phase]
                g0 = TILE0[phase]

                def step(t, i=None, jobs=False):
                    def at(n, per):
                        return n if i is None else i * per + n

                    b = base + 3 * (t + 1)
                    split = t < FT - 1 or base + 3 * FT < N_UNITS
                    for c in range(2):
                        if split:
                            split_low(b + c, i)
                    up = bank[4 + t % 2][:, S:2 * S]
                    if phase == "f2":
                        row = conv[:, t] if i is None else conv[:, bass.ds(i * 2 + t, 1)].rearrange("p o c -> p (o c)")
                        dve.wait_ge(zc_ready, at(t + 1, 2))
                        for n in range(2):
                            z = bank[4 + t % 2][:, n * S:(n + 1) * S]
                            dst = pr[:, t % 2, n * S:(n + 1) * S]
                            link(V.scalar_tensor_tensor(out=dst[:, 1:S], in0=z[:, 0:S - 1],
                                                        scalar=row[:, 4 * n:4 * n + 1], in1=dst[:, 1:S],
                                                        op0=ALU.mult, op1=ALU.add))
                            ins = V.scalar_tensor_tensor(out=dst[:, 0:S - 1], in0=z[:, 1:S],
                                                         scalar=row[:, 4 * n + 2:4 * n + 3], in1=dst[:, 0:S - 1],
                                                         op0=ALU.mult, op1=ALU.add)
                        ins.then_inc(conv_ready, 1)
                        up = pr[:, t % 2, S:2 * S]
                    dve.wait_ge(silu_ready, at(g0 + t + 1, 2))
                    V.tensor_tensor(sn[:, t % 2, S:2 * S], sn[:, t % 2, 0:S], up, ALU.mult).then_inc(af_ready, 1)
                    if jobs:
                        par_ = t % 2
                        acc = (acc1, acc0[:, :])[par_]
                        cc = cvec[:, 0] if job0 == N_JOBS else csil[:, :]
                    for n in range(2):
                        if n == 1:
                            dve.wait_ge(aH_ready, at(g0 + t + 1, 2))
                            V.tensor_tensor(aL[:, t % 2, :], sn[:, t % 2, S:2 * S], aH[:, t % 2, :].bitcast(F32),
                                            ALU.subtract).then_inc(aL_ready, 1)
                        if jobs:
                            q = job0 + 2 * par_ + n
                            dve.wait_ge(mod_full[q % 2], i * 32 + job_value(q))
                            dve.wait_ge(mod_used, i * 4 + q)
                            V.scalar_tensor_tensor(out=acc[:, n * MC:(n + 1) * MC], in0=modbuf[:, q % 2, :],
                                                   scalar=cc[:, bass.ds(i, 1)], in1=acc[:, n * MC:(n + 1) * MC],
                                                   op0=ALU.mult, op1=ALU.add).then_inc(mod_used, 1)

                step(0)
                step(1)
                if mods:
                    dve.wait_ge(acc_zero, 2 if phase == "f0" else 4)
                    dve.wait_ge(csil_ready, 1)
                per = 4 if phase == "f2" else 0
                with dve.Fori(0, 8) as i:
                    chain.enter(i, per)
                    step(2, i, mods)
                    step(3, i, mods)
                chain.leave(8)
                for t in range(18, FT):
                    step(t)
                lo.at = base + 3 * FT + 3

            dve.wait_ge(small_landed, 32)
            link(V.tensor_scalar(nsink[:, :], param("sinks"), -1.0, None, ALU.mult))
            dve.wait_ge(gw_ready, 1)
            V.tensor_tensor(gwL[:, :, :].rearrange("p k n -> p (k n)"), param("wga"),
                            gwH[:, :, :].rearrange("p k n -> p (k n)").bitcast(F32), ALU.subtract).then_inc(gw_ready, 1)
            jobs_upto(KT)
            dve.wait_ge(early_landed, 16)
            take("table")
            taken(V.scalar_tensor_tensor(out=pt[0:16, 1, :], in0=bank[7][0:16, :], scalar=-1.0,
                                         in1=early_const("negmask", 16), op0=ALU.mult, op1=ALU.add))
            take("bc")
            link(V.tensor_scalar(bc[:, :, :, :].rearrange("p q n h -> p (q n h)"), bank[7][:, 0:S], -1.0, None,
                                 ALU.mult))
            cmask = bcast(const("cmpmask").rearrange("p (q n) -> p q n", q=QT).unsqueeze(3), [P, QT, 16, H])
            taken(V.tensor_tensor(bc[:, :, :, :], bc[:, :, :, :], cmask, ALU.add))
            jobs_upto(JOBS_AT_START)
            mod_vector(0, "mod0a", 0, 16)

            norm_a(0)
            split_upto(3)

            def compressed_input(e, n):
                dve.wait_ge(proj_done, e + 1)
                base_ap = proj[:, e, :]
                win = bass.AP(base_ap.tensor, base_ap.offset, [list(base_ap.ap[0]), [1, CLEN], [CSTR, NCMP]])
                V.tensor_tensor(sn[:, n, :].rearrange("p (l n) -> p l n", n=16)[:, :, 0:NCMP], win,
                                bcast(param("pe").unsqueeze(2), [P, CLEN, NCMP]), ALU.add).then_inc(kpe_ready, 1)

            for e in range(16):
                split_upto(min(e + 5, 27))
                if e == 1:
                    compressed_input(0, 0)
                if e == 2:
                    compressed_input(1, 1)
                if e == 4:
                    take("cmpk")
                    taken(V.tensor_copy(kcs[0:NCMP, :], bank[7][0:NCMP, 0:P]))
                if e == 6:
                    take("kcT")
                    taken(V.tensor_copy(kc[:, 0:NCMP], bank[7][:, 0:NCMP]))
                if e == 8:
                    take("cmpv")
                    taken(V.tensor_copy(vcs[0:NCMP, :], bank[7][0:NCMP, 0:P]))
                if e == 10:
                    take("vrep")
                    vcb = pt[:, 0, :].rearrange("p (h d) -> p h d", d=HD)
                    for g in range(G):
                        rep = bcast(bank[7][:, g * HD:(g + 1) * HD].unsqueeze(1), [P, H // G, HD])
                        hm = bcast(const("headmask")[:, g * 4:(g + 1) * 4].unsqueeze(2), [P, H // G, HD])
                        ins = V.tensor_tensor(vcb[:, g * 4:(g + 1) * 4, :], rep, hm, ALU.mult)
                    taken(ins)
                    mod_vector(0, "mod0g", 16, 24)
                if e == 11:
                    take("cscore")
                    s3 = sn[:, 0, 0:S].rearrange("p (r n) -> p r n", n=16)
                    for q in range(QT):
                        for g in range(G):
                            heads = slice(g * (H // G), (g + 1) * (H // G))
                            s4 = sn[:, 0, q * P:(q + 1) * P].rearrange("p (h n) -> p h n", n=16)[:, heads]
                            scores_ = bank[7 - g][:, q * HD:(q + 1) * HD].rearrange("p (h n) -> p h n", n=16)
                            ins = V.tensor_tensor(s4, scores_, bc[:, q, :, heads].rearrange("p n h -> p h n"), ALU.add)
                            taken(ins) if q == QT - 1 and g == G - 1 else link(ins)
                    dve.wait_ge(misc_taken, misc["cscore"] + 1)
                    link(V.tensor_reduce(cm[:, 0, :], s3, AX, ALU.min))
                    V.tensor_tensor(s3, s3, bcast(cm[:, 0, :].unsqueeze(2), [P, 16, 16]),
                                    ALU.subtract).then_inc(cmp_sub, 1)
                if e == 12:
                    take("gates")
                    taken(V.tensor_copy(gt[:, :, :].rearrange("p q n -> p (q n)"), bank[7][:, 0:48]))
                if e == 14:
                    dve.wait_ge(cmp_exp, 1)
                    p3 = pr[:, 0, 0:S].rearrange("p (r n) -> p r n", n=16)
                    link(V.tensor_reduce(cm[:, 1, :], p3, AX, ALU.add))
                    link(V.reciprocal(cm[:, 2, :], cm[:, 1, :]))
                    link(V.tensor_tensor(rg[:, :, :], cm[:, 2, :].rearrange("p (q h) -> p h q", q=QT),
                                         bcast(const("rowvalid").unsqueeze(1), [P, H, QT]), ALU.mult))
                    take("cpt0")
                    taken(V.tensor_copy(sn[:, 1, 0:P], bank[7][:, 0:P]))
                if e == 15:
                    take("cpt1")
                    taken(V.tensor_copy(sn[:, 1, P:2 * P], bank[7][:, 0:P]))
                    dve.wait_ge(gate_exp, 1)
                    link(V.tensor_scalar(small[:, 0:48], small[:, 0:48], 1.0, None, ALU.add))
                    link(V.reciprocal(gt[:, :, :].rearrange("p q n -> p (q n)"), small[:, 0:48]))
                    link(V.tensor_tensor(rg[:, :, :], rg[:, :, :],
                                         gt[:, :, :].rearrange("p q (h j) -> p j h q", j=3)[:, 0], ALU.mult))
                    for q in range(QT):
                        take(f"cpv{q}")
                        taken(V.tensor_tensor(otok[:, q, 0:512].rearrange("p (h d) -> p h d", d=HD),
                                              bank[7][:, :].rearrange("p (h d) -> p h d", d=HD),
                                              bcast(rg[:, :, q:q + 1], [P, H, HD]), ALU.mult))
                    dve.wait_ge(misc_taken, misc["cpv1"] + 1)
                values("ab", e)
                jobs_upto(JOBS_AB[e])
            values("ab", 16)
            dve.wait_ge(strips_landed, 16 * (P // COPIES))
            for s in range(24 + 4):
                if s < 24:
                    j = s // 8
                    strip = s % 8 + (8 if j == 2 else 0)
                    neg_scores(s, strip, nsink[:, s % 8:s % 8 + 1] if j == 2 else 3e38)
                if 1 <= s <= 24:
                    take_pt(s - 1)
                if s >= 10 and (s - 10) % 8 == 0 and s < 28:
                    j = (s - 10) // 8
                    if j < 2:
                        row_factor(8 * j, j + 1)
                        take_o(j, 8 * j, 0, True, o_taken)
                        dve.wait_ge(o_taken, j + 1)
            dve.wait_ge(neg_ready, 24)
            V.tensor_tensor(sinkx[:, :, :], nm[:, 16:24, :], bcast(param("sinks").unsqueeze(2), [P, H, QT]),
                            ALU.add).then_inc(sink_in, 1)
            dve.wait_ge(sink_exp, 1)
            dve.wait_ge(prob_ready, 24)
            link(V.tensor_tensor(sm[:, 16:24, :], sm[:, 16:24, :], sinkx[:, :, :], ALU.add))
            row_factor(16, None)
            take_o(2, 16, 512, False, otok_ready)
            oT_low(0)
            for e in range(16, 24):
                split_upto(min(e + 5, 27))
                jobs_upto(JOBS_AB[e])
            norm_b(0, 0)
            norm_a(1)
            ffn("f0", N_JOBS, True)
            norm_b(1, 1)
            norm_a(2)

            base = BASE["cd"]
            end = base + CD_UNITS
            for e in range(18):
                split_upto(min(base + e + 5, end + 3))
                values("cd", e)
            values("cd", 18)
            for s in range(24, 32 + 1):
                if s < 32:
                    neg_scores(s, s - 24)
                if s >= 25:
                    take_pt(s - 1)
            mask = const("stickmask")
            for s in range(H + 1):
                if s < H:
                    dve.wait_ge(z_psum, s + 1)
                    if s >= 2:
                        dve.wait_ge(fw_ready, s - 1)
                    link(V.tensor_tensor(sn[:, s % 2, 0:384], bank[4 + s % 2][:, 0:384], mask, ALU.add))
                    if s < 2:
                        dve.wait_ge(pv_done, 31 + s)
                    else:
                        dve.wait_ge(suf_psum, s - 1)
                    V.scalar_tensor_tensor(out=pt[:, s % 2, 0:384], in0=sn[:, s % 2, 0:384], scalar=-1.0,
                                           in1=sn[:, s % 2, 0:384], op0=ALU.mult, op1=ALU.max).then_inc(zabs_ready, 1)
                if s >= 1:
                    h = s - 1
                    dve.wait_ge(suf_psum, h + 1)
                    if h >= 2:
                        dve.wait_ge(stick_pv, h - 1)
                    else:
                        dve.wait_ge(pt_psum, 31 + h)
                    V.tensor_tensor(pr[:, h % 2, 0:384], bank[6 + h % 2][:, 0:384], sn[:, h % 2, 0:384],
                                    ALU.add).then_inc(fw_ready, 1)
                if s < H:
                    dve.wait_ge(zlog_ready, s + 1)
                    V.scalar_tensor_tensor(out=pt[:, s % 2, 0:384], in0=sn[:, s % 2, 0:384], scalar=0.0,
                                           in1=pt[:, s % 2, 0:384], op0=ALU.max, op1=ALU.add).then_inc(sp_ready, 1)
                if s == 3:
                    dve.wait_ge(prob_ready, 32)
                    row_factor(24, None)
                    take_o(0, 24, 0, False)
            dve.wait_ge(stick_pv, H)
            V.tensor_copy(otok[:, 0, 512:1024], bank[2][:, :])
            V.tensor_copy(otok[:, 1, 512:1024], bank[3][:, :]).then_inc(otok_ready, 1)
            oT_low(4)
            for e in range(18, 27):
                split_upto(min(base + e + 5, end + 3))
            norm_b(2, 2)
            norm_a(3)
            ffn("f1", N_JOBS + 32, True)
            norm_b(3, 3)
            norm_a(4)

            base = BASE["sb"]
            end = base + SB_UNITS
            link(V.tensor_scalar(qgain[:, 0:1], param("gqk")[:, 0:1], -0.125, None, ALU.mult))
            for e in range(14):
                split_upto(min(base + e + 5, end + 3))
                values("sb", e)
                if e == 7:
                    for n, tiles in enumerate(qk_tiles):
                        flat = tiles.rearrange("p a s -> p (a s)")
                        dve.wait_ge(qk_rstd, n + 1)
                        V.scalar_tensor_tensor(out=flat, in0=flat,
                                               scalar=qgain[:, 0:1] if n < 2 else param("gqk")[:, 1:2],
                                               in1=qk_rs[n], op0=ALU.mult, op1=ALU.mult).then_inc(qk_n, 1)
                if e == 9:
                    for n, tiles in enumerate(qk_tiles):
                        w = 2 if n < 2 else 1
                        cos, sin = (bcast(const(c).unsqueeze(1), [P, w, S]) for c in ("cos", "sin"))
                        rot = pr[:, n % 2, 0:w * S].rearrange("p (a s) -> p a s", a=w)
                        src = bank[(2, 3, 6)[n]][:, 0:w * S].rearrange("p (a s) -> p a s", a=w)
                        dve.wait_ge(qk_rot, n + 1)
                        link(V.tensor_tensor(rot, src, sin, ALU.mult))
                        link(V.tensor_tensor(tiles, tiles, cos, ALU.mult))
                        V.tensor_tensor(tiles, tiles, rot, ALU.add).then_inc(qk_done, 1)
                if e == 11:
                    dve.wait_ge(v_ready, 13)
                    for q in range(QT):
                        v2 = vt[:, q, 1:5, :].rearrange("p a b -> p (a b)")
                        link(V.tensor_tensor(sn[:, q, :], v2, v2, ALU.mult))
                    V.tensor_reduce(small[:, 0:16], sn[:, :, :].rearrange("p q (h d) -> p (q h) d", d=HD), AX,
                                    ALU.add).then_inc(tokv_ms, 1)

            def token_values():
                dve.wait_ge(tokv_rstd, 1)
                for q in range(QT):
                    v3 = vt[:, q, 1:5, :].rearrange("p a b -> p (a b)").rearrange("p (h d) -> p h d", d=HD)
                    link(V.tensor_tensor(v3, v3, bcast(small[:, 32 + 8 * q:40 + 8 * q].unsqueeze(2), [P, H, HD]),
                                         ALU.mult))
                    V.tensor_tensor(v3, v3, bcast(param("gtokv").unsqueeze(1), [P, H, HD]),
                                    ALU.mult).then_inc(tokv_ready, 1)

            def token_mixed(t):
                dve.wait_ge(tok_psum, t + 1)
                u = proj[:, 5 + t, :]
                if t == 0:
                    dve.wait_ge(proj_done, PROJ0["sb"] + 14)
                bs = bcast(param("bs")[:, t * P:(t + 1) * P].unsqueeze(1), [P, QT, P])
                dst = sn[:, t % 2, 0:S]
                link(V.tensor_tensor(dst.rearrange("p (c n) -> p c n", c=QT),
                                     bank[2 + t % 2][:, 0:S].rearrange("p (c n) -> p c n", c=QT), bs, ALU.add))
                link(V.tensor_tensor(u, dst, u, ALU.mult))
                V.tensor_tensor(sq[:, t // 2, (t % 2) * S:(t % 2 + 1) * S], u, u, ALU.mult).then_inc(tok_ready, 1)

            for a in range(32, 40 + 1):
                if a < 40:
                    dve.wait_ge(scores_psum, a + 1)
                    V.tensor_reduce(nm[:, a, :], bank[4 + a % 2][:, :].rearrange("p (q n) -> p q n", q=QT), AX,
                                    ALU.min).then_inc(neg_ready, 1)
                if a >= 33:
                    take_pt(a - 1, 512)
                if a == 32:
                    token_values()
                if 33 <= a <= 36:
                    token_mixed(a - 33)
            gout = param("gout")
            dve.wait_ge(tokrstd, 1)
            for b in range(2):
                for k in range(2):
                    t = 2 * b + k
                    last = V.scalar_tensor_tensor(out=proj[:, 5 + t, :], in0=proj[:, 5 + t, :],
                                                  scalar=gout[:, 4 + t:5 + t], in1=rstd[:, :],
                                                  op0=ALU.mult, op1=ALU.mult)
                last.then_inc(mixf_ready, 1)

            def mix_low(n):
                b = MIX_ORDER[n]
                dve.wait_ge(mixH_ready, n + 1)
                V.tensor_tensor(hLf[:, b * 512:(b + 1) * 512], mix_src(b),
                                hHf[:, b * 512:(b + 1) * 512].bitcast(F32), ALU.subtract).then_inc(oT_ready, 1)

            dve.wait_ge(prob_ready, 40)
            row_factor(32, None)
            take_o(0, 32, 0, False, otok_ready)
            dve.wait_ge(an_in, 1)
            for q in range(QT):
                V.tensor_scalar(otok[:, q, 0:512], otok[:, q, 0:512], small[:, 52 + q:53 + q], None,
                                ALU.mult).then_inc(an_out, 1)
            for b in range(2):
                dve.wait_ge(oT_psum, 8 + b + 1)
                for k in range(2):
                    last = V.tensor_scalar(sn[:, b, k * S:(k + 1) * S], bank[4 + b][:, k * S:(k + 1) * S],
                                           gout[:, 2 * b + k:2 * b + k + 1], None, ALU.mult)
                last.then_inc(mixf_ready, 1)
            for n in range(4):
                mix_low(n)
            for e in range(14, 24):
                split_upto(min(base + e + 5, end + 3))
            residual("sb", 4)
            norm_a(5)
            ffn("f2", 0, False)
            residual("f2", 5)
            norm_a(6)

        @block.tensor
        def _(pe):
            mm = nc.tensor.matmul

            def unit_ready(p, i=None):
                c, n = cls(p)
                pe.wait_ge(lo_ready[c], n if i is None else i * 2 + n)

            def three(out, lhs_h, lhs_l, rhs_h, rhs_l, start, stop):
                mm(out, lhs_h, rhs_h, start=start, stop=False, skip_group_check=True)
                mm(out, lhs_h, rhs_l, start=False, stop=False, skip_group_check=True)
                return mm(out, lhs_l, rhs_h, start=False, stop=stop, skip_group_check=True)

            def misc_free(name):
                if misc[name] > 0:
                    pe.wait_ge(misc_taken, misc[name])

            def sum_squares(n, fill=None):
                if n >= 1:
                    pe.wait_ge(rstd_ready, n)
                for b in range(4):
                    if b >= 1 and fill is not None:
                        fill(b)
                    pe.wait_ge(pair_ready, 4 * n + b + 1)
                    mm(bank[6][:, 0:S], ones, sq[:, b % 2, 0:S], start=(b == 0), stop=(b == 3),
                       skip_group_check=True).then_inc(sq_used, 1)

            def mod_columns(cols, acc):
                for j in cols:
                    last = mm(bank[7][:, j:j + 1], acc[:, j * P:(j + 1) * P], ones[:, 0:1], start=True, stop=True,
                              skip_group_check=True)
                return last

            def mod_sum(name, cols, acc):
                misc_free(name)
                mod_columns(cols, acc).then_inc(misc_psum, 1)

            def project(phase, e, first_h=None):
                p = BASE[phase] + e
                if e >= 2:
                    pe.wait_ge(proj_done, PROJ0[phase] + e - 1)
                unit_ready(p)
                slot = p % RING
                H3 = wH[:, slot, :].rearrange("p (k n) -> p k n", k=KT)
                L3 = wL[:, slot, :].rearrange("p (k n) -> p k n", k=KT)
                out = bank[4 + e % 2][:, 0:S]
                for k in range(KT):
                    if first_h is not None and k % 2 == 0:
                        pe.wait_ge(h_ready, first_h + k // 2 + 1)
                    last = three(out, H3[:, k], L3[:, k], hH[:, k], hL[:, k], k == 0, k == KT - 1)
                last.then_inc(unit_used[p % 3], 1)

            def turn_values(phase, e):
                tiles, first = VALUES[phase]
                if e - 1 in tiles:
                    n = first + e - 1 - tiles[0]
                    pe.wait_ge(proj_done, PROJ0[phase] + e)
                    if n - first >= 2:
                        pe.wait_ge(v_ready, n - 1)
                    for q in range(QT):
                        last = nc.tensor.transpose(bank[n % 2][:, q * P:(q + 1) * P],
                                                   sq[:, n % 2, q * P:(q + 1) * P], ident)
                    last.then_inc(v_turned, 1)

            def y_unit(phase, m, p, extra=()):
                unit_ready(p)
                slot = p % RING
                H3 = wH[:, slot, :].rearrange("p (k n) -> p k n", k=KT)
                L3 = wL[:, slot, :].rearrange("p (k n) -> p k n", k=KT)
                out = bank[m // 2][:, (m % 2) * S:(m % 2 + 1) * S]
                chunks = MIX_ORDER if phase == "sb" else range(4)
                for n, k in enumerate([2 * b + half for b in chunks for half in range(2)]):
                    if m == 0 and n % 2 == 0:
                        pe.wait_ge(oT_ready, OT0[phase] + n // 2 + 1)
                    last = three(out, H3[:, k], L3[:, k], hH[:, k], hL[:, k], n == 0, n == KT - 1)
                    if n < len(extra):
                        last.then_inc(extra[n], 1)
                last.then_inc(unit_used[p % 3], 1)

            OT0 = {"ab": 0, "cd": 4, "sb": 8}

            def scores(a, h, qtile, ktile):
                r = slice((h // 4) * HD, (h // 4 + 1) * HD)
                q, k = proj[r, qtile + h % 4, :], proj[r, ktile, :]
                bk = bank[4 + a % 2]
                mm(bk[:, 0:P], q[:, 0:P], k[:, 0:P], start=True, stop=True, skip_group_check=True)
                mm(bk[:, P:3 * P], q[:, P:2 * P], k, start=True, stop=True,
                   skip_group_check=True).then_inc(scores_psum, 1)

            def transposes(a, cuts):
                pe.wait_ge(prob_ready, a + 1)
                if a >= 2:
                    pe.wait_ge(pt_ready, a - 1)
                for n in range(cuts):
                    last = nc.tensor.transpose(bank[6 + a % 2][:, n * P:(n + 1) * P], pr[:, a % 2, n * P:(n + 1) * P],
                                               ident)
                last.then_inc(pt_psum, 1)

            def pv(a, h, j, vcol):
                pe.wait_ge(pt_ready, a + 1)
                g = h // 4
                v = [vt[:, kt, vcol, g * HD:(g + 1) * HD] for kt in range(QT)]
                o = [bank[2 * (j % 2) + q][:, h * HD:(h + 1) * HD] for q in range(QT)]
                w = pt[:, a % 2, :]
                mm(o[0], w[:, 0:P], v[0], start=True, stop=True, skip_group_check=True)
                mm(o[1], w[:, P:2 * P], v[0], start=True, stop=False, skip_group_check=True)
                mm(o[1], w[:, 2 * P:3 * P], v[1], start=False, stop=True, skip_group_check=True).then_inc(pv_done, 1)

            def turn_otok(o0, phase_n, tiles=8):
                pe.wait_ge(otok_ready, phase_n)
                for b in range(tiles // 2):
                    if b >= 2:
                        pe.wait_ge(oT_ready, o0 + b - 1)
                    for n in range(2):
                        for q in range(QT):
                            f = 2 * b + n
                            last = nc.tensor.transpose(bank[4 + b % 2][:, n * S + q * P:n * S + (q + 1) * P],
                                                       otok[:, q, f * P:(f + 1) * P], ident)
                    last.then_inc(oT_psum, 1)

            def norm_sums(name):
                sum_squares(NORMS.index(name))

            def norm_sums_with(name, m, jobs_done, acc):
                pe.wait_ge(mod_used, jobs_done)
                misc_free(f"mod{m}a")
                mod_columns(range(10), acc)

                def between(b):
                    last = mod_columns(range(8 + 2 * b, 10 + 2 * b), acc)
                    if b == 3:
                        last.then_inc(misc_psum, 1)

                sum_squares(NORMS.index(name), between)
                mod_sum(f"mod{m}g", range(16, 24), acc)

            def ffn(phase, a):
                base = BASE[phase]
                g0 = TILE0[phase]

                def gate_up(t, i=None, first=False):
                    def at(n, per):
                        return n if i is None else i * per + n

                    bk = bank[4 + t % 2]
                    if t >= 2:
                        if phase == "f2":
                            pe.wait_ge(conv_ready, at(t - 1, 2))
                        else:
                            pe.wait_ge(af_ready, at(g0 + t - 1, 2))
                    order = ([(n, k) for b in range(4) for n in range(2) for k in (2 * b, 2 * b + 1)] if first
                             else [(n, k) for n in range(2) for k in range(KT)])
                    for n, k in order:
                        p = base + 3 * t + n
                        if k == 0:
                            unit_ready(p, i)
                        slot = p % RING
                        H3 = wH[:, slot, :].rearrange("p (k n) -> p k n", k=KT)
                        L3 = wL[:, slot, :].rearrange("p (k n) -> p k n", k=KT)
                        if first and n == 0 and k % 2 == 0:
                            pe.wait_ge(h_ready, 4 * a + k // 2 + 1)
                        last = three(bk[:, n * S:(n + 1) * S], H3[:, k], L3[:, k], hH[:, k], hL[:, k],
                                     k == 0 and not (first and n == 1), k == KT - 1)
                        if k == KT - 1:
                            last.then_inc(unit_used[p % 3], 1)

                def down(t, i=None):
                    p = base + 3 * t + 2
                    unit_ready(p, i)
                    pe.wait_ge(aL_ready, g0 + t + 1 if i is None else i * 2 + (g0 + t + 1))
                    slot = p % RING
                    for m in range(KT):
                        out = bank[m // 2][:, (m % 2) * S:(m % 2 + 1) * S]
                        last = three(out, wH[:, slot, m * P:(m + 1) * P], wL[:, slot, m * P:(m + 1) * P],
                                     aH[:, t % 2, :], aL[:, t % 2, :], t == 0 and m % 2 == 0, t == FT - 1)
                        if t == FT - 1 and m in (1, 3, 5):
                            last.then_inc(y_ready, 1)
                    last.then_inc(unit_used[2], 1)

                gate_up(0, first=True)
                gate_up(1)
                down(0)
                with pe.Fori(0, 8) as i:
                    gate_up(2, i)
                    down(1, i)
                    gate_up(3, i)
                    down(2, i)
                for t in range(18, FT):
                    gate_up(t)
                    down(t - 1)
                down(FT - 1)

            pe.wait_ge(small_landed, 32)
            pe.wait_ge(early_landed, 16)
            mm(bank[7][0:16, :], param("reltab", REL), early_const("onehot_rel", REL), start=True,
               stop=True).then_inc(misc_psum, 1)
            misc_free("bc")
            hot = early_const("onehot_cmp").rearrange("p (g q) -> p g q", g=4)
            for q in range(QT):
                for g in range(4):
                    last = mm(bank[7][:, q * P + g * 32:q * P + (g + 1) * 32], hot[:, g, q * P:(q + 1) * P],
                              param("relblock"), start=True, stop=True, skip_group_check=True)
            last.then_inc(misc_psum, 1)
            norm_sums("A0")
            misc_free("mod0a")
            for half in range(2):
                pe.wait_ge(mod_used, KT * (half + 1))
                last = mod_columns(range(KT * half, KT * (half + 1)), acc0)
            last.then_inc(misc_psum, 1)

            def compress(name, n):
                pe.wait_ge(cw_landed, 32 * (n + 1))
                pe.wait_ge(kpe_ready, n + 1)
                misc_free(name)
                win = sn[:, n, :].rearrange("p (l n) -> p l n", n=16)
                for l in range(CLEN):
                    last = mm(bank[7][0:NCMP, 0:P], win[:, l, 0:NCMP], cw[:, :, l, :], start=(l == 0),
                              stop=(l == CLEN - 1))
                last.then_inc(misc_psum, 1)

            for e in range(16):
                project("ab", e, 0 if e == 0 else None)
                turn_values("ab", e)
                if e == 3:
                    compress("cmpk", 0)
                if e == 7:
                    compress("cmpv", 1)
                if e == 5:
                    misc_free("kcT")
                    nc.tensor.transpose(bank[7][:, 0:NCMP], kcs[0:NCMP, :],
                                        const("ident", NCMP)[:, 0:NCMP]).then_inc(misc_psum, 1)
                if e == 9:
                    misc_free("vrep")
                    mm(bank[7][:, 0:P], const("select", NCMP), vcs[0:NCMP, :], start=True,
                       stop=True).then_inc(misc_psum, 1)
                    pe.wait_ge(mod_used, JOBS_AT_START + KT)
                    mod_sum("mod0g", range(16, 24), acc0)
                if e == 10:
                    misc_free("cscore")
                    pe.wait_ge(proj_done, 9)
                    for g in range(G):
                        mm(bank[7 - g][:, 0:P], ident, const("stickmask")[:, P:S],
                           start=True, stop=False, skip_group_check=True)
                        r = slice(g * HD, (g + 1) * HD)
                        for q in range(QT):
                            for h in range(H // G):
                                c0 = (q * (H // G) + h) * 16
                                last = mm(bank[7 - g][:, c0:c0 + NCMP], proj[r, 5 + h, q * P:(q + 1) * P],
                                          kc[r, 0:NCMP], start=False, stop=True, skip_group_check=True)
                    last.then_inc(misc_psum, 1)
                if e == 11:
                    misc_free("gates")
                    pe.wait_ge(gw_ready, 2)
                    for q in range(QT):
                        for k in range(KT):
                            last = three(bank[7][:, q * 24:(q + 1) * 24], hH[:, k, q * P:(q + 1) * P],
                                         hL[:, k, q * P:(q + 1) * P], gwH[:, k], gwL[:, k], k == 0, k == KT - 1)
                    last.then_inc(misc_psum, 1)
                if e in (13, 14):
                    q = e - 13
                    misc_free(f"cpt{q}")
                    pe.wait_ge(cmp_exp, 1)
                    nc.tensor.transpose(bank[7][:, 0:P], pr[:, 0, q * P:(q + 1) * P], ident).then_inc(misc_psum, 1)
            turn_values("ab", 16)
            for q in range(QT):
                misc_free(f"cpv{q}")
                mm(bank[7][:, :], sn[:, 1, q * P:(q + 1) * P], pt[:, 0, :], start=True,
                   stop=True).then_inc(misc_psum, 1)

            def attention(phase):
                atts = ATT[phase]
                a0 = atts[0][0]
                n = 8 * len(atts)
                for s in range(n + 2):
                    if s < n:
                        j, h = s // 8, s % 8
                        if s == 0:
                            pe.wait_ge(proj_done, PROJ0[phase] + NPROJ[phase])
                            pe.wait_ge(v_ready, VALUES[phase][1] + len(VALUES[phase][0]))
                            if phase == "ab":
                                pe.wait_ge(misc_taken, misc["cpv1"] + 1)
                        if s >= 2:
                            pe.wait_ge(neg_ready, a0 + s - 1)
                        scores(a0 + s, h, atts[j][1], atts[j][2])
                    if 1 <= s <= n:
                        transposes(a0 + s - 1, 3)
                    if s >= 2:
                        a = s - 2
                        j, h = a // 8, a % 8
                        if j == 2 and h == 0:
                            pe.wait_ge(o_taken, 1)
                        pv(a0 + a, h, j, atts[j][3])

            attention("ab")
            turn_otok(0, 1)
            for m in range(KT):
                y_unit("ab", m, 16 + m)
            norm_sums("B0")
            norm_sums_with("A1", 1, N_JOBS, acc0)
            ffn("f0", 1)
            norm_sums("B1")
            norm_sums_with("A2", 2, N_JOBS + 32, acc1)

            base = BASE["cd"]
            for e in range(18):
                project("cd", e, 8 if e == 0 else None)
                turn_values("cd", e)
            turn_values("cd", 18)
            attention("cd")

            def stick_z(h):
                r = slice((h % 2) * HD, (h % 2 + 1) * HD)
                q, k = proj[r, 5 + h // 2, :], proj[r, 9 + h // 2, :]
                bk = bank[4 + h % 2]
                if h < 2:
                    pe.wait_ge(neg_ready, 31 + h)
                else:
                    pe.wait_ge(zabs_ready, h - 1)
                mm(bk[:, 0:S], k[:, 0:P], q, start=True, stop=True, skip_group_check=True)
                mm(bk[:, S:3 * P], k[:, P:S], q[:, P:S], start=True, stop=True,
                   skip_group_check=True).then_inc(z_psum, 1)

            def stick_suffix(h):
                pe.wait_ge(sp_ready, h + 1)
                if h < 2:
                    pe.wait_ge(pt_ready, 31 + h)
                else:
                    pe.wait_ge(fw_ready, h - 1)
                bk, w = bank[6 + h % 2], pt[:, h % 2, :]
                mm(bk[:, S:3 * P], const("tri"), w[:, S:3 * P], start=True, stop=True, skip_group_check=True)
                mm(bk[:, 0:S], const("tri"), w[:, 0:S], start=True, stop=False, skip_group_check=True)
                mm(bk[:, P:S], const("neg1"), w[:, S:3 * P], start=False, stop=True,
                   skip_group_check=True).then_inc(suf_psum, 1)

            def stick_out(h):
                pe.wait_ge(w_ready, h + 1)
                v = [vt[:, kt, 1 + h // 2, (h % 2) * HD:(h % 2 + 1) * HD] for kt in range(QT)]
                o = [bank[2 + q][:, h * HD:(h + 1) * HD] for q in range(QT)]
                w = pr[:, h % 2, :]
                mm(o[0], w[:, 0:P], v[0], start=True, stop=True, skip_group_check=True)
                mm(o[1], w[:, P:S], v[0], start=True, stop=False, skip_group_check=True)
                mm(o[1], w[:, S:3 * P], v[1], start=False, stop=True, skip_group_check=True).then_inc(stick_pv, 1)

            stick_z(0)
            for s in range(H + 1):
                if s + 1 < H:
                    stick_z(s + 1)
                if s < H:
                    stick_suffix(s)
                if s >= 1:
                    stick_out(s - 1)
            turn_otok(4, 2)
            for m in range(KT):
                y_unit("cd", m, base + 18 + m, (unit_used[2],) if m == 7 else ())
            norm_sums("B2")
            norm_sums_with("A3", 3, N_JOBS + 32, acc0)
            ffn("f1", 3)
            norm_sums("B3")
            norm_sums_with("A4", 4, N_JOBS + 64, acc1)

            base = BASE["sb"]
            for e in range(14):
                project("sb", e, 16 if e == 0 else None)
                turn_values("sb", e)
                if 1 <= e <= 5:
                    pe.wait_ge(qk_sq, e)
                    out = bank[(2, 2, 3, 3, 6)[e - 1]][:, ((e - 1) % 2) * S:((e - 1) % 2 + 1) * S]
                    mm(out, const("blockones"), tt[:, e - 1, :], start=True, stop=True,
                       skip_group_check=True).then_inc(qk_ms, 1)
                if e == 8:
                    for n, tiles in enumerate(qk_tiles):
                        w = 2 if n < 2 else 1
                        pe.wait_ge(qk_n, n + 1)
                        mm(bank[(2, 3, 6)[n]][:, 0:w * S], const("rot"), tiles.rearrange("p a s -> p (a s)"),
                           start=True, stop=True).then_inc(qk_rot, 1)
            turn_values("sb", 14)

            def token_mix(t):
                if t == 0:
                    pe.wait_ge(wst_landed, 16)
                    pe.wait_ge(tokv_ready, 2)
                if t >= 2:
                    pe.wait_ge(tok_ready, t - 1)
                for n in range(2):
                    h = 2 * t + n
                    for c in range(QT):
                        last = mm(bank[2 + t % 2][n * HD:(n + 1) * HD, c * P:(c + 1) * P],
                                  vt[:, c, 1 + t, n * HD:(n + 1) * HD], wst[:, h, :], start=True, stop=True,
                                  skip_group_check=True)
                last.then_inc(tok_psum, 1)

            a0 = 32
            for s in range(H + 2):
                if s < H:
                    a = a0 + s
                    r = slice((s // 4) * HD, (s // 4 + 1) * HD)
                    q, k = proj[r, s % 4, :], proj[r, 4, :]
                    if s == 0:
                        pe.wait_ge(qk_done, 3)
                        pe.wait_ge(proj_done, PROJ0["sb"] + 14)
                    if s >= 2:
                        pe.wait_ge(prob_ready, a - 1)
                    mm(bank[4 + a % 2][:, 0:S], q[:, 0:P], k, start=True, stop=True, skip_group_check=True)
                    mm(bank[4 + a % 2][:, S:2 * S], q[:, P:S], k, start=True, stop=True,
                       skip_group_check=True).then_inc(scores_psum, 1)
                if 1 <= s <= H:
                    transposes(a0 + s - 1, 4)
                if 1 <= s <= 4:
                    token_mix(s - 1)
                if s == 6:
                    pe.wait_ge(tok_ready, 4)
                    for t in range(4):
                        last = mm(bank[2][:, 0:S], ones, sq[:, t // 2, (t % 2) * S:(t % 2 + 1) * S], start=(t == 0),
                                  stop=(t == 3))
                    last.then_inc(tokms, 1)
                if s >= 2:
                    h = s - 2
                    a = a0 + h
                    pe.wait_ge(pt_ready, a + 1)
                    g = h // 4
                    for q in range(QT):
                        for kt in range(QT):
                            last = mm(bank[q][:, h * HD:(h + 1) * HD], pt[:, a % 2, (2 * q + kt) * P:(2 * q + kt + 1) * P],
                                      vt[:, kt, 0, g * HD:(g + 1) * HD], start=(kt == 0), stop=(kt == 1),
                                      skip_group_check=True)
                    last.then_inc(pv_done, 1)
            pe.wait_ge(an_out, 2)
            for b in range(2):
                for n in range(2):
                    for q in range(QT):
                        f = 2 * b + n
                        last = nc.tensor.transpose(bank[4 + b][:, n * S + q * P:n * S + (q + 1) * P],
                                                   otok[:, q, f * P:(f + 1) * P], ident)
                last.then_inc(oT_psum, 1)
            for m in range(KT):
                y_unit("sb", m, base + 14 + m, (unit_used[1], unit_used[2]) if m == 7 else ())
            norm_sums_with("A5", 5, N_JOBS + 64, acc0)
            ffn("f2", 5)
            norm_sums("A6")


def kernel(**inputs):
    import concourse.bacc as _bacc
    from concourse.bass_utils import run_bass_kernel_spmd as _run

    a = {k: np.asarray(v) for k, v in inputs.items()}
    heads = [n for t in range(4) for n in (t, t + 4)]
    paired = np.concatenate([np.arange(h * HD, (h + 1) * HD) for h in heads])

    units = np.zeros((N_UNITS, P, UW), np.float32)

    def columns(at, w, cols):
        for n in range(len(cols) // P):
            sel = w[:, cols[n * P:(n + 1) * P]]
            units[at + n] = sel.reshape(KT, P, P).transpose(1, 0, 2).reshape(P, UW)
        return at + len(cols) // P

    r = np.arange
    w = a["w_in_ab"][0]
    cuts = dict(zip(("qa", "kc", "vc", "ks", "vs", "kw", "vw", "ga", "qb", "kb", "vb"),
                    np.cumsum([0, 512, 128, 128, 128, 128, 128, 128, 24, 512, 128])))
    p = BASE["ab"]
    for name in ("kc", "vc", "ks", "kw", "kb"):
        p = columns(p, w, cuts[name] + r(P))
    for name in ("qa", "qb"):
        p = columns(p, w, cuts[name] + paired)
    for name in ("vs", "vw", "vb"):
        p = columns(p, w, cuts[name] + r(P))
    columns(p, a["w_out_ab"][0], r(D))
    wga = w[:, cuts["ga"]:cuts["ga"] + 24]
    w = a["w_in_cd"][0]
    p = columns(BASE["cd"], w, paired)
    p = columns(p, w, 512 + r(P))
    p = columns(p, w, 768 + r(1024))
    p = columns(p, w, 640 + r(P))
    p = columns(p, w, 1792 + r(512))
    columns(p, a["w_out_cd"][0], r(D))
    w = a["w_in_2"][0]
    p = columns(BASE["sb"], w, paired)
    p = columns(p, w, 512 + r(P))
    p = columns(p, w, 640 + r(P))
    p = columns(p, w, 1280 + r(512))
    p = columns(p, w, 768 + r(512))
    columns(p, a["w_out_2"][0], r(D))
    for name, wi, wo in (("f0", a["ffn_w_in"][0], a["ffn_w_out"][0]), ("f1", a["ffn_w_in"][1], a["ffn_w_out"][1]),
                         ("f2", a["w_up_2"][0], a["w_down_2"][0])):
        for t in range(FT):
            columns(BASE[name] + 3 * t, wi, t * P + r(P))
            columns(BASE[name] + 3 * t + 1, wi, FF + t * P + r(P))
            units[BASE[name] + 3 * t + 2] = wo[t * P:(t + 1) * P]

    def tiles(v):
        return v.reshape(-1, P).T

    params = np.zeros((P, PARAM_COLS), np.float32)

    def put(name, v, rows=P, at=0):
        c0 = PARAM[name][0] + at
        params[:rows, c0:c0 + v.shape[1]] = v

    put("c", tiles(a["c"][0]))
    put("c", tiles(a["c_2"][0]), at=KT)
    for m in range(4):
        put("modb", tiles(a["mod_b"][m // 2, m % 2]), at=24 * m)
    put("modb", tiles(a["b_ada_2"][0]), at=96)
    put("normw", tiles(a["norm_w"].reshape(-1)))
    put("normw", tiles(a["g_norm1_2"][0]), at=64)
    put("normw", tiles(a["g_norm2_2"][0]), at=72)
    put("normw", tiles(a["g_final_2"]), at=80)
    put("gout", tiles(a["g_attn_out_2"][0]))
    put("gout", tiles(a["g_tok_out_2"][0]), at=4)
    put("gqk", np.tile(a["g_q_2"][0], 2)[:, None])
    put("gqk", np.tile(a["g_k_2"][0], 2)[:, None], at=1)
    put("gtokv", np.tile(a["g_tok_v_2"], (P, 1)))
    put("sinks", np.tile(a["swa_sinks"], (P, 1)))
    put("pe", np.tile(a["nsa_cmp_pe"][0].T, (2, 1)))
    put("wga", wga.reshape(KT, P, 24).transpose(1, 0, 2).reshape(P, -1))
    cw = np.concatenate([a["w_conv_2"][0], a["b_conv_2"]], 0)
    cw = cw.reshape(4, 2, FT, P).transpose(3, 2, 1, 0)
    put("conv", cw.reshape(P, -1))
    bs = a["b_s_2"][0].reshape(4, 2, P)
    put("bs", np.repeat(bs.transpose(1, 0, 2), HD, 0).reshape(P, -1))
    put("reltab", a["rel_table"], REL)
    blk = np.zeros((4, REL, 4, H), np.float32)
    for n in range(4):
        blk[n, :, n, :] = a["rel_table"][:, :H]
    put("relblock", blk.reshape(P, 32))
    consts, early = shape_constants()
    arrays = {
        "weights": units,
        "mod_w": np.ascontiguousarray(a["mod_w"].reshape(4, D, MW)),
        "w_ada": np.ascontiguousarray(a["w_ada_2"][0]),
        "params": params,
        "consts": consts,
        "early": early,
        "xT": np.ascontiguousarray(a["x"][0].T.reshape(KT, P, S).transpose(1, 0, 2)),
        "cmp_w": np.ascontiguousarray(np.stack([a["nsa_cmp_wk"][0].transpose(1, 0, 2),
                                                a["nsa_cmp_wv"][0].transpose(1, 0, 2)])),
        "w_s": np.ascontiguousarray(a["w_s_2"][0].transpose(2, 0, 1)),
    }
    nc = _bacc.Bacc("TRN2", target_bir_lowering=False, num_devices=1)
    aps = {n: nc.dram_tensor(f"in_{n}", v.shape, F32, kind="ExternalInput").ap() for n, v in arrays.items()}
    aps["table"] = nc.dram_tensor("bias_table", (COPIES, 16, 512), F32, kind="Internal").ap()
    aps["out"] = nc.dram_tensor("out_dram", (P, KT, S), F32, kind="ExternalOutput").ap()
    build_program(nc, aps)
    res = _run(nc, [{f"in_{n}": v for n, v in arrays.items()}], core_ids=[0])
    y = res.results[0]["out_dram"]
    return np.ascontiguousarray(y.transpose(1, 0, 2).reshape(D, S).T)[None]
```

```python
import math
from contextlib import ExitStack

import numpy as np

import concourse.bass as bass
from concourse import mybir

F32 = mybir.dt.float32
F32R = mybir.dt.float32r
ALU = mybir.AluOpType
ACT = mybir.ActivationFunctionType
AX = mybir.AxisListType.X

P = 128
D = 1024
KT = D // P
S = 256
QT = S // P
HD = 64
H = 8
G = 2
FF = 2816
FT = FF // P
REL = 32
NCMP, CLEN, CSTR = 15, 32, 16
EPS = 1e-6
BIG = 1e30
UW = 1024
COPIES = 16
RING = 6
MW = 3 * D
MC = MW // 2

AB_UNITS, CD_UNITS, SB_UNITS = 24, 27, 24
FFN_UNITS = 3 * FT
BASE = {}
_p = 0
for _name, _n in (("ab", AB_UNITS), ("f0", FFN_UNITS), ("cd", CD_UNITS), ("f1", FFN_UNITS),
                  ("sb", SB_UNITS), ("f2", FFN_UNITS)):
    BASE[_name] = _p
    _p += _n
N_UNITS = _p

CONST = {}
_c = 0
for _name, _n in (("ident", P), ("ones", P), ("blockones", P), ("rot", P), ("tri", P), ("neg1", P),
                  ("cos", S), ("sin", S), ("stickmask", 3 * P), ("cmpmask", QT * 16),
                  ("rowvalid", QT), ("select", P), ("headmask", H)):
    CONST[_name] = (_c, _n)
    _c += _n
CONST_COLS = _c
EARLY = {}
_c = 0
for _name, _n in (("onehot_cmp", 4 * S), ("onehot_rel", 512), ("negmask", 512)):
    EARLY[_name] = (_c, _n)
    _c += _n
EARLY_COLS = _c
PARAM = {}
_c = 0
for _name, _n in (("c", 2 * KT), ("modb", 6 * 24), ("normw", 11 * KT), ("gout", 8), ("gqk", 2),
                  ("gtokv", HD), ("sinks", H), ("pe", CLEN), ("wga", KT * 24), ("conv", FT * 8),
                  ("bs", 4 * P), ("reltab", 16), ("relblock", 32)):
    PARAM[_name] = (_c, _n)
    _c += _n
PARAM_COLS = _c


def rel_bucket(dist):
    n = np.maximum(dist, 0)
    nf = np.maximum(n, 1).astype(np.float32)
    large = 16 + (np.log(nf / np.float32(16)) / np.float32(math.log(8.0)) * np.float32(16)).astype(np.int32)
    return np.where(n < 16, n, np.minimum(large, 31))


def shape_constants():
    c = np.zeros((P, CONST_COLS), np.float32)
    e = np.zeros((P, EARLY_COLS), np.float32)

    def put(name, a, to=c, where=CONST):
        at, n = where[name]
        a = np.asarray(a, np.float32).reshape(a.shape[0], -1)
        assert a.shape[1] == n, name
        to[:a.shape[0], at:at + n] = a

    i = np.arange(P)
    put("ident", np.eye(P))
    put("ones", np.ones((P, P)))
    put("blockones", (i[:, None] // HD == i[None, :] // HD).astype(np.float32))
    rot = np.zeros((P, P), np.float32)
    for m in range(P):
        if m % 32 < 16:
            rot[m + 16, m] = -1.0
        else:
            rot[m - 16, m] = 1.0
    put("rot", rot)
    put("tri", -(i[:, None] >= i[None, :]).astype(np.float32))
    put("neg1", -np.ones((P, P)))
    t = np.arange(S)
    inv = np.power(np.float32(10000.0), -np.arange(0, 32, 2, dtype=np.float32) / np.float32(32))
    ang_r = (t // 64).astype(np.float32)[:, None] * inv[None]
    ang_c = (t % 64).astype(np.float32)[:, None] * inv[None]
    ang = np.concatenate([ang_r, ang_r, ang_c, ang_c] * 2, -1).T
    put("cos", np.cos(ang))
    put("sin", np.sin(ang))
    tri = np.where(i[:, None] < i[None, :], 0.0, -BIG)
    put("stickmask", np.concatenate([tri, np.zeros((P, P)), tri], 1))
    q = np.arange(S)
    n = np.arange(16)
    dist = q[:, None] - (CSTR * n + CLEN - 1)[None]
    ok = (dist >= 0) & (n < NCMP)[None]
    put("cmpmask", np.where(ok, 0.0, BIG).reshape(QT, P, 16).transpose(1, 0, 2))
    put("rowvalid", ok.any(1).astype(np.float32).reshape(QT, P).T)
    sel = np.zeros((NCMP, P), np.float32)
    for h in range(H):
        for m in range(NCMP):
            sel[m, h * 16 + m] = 1.0
    put("select", sel)
    put("headmask", (i[:, None] // 16 == np.arange(H)[None]).astype(np.float32))
    hot = np.zeros((4, REL, 4, S), np.float32)
    for m in range(NCMP):
        hot[m % 4, rel_bucket(dist[:, m]), m // 4, q] = 1.0
    put("onehot_cmp", hot.reshape(P, 4 * S), e, EARLY)
    far = 255 - np.arange(512)
    hot = np.zeros((REL, 512), np.float32)
    hot[rel_bucket(far), np.arange(512)] = 1.0
    put("onehot_rel", hot, e, EARLY)
    neg = np.zeros((16, 512), np.float32)
    neg[:, far < 0] = BIG
    neg[8:, far >= 128] = BIG
    put("negmask", neg, e, EARLY)
    return c, e


class Count:

    def __init__(self, sem):
        self.sem, self.n, self.i, self.per = sem, 0, None, 0

    def inc(self, ins):
        ins.then_inc(self.sem, 1)
        self.n += 1
        return ins

    def now(self):
        return self.n if self.i is None else self.i * self.per + self.n

    def enter(self, i, per):
        self.i, self.per, self.first = i, per, self.n

    def leave(self, turns):
        assert self.n - self.first == self.per, (self.n - self.first, self.per)
        self.n = self.first + turns * self.per
        self.i = None


def build_program(nc, A):
    with ExitStack() as ctx:
        def sb(name, shape, dt=F32):
            return ctx.enter_context(nc.sbuf_tensor(name, shape, dt))

        def sem(name):
            return ctx.enter_context(nc.semaphore(name))

        x = sb("x", [P, KT, S])
        hH = sb("hH", [P, KT, S], F32R)
        hL = sb("hL", [P, KT, S], F32R)
        raw = sb("raw", [P, RING, UW])
        wH = sb("wH", [P, RING, UW], F32R)
        wL = sb("wL", [P, RING, UW], F32R)
        modbuf = sb("modbuf", [P, 2, MC])
        acc0 = sb("acc0", [P, MW])
        proj = sb("proj", [P, 13, S])
        acc1 = proj[:, :, :].rearrange("p a b -> p (a b)")[:, 0:MW]
        early = proj[:, :, :].rearrange("p a b -> p (a b)")[:, 0:EARLY_COLS]
        vt = sb("vt", [P, QT, 5, P])
        strips = sb("strips", [P, 16, S])
        cw = strips[:, :, :].rearrange("p (g a) b -> p g (a b)", g=G).rearrange(
            "p g (l e) -> p g l e", e=HD)
        wst = strips[:, 0:4, :].rearrange("p a (b c) -> p (a b) c", b=2)
        bc = sb("bc", [P, QT, 16, H])
        otok = sb("otok", [P, QT, D])
        tt = otok[:, :, :].rearrange("p q (k s) -> p (q k) s", s=S)
        sn = sb("sn", [P, 2, 512])
        pr = sb("pr", [P, 2, 512])
        pt = sb("pt", [P, 2, 512])
        sq = sb("sq", [P, 2, 512])
        lnms = sb("lnms", [P, S])
        rstd = sb("rstd", [P, S])
        aH = sb("aH", [P, 2, S], F32R)
        aL = sb("aL", [P, 2, S], F32R)
        gwH = sb("gwH", [P, KT, 24], F32R)
        gwL = sb("gwL", [P, KT, 24], F32R)
        con = sb("con", [P, CONST_COLS])
        par = sb("par", [P, PARAM_COLS])
        mv = sb("mv", [P, 6, 24])
        sc1 = sb("sc1", [P, 6, KT])
        gw1 = sb("gw1", [P, 6, KT])
        csil = sb("csil", [P, KT])
        epst = sb("epst", [P, 1])
        nm = sb("nm", [P, 48, QT])
        sm = sb("sm", [P, 48, QT])
        rg = sb("rg", [P, H, QT])
        gt = sb("gt", [P, QT, 24])
        nsink = sb("nsink", [P, H])
        qgain = sb("qgain", [P, 1])
        sinkx = sb("sinkx", [P, H, QT])
        kc = sb("kc", [P, 16])
        kcs = sb("kcs", [16, P])
        vcs = sb("vcs", [16, P])
        cm = sb("cm", [P, 3, 16])
        small = sb("small", [P, 64])

        bank = [ctx.enter_context(nc.psum_tensor(f"bank{i}", [P, 512], F32)) for i in range(8)]

        def const(name, rows=P):
            at, n = CONST[name]
            return con[0:rows, at:at + n]

        def param(name, rows=P):
            at, n = PARAM[name]
            return par[0:rows, at:at + n]

        def early_const(name, rows=P):
            at, n = EARLY[name]
            return early[0:rows, at:at + n]

        ident, ones = const("ident"), const("ones")
        normw = param("normw").rearrange("p (n k) -> p n k", k=KT)
        modb = param("modb").rearrange("p (m j) -> p m j", j=24)
        cvec = param("c").rearrange("p (n k) -> p n k", k=KT)
        conv = param("conv").rearrange("p (t c) -> p t c", c=8)
        xfl = x[:, :, :].rearrange("p k s -> p (k s)")
        hHf = hH[:, :, :].rearrange("p k s -> p (k s)")
        hLf = hL[:, :, :].rearrange("p k s -> p (k s)")
        ttf = tt.rearrange("p k s -> p (k s)")

        small_landed = sem("small_landed")
        x_landed = sem("x_landed")
        early_landed = sem("early_landed")
        raw_full = [sem(f"raw_full{i}") for i in range(RING)]
        hi_ready = [sem(f"hi_ready{i}") for i in range(3)]
        lo_ready = [sem(f"lo_ready{i}") for i in range(3)]
        unit_used = [sem(f"unit_used{i}") for i in range(3)]
        mod_full = [sem(f"mod_full{i}") for i in range(2)]
        start_full = [sem(f"start_full{i}") for i in range(6)]
        mod_used = sem("mod_used")
        acc_zero = sem("acc_zero")
        cw_zero = sem("cw_zero")
        cw_landed = sem("cw_landed")
        table_out = sem("table_out")
        strips_landed = sem("strips_landed")
        wst_landed = sem("wst_landed")
        misc_psum = sem("misc_psum")
        misc_taken = sem("misc_taken")
        sq_ready = sem("sq_ready")
        sq_used = sem("sq_used")
        pair_ready = sem("pair_ready")
        rstd_ready = sem("rstd_ready")
        x_ready = sem("x_ready")
        y_ready = sem("y_ready")
        hf_ready = sem("hf_ready")
        hH_ready = sem("hH_ready")
        h_ready = sem("h_ready")
        proj_done = sem("proj_done")
        v_turned = sem("v_turned")
        v_ready = sem("v_ready")
        gw_ready = sem("gw_ready")
        gate_exp = sem("gate_exp")
        cmp_sub = sem("cmp_sub")
        cmp_exp = sem("cmp_exp")
        kpe_ready = sem("kpe_ready")
        scores_psum = sem("scores_psum")
        neg_ready = sem("neg_ready")
        prob_ready = sem("prob_ready")
        pt_psum = sem("pt_psum")
        pt_ready = sem("pt_ready")
        pv_done = sem("pv_done")
        o_taken = sem("o_taken")
        sink_in = sem("sink_in")
        sink_exp = sem("sink_exp")
        otok_ready = sem("otok_ready")
        oT_psum = sem("oT_psum")
        oT_ready = sem("oT_ready")
        oTH_ready = sem("oTH_ready")
        z_psum = sem("z_psum")
        zabs_ready = sem("zabs_ready")
        zlog_ready = sem("zlog_ready")
        sp_ready = sem("sp_ready")
        suf_psum = sem("suf_psum")
        fw_ready = sem("fw_ready")
        w_ready = sem("w_ready")
        stick_pv = sem("stick_pv")
        silu_ready = sem("silu_ready")
        af_ready = sem("af_ready")
        aH_ready = sem("aH_ready")
        aL_ready = sem("aL_ready")
        zc_ready = sem("zc_ready")
        conv_ready = sem("conv_ready")
        csil_ready = sem("csil_ready")
        eps_ready = sem("eps_ready")
        dve_done = sem("dve_done")
        act_done = sem("act_done")
        qk_sq = sem("qk_sq")
        qk_ms = sem("qk_ms")
        qk_rstd = sem("qk_rstd")
        qk_n = sem("qk_n")
        qk_rot = sem("qk_rot")
        qk_done = sem("qk_done")
        tokv_sq = sem("tokv_sq")
        tokv_ms = sem("tokv_ms")
        tokv_rstd = sem("tokv_rstd")
        tokv_ready = sem("tokv_ready")
        tok_psum = sem("tok_psum")
        tok_ready = sem("tok_ready")
        tokms = sem("tokms")
        tokrstd = sem("tokrstd")
        an_in = sem("an_in")
        an_out = sem("an_out")
        mixf_ready = sem("mixf_ready")
        mixH_ready = sem("mixH_ready")
        out_ready = sem("out_ready")
        out_stored = sem("out_stored")

        NORMS = ["A0", "B0", "A1", "B1", "A2", "B2", "A3", "B3", "A4", "A5", "A6"]
        MISC = ["table", "bc", "mod0a", "cmpk", "kcT", "cmpv", "vrep", "mod0g", "cscore", "gates", "gatesT", "cpt0",
                "cpt1", "cpv0", "cpv1", "mod1a", "mod1g", "mod2a", "mod2g", "mod3a", "mod3g", "mod4a", "mod4g",
                "mod5a", "mod5g"]
        misc = {name: i for i, name in enumerate(MISC)}
        PROJ0 = {"ab": 0, "cd": 16, "sb": 34}
        NPROJ = {"ab": 16, "cd": 18, "sb": 14}
        VALUES = {"ab": (range(13, 16), 0), "cd": (range(13, 18), 3), "sb": (range(5, 10), 8)}
        ATT = {"ab": [(0, 5, 2, 0, 0), (8, 5, 3, 1, 0), (16, 9, 4, 2, 8)], "cd": [(24, 0, 4, 0, 0)],
               "sb": [(32, 0, 4, 0, None)]}
        gates_f = sq[0:24, 0, S:2 * S]
        MIX_ORDER = (2, 3, 0, 1)

        def mix_src(b):
            if b < 2:
                return sn[:, b, :]
            return proj[:, 5 + 2 * (b - 2):7 + 2 * (b - 2), :].rearrange("p a s -> p (a s)")

        def slot_of(a):
            return 0 if 24 <= a < 32 else a % 2

        def slot_freed(a):
            return a if 24 <= a < 32 else a - 1

        def proj_bank(phase, e):
            last = NPROJ[phase] - e
            return bank[4 + e % 2] if last > 2 or phase == "sb" else bank[4 - last]

        stick_z_buf = [sq[:, n, 0:384] for n in range(2)]
        stick_sp = [otok[:, n, 512:896] for n in range(2)]
        stick_w = [pr[:, 1, 0:384], sn[:, 1, 0:384]]
        qk_rs = (sn[:, 0, :], sn[:, 1, :], pt[:, 0, 0:S])
        qk_tiles = (proj[:, 0:2, :], proj[:, 2:4, :], proj[:, 4:5, :])
        TILE0 = {"f0": 0, "f1": FT, "f2": 2 * FT}
        def mod_jobs(m):
            return [(m, k, n * MC, MC) for k in range(KT) for n in range(2)]

        JOBS = ([(0, k, n * D, D) for n in range(2) for k in range(KT)] + [(0, k, 2 * D, D) for k in range(KT)]
                + mod_jobs(1) + mod_jobs(2) + mod_jobs(3) + mod_jobs(4) + mod_jobs(5))
        JOBS_AT_START = 2 * KT
        JOBS_END = [JOBS_AT_START + KT + 2 * KT * m for m in range(6)]
        assert JOBS_END[-1] == len(JOBS)

        def jobs_done(phase, e):
            if phase == "ab":
                return JOBS_AT_START + min(KT, e + 1) if e < 100 else JOBS_END[0] + min(16, (e - 100) * 2 // 3)
            at = JOBS_END[2 if phase == "cd" else 4]
            n = NPROJ[phase]
            if phase == "cd":
                return at + min(10, (e * 5 + 5) // 8)
            return at + min(n // 2, (e + 1) // 2) if e < 100 else at + min(16, n // 2 + (e - 99))
        start_slots = ([modbuf[:, :, :].rearrange("p a b -> p (a b)")[:, n * D:(n + 1) * D] for n in range(3)]
                       + [otok[:, q, :] for q in range(QT)]
                       + [vt[:, :, :, :].rearrange("p q a b -> p (q a b)")[:, 0:D]])
        SLOTS = len(start_slots)

        def job_value(q):
            return 16 * ((q - JOBS_AT_START) // 2 + 1)

        def job_buffer(q):
            width = JOBS[q][3]
            if q < JOBS_AT_START:
                return start_slots[q % SLOTS], start_full[q % SLOTS], 16 * (q // SLOTS + 1)
            return modbuf[:, q % 2, 0:width], mod_full[q % 2], job_value(q)
        mod_src = [A["mod_w"][m] for m in range(4)] + [A["w_ada"][:, 0:MW], A["w_ada"][:, MW:2 * MW]]

        def cls(p):
            return p % 3, p // 3 + 1

        def wait_unit(eng, p):
            c, n = cls(p)
            eng.wait_ge(unit_used[c], n)

        Y_UNIT = {"ab": BASE["ab"] + 16, "cd": BASE["cd"] + 18, "sb": BASE["sb"] + 14}
        FIDX = {"f0": 0, "f1": 1, "f2": 2}

        def wait_y(eng, phase, b):
            if phase in Y_UNIT:
                wait_unit(eng, Y_UNIT[phase] + 2 * b + 1)
            elif b < 3:
                eng.wait_ge(y_ready, 3 * FIDX[phase] + b + 1)
            else:
                wait_unit(eng, BASE[phase] + 3 * FT - 1)

        def bcast(ap, shape):
            return ap.broadcast_to(shape)

        def add_pairs(eng, tensor_tensor, norm):
            n = NORMS.index(norm)
            for b in range(4):
                eng.wait_ge(sq_ready, 4 * n + b + 1)
                tensor_tensor(sq[:, b % 2, 0:S], sq[:, b % 2, 0:S], sq[:, b % 2, S:2 * S],
                              ALU.add).then_inc(pair_ready, 1)

        block = ctx.enter_context(nc.Block())

        @block.sync
        def _(sp):
            def load_unit(p, b=None, i=None):
                if p >= N_UNITS and i is None:
                    return
                c, n = cls(p)
                slot = p % RING
                if i is None:
                    if p >= RING:
                        sp.wait_ge(lo_ready[c], n - 2)
                    src = A["weights"][p]
                else:
                    sp.wait_ge(lo_ready[c], i * 2 + (n - 2))
                    src = A["weights"][bass.ds(i * RING + p, 1)].rearrange("o p n -> (o p) n")
                sp.dma_start(raw[:, slot, :], src).then_inc(raw_full[slot], 16)

            def load_job(q):
                m, k, col, width = JOBS[q]
                depth = SLOTS if q < JOBS_AT_START else 2
                if q >= depth:
                    sp.wait_ge(mod_used, q - depth + 1)
                dst, landed, _ = job_buffer(q)
                sp.dma_start(dst, mod_src[m][k * P:(k + 1) * P, col:col + width]).then_inc(landed, 16)

            sp.dma_start(par[:, :], A["params"]).then_inc(small_landed, 16)
            sp.dma_start(con[:, :], A["consts"]).then_inc(small_landed, 16)
            sp.dma_start(x[:, :, :], A["xT"]).then_inc(x_landed, 16)
            for q in range(SLOTS):
                load_job(q)
            sp.dma_start(early, A["early"]).then_inc(early_landed, 16)
            for q in range(SLOTS, JOBS_AT_START):
                load_job(q)
            sp.wait_ge(misc_taken, misc["table"] + 1)
            sp.dma_start(A["table"].rearrange("b h n -> h b n"),
                         pt[0:16, 1:2, :].broadcast_to((16, COPIES, 512))).then_inc(table_out, 16)
            for p in range(2):
                load_unit(p)
            sp.wait_ge(cw_zero, 1)
            for g in range(G):
                sp.dma_start(cw[g * HD:(g + 1) * HD, g], A["cmp_w"][0]).then_inc(cw_landed, 16)
            for p in range(2, RING):
                load_unit(p)
            done = JOBS_AT_START
            for e in range(24):
                load_unit(e + RING)
                up = jobs_done("ab", e) if e < 16 else JOBS_END[1] if e >= 19 else done
                for q in range(done, up):
                    load_job(q)
                done = up
                if e == 4:
                    sp.wait_ge(misc_psum, misc["cmpk"] + 1)
                    for g in range(G):
                        sp.dma_start(cw[g * HD:(g + 1) * HD, g], A["cmp_w"][1]).then_inc(cw_landed, 16)
                if e == 9:
                    sp.wait_ge(misc_psum, misc["cmpv"] + 1)
                    sp.wait_ge(table_out, 16)
                    for a in range(P // COPIES):
                        diag = bass.AP(A["table"].tensor, P - 1 - COPIES * a,
                                       [[16 * 512 - 1, COPIES], [512, 16], [1, S]])
                        sp.dma_start(strips[COPIES * a:COPIES * (a + 1), :, :],
                                     diag).then_inc(strips_landed, 16)

            def ffn(base, m):
                def step(t, i=None, jobs=False):
                    for c in range(3):
                        p = base + 3 * (t + 2) + c
                        if i is None:
                            load_unit(p)
                        else:
                            load_unit(p, i=i)
                    if jobs:
                        n = t % 2
                        q = JOBS_END[m - 1] + n
                        sp.wait_ge(mod_used, i * 2 + (q - 1))
                        src = mod_src[m][bass.ds(i * P, P), n * MC:(n + 1) * MC]
                        sp.dma_start(modbuf[:, q % 2, :], src).then_inc(mod_full[q % 2], 16)

                step(0)
                step(1)
                with sp.Fori(0, KT) as i:
                    step(2, i, m is not None)
                    step(3, i, m is not None)
                for t in range(2 + 2 * KT, FT):
                    step(t)

            def jobs_between(phase, e, done):
                up = (jobs_done(phase, e) if e < NPROJ[phase] else done if e < NPROJ[phase] + 2 else
                      JOBS_END[5] if phase == "sb" else min(done + 2, JOBS_END[3]))
                for q in range(done, up):
                    load_job(q)
                return up

            ffn(BASE["f0"], 2)
            done = JOBS_END[2]
            for e in range(CD_UNITS):
                load_unit(BASE["cd"] + e + RING)
                done = jobs_between("cd", e, done)
            ffn(BASE["f1"], 4)
            done = JOBS_END[4]
            for e in range(SB_UNITS):
                load_unit(BASE["sb"] + e + RING)
                done = jobs_between("sb", e, done)
                if e == 0:
                    sp.dma_start(wst, A["w_s"]).then_inc(wst_landed, 16)
            ffn(BASE["f2"], None)
            for b in range(4):
                sp.wait_ge(out_ready, b + 1)
                sp.dma_start(A["out"][:, 2 * b:2 * b + 2, :], tt[:, 2 * b:2 * b + 2, :]).then_inc(out_stored, 16)
            sp.wait_ge(out_stored, 64)

        @block.gpsimd
        def _(pool):
            def split_low(b, par_=None, i=None):
                slot = 3 * (b % 2) + 2
                n = b + 1
                pool.wait_ge(hi_ready[2], n if i is None else i * 2 + n)
                nc.gpsimd.tensor_tensor(wL[:, slot, :], raw[:, slot, :], wH[:, slot, :].bitcast(F32),
                                        ALU.subtract).then_inc(lo_ready[2], 1)

            nc.gpsimd.memset(strips[:, :, :], 0.0).then_inc(cw_zero, 1)
            nc.gpsimd.memset(epst[:, :], EPS).then_inc(eps_ready, 1)

            def plain(first, last):
                for b in range(first, last):
                    split_low(b)

            def looped(b0):
                with pool.Fori(0, 8) as i:
                    split_low(b0, i=i)
                    split_low(b0 + 1, i=i)

            def zero_acc1():
                nc.gpsimd.memset(acc1, 0.0).then_inc(acc_zero, 1)

            def pairs(norm):
                add_pairs(pool, nc.gpsimd.tensor_tensor, norm)

            f0, cd, f1, sb0, f2 = (BASE[f] // 3 for f in ("f0", "cd", "f1", "sb", "f2"))
            pairs("A0")
            plain(0, f0 + 1)
            pairs("A1")
            wait_y(pool, "ab", 3)
            zero_acc1()
            plain(f0 + 1, f0 + 3)
            looped(f0 + 3)
            plain(f0 + 19, cd + 1)
            pairs("A2")
            plain(cd + 1, f1 + 1)
            pairs("A3")
            wait_y(pool, "cd", 3)
            zero_acc1()
            plain(f1 + 1, f1 + 3)
            looped(f1 + 3)
            plain(f1 + 19, sb0 + 1)
            pairs("A4")
            plain(sb0 + 1, f2 + 1)
            pairs("A5")
            plain(f2 + 1, f2 + 3)
            looped(f2 + 3)
            plain(f2 + 19, N_UNITS // 3)
            pairs("A6")

        @block.scalar
        def _(act):
            chain = Count(act_done)

            def link(ins):
                chain.inc(ins)
                act.wait_ge(chain.sem, chain.now())

            class Cursor:
                at = 0
            hi = Cursor()

            def split_high(p, i=None):
                c, n = cls(p)
                slot = p % RING
                if i is None:
                    act.wait_ge(raw_full[slot], 16 * (p // RING + 1))
                    if p >= RING:
                        act.wait_ge(unit_used[c], n - 2)
                else:
                    act.wait_ge(raw_full[slot], i * 16 + 16 * (p // RING + 1))
                    act.wait_ge(unit_used[c], i * 2 + (n - 2))
                nc.scalar.activation(wH[:, slot, :], raw[:, slot, :], ACT.Copy).then_inc(hi_ready[c], 1)

            def split_upto(n):
                while hi.at < min(n, N_UNITS):
                    split_high(hi.at)
                    hi.at += 1

            def norm_rstd(n):
                act.wait_ge(sq_used, 4 * n + 4)
                link(nc.scalar.activation(lnms[:, :], bank[6][:, 0:S], ACT.Ln, bias=epst[:, 0:1], scale=1.0 / D))
                nc.scalar.activation(rstd[:, :], lnms[:, :], ACT.Exp, scale=-0.5).then_inc(rstd_ready, 1)

            def squares(n, ready, src):
                for b in range(4):
                    ready(b)
                    if 4 * n + b >= 2:
                        act.wait_ge(sq_used, 4 * n + b - 1)
                    nc.scalar.activation(sq[:, b % 2, :], src(b), ACT.Square).then_inc(sq_ready, 1)

            def norm_a(a, split_first=False):
                n = NORMS.index(f"A{a}")
                squares(n, lambda b: act.wait_ge(x_landed, 16) if a == 0 else act.wait_ge(x_ready, 4 * a - 4 + b + 1),
                        lambda b: xfl[:, b * 512:(b + 1) * 512])
                norm_rstd(n)
                if split_first:
                    split_upto(3)
                if a < 6:
                    for b in range(4):
                        act.wait_ge(hf_ready, 4 * a + b + 1)
                        if b == 0:
                            act.wait_ge(misc_taken, misc[f"mod{a}a"] + 1)
                        for k in range(2 * b, 2 * b + 2):
                            last = nc.scalar.activation(hH[:, k, :], tt[:, k, :], ACT.Identity,
                                                        bias=mv[:, a, k:k + 1])
                        last.then_inc(hH_ready, 1)

            def norm_b(i, phase):
                n = NORMS.index(f"B{i}")
                squares(n, lambda b: wait_y(act, phase, b), lambda b: bank[b][:, :])
                norm_rstd(n)

            def take_proj(phase, e, dst, scale=1.0, func=ACT.Copy):
                wait_unit(act, BASE[phase] + e)
                nc.scalar.activation(dst, proj_bank(phase, e)[:, 0:S], func, scale=scale).then_inc(proj_done, 1)

            def take_value(phase, e, func=ACT.Copy):
                tiles, first = VALUES[phase]
                n = first + e - tiles[0]
                if e - tiles[0] >= 2:
                    act.wait_ge(v_turned, n - 1)
                take_proj(phase, e, sq[:, n % 2, 0:S], func=func)

            def exp_rows(a, buf, src_banks=None):
                act.wait_ge(neg_ready, a + 1)
                if src_banks is None:
                    cuts = ((0, P), (P, 3 * P))
                else:
                    cuts = ((0, S), (S, 2 * S))
                for q, (lo, up) in enumerate(cuts):
                    src = sn[:, buf, lo:up] if src_banks is None else src_banks[:, lo:up]
                    last = nc.scalar.activation(pr[:, buf, lo:up], src, ACT.Exp, bias=nm[:, a, q:q + 1],
                                                scale=-1.0, accum_out=sm[:, a, q:q + 1])
                last.then_inc(prob_ready, 1)

            def oT_high(o0, n=4):
                for b in range(n):
                    act.wait_ge(oT_psum, o0 + b + 1)
                    nc.scalar.activation(hHf[:, b * 512:(b + 1) * 512], bank[4 + b % 2][:, :],
                                         ACT.Copy).then_inc(oTH_ready, 1)

            def ffn(phase, norm):
                base = BASE[phase]
                g0 = TILE0[phase]

                def step(t, i=None):
                    def at(n, per):
                        return n if i is None else i * per + n

                    b = base + 3 * (t + 1)
                    split = t < FT - 1 or base + 3 * FT < N_UNITS
                    for c in range(2):
                        if split:
                            split_high(b + c, i)
                    act.wait_ge(unit_used[1], at((base + 3 * t + 1) // 3 + 1, 2))
                    bk = bank[4 + t % 2]
                    if phase != "f2":
                        nc.scalar.activation(sn[:, t % 2, 0:S], bk[:, 0:S], ACT.Silu).then_inc(silu_ready, 1)
                    else:
                        row = conv[:, t] if i is None else conv[:, bass.ds(i * 2 + t, 1)].rearrange("p o c -> p (o c)")
                        for n in range(2):
                            last = nc.scalar.activation(pr[:, t % 2, n * S:(n + 1) * S], bk[:, n * S:(n + 1) * S],
                                                        ACT.Identity, bias=row[:, 4 * n + 3:4 * n + 4],
                                                        scale=row[:, 4 * n + 1:4 * n + 2])
                        last.then_inc(zc_ready, 1)
                        act.wait_ge(conv_ready, at(t + 1, 2))
                        nc.scalar.activation(sn[:, t % 2, 0:S], pr[:, t % 2, 0:S], ACT.Silu).then_inc(silu_ready, 1)
                    if split:
                        split_high(b + 2, i)
                    act.wait_ge(af_ready, at(g0 + t + 1, 2))
                    if t >= 2:
                        act.wait_ge(unit_used[2], at((base + 3 * (t - 2) + 2) // 3 + 1, 2))
                    nc.scalar.activation(aH[:, t % 2, :], sn[:, t % 2, S:2 * S], ACT.Copy).then_inc(aH_ready, 1)

                step(0)
                step(1)
                with act.Fori(0, 8) as i:
                    step(2, i)
                    step(3, i)
                for t in range(18, FT):
                    step(t)
                hi.at = base + 3 * FT + 3
                nc.scalar.preload_act_table_set("natural_log_exp_and_others")
                if norm is not None:
                    norm_b(norm, phase)

            act.wait_ge(small_landed, 32)
            nc.scalar.activation(csil[:, :], cvec[:, 1, :], ACT.Silu).then_inc(csil_ready, 1)
            nc.scalar.preload_act_table_set("natural_log_exp_and_others")
            nc.scalar.activation(gwH[:, :, :].rearrange("p k n -> p (k n)"), param("wga"), ACT.Copy).then_inc(gw_ready, 1)
            act.wait_ge(eps_ready, 1)

            norm_a(0, split_first=True)
            act.wait_ge(misc_taken, misc["bc"] + 1)
            for e in range(16):
                split_upto(min(e + 5, 27))
                if e == 12:
                    act.wait_ge(cmp_sub, 1)
                    nc.scalar.activation(pr[:, 0, 0:S], sn[:, 0, 0:S], ACT.Exp, scale=-1.0).then_inc(cmp_exp, 1)
                if e == 15:
                    act.wait_ge(misc_psum, misc["cpt1"] + 1)
                    exp_rows(0, 0)
                if e < 13:
                    scale = -0.125 if e >= 5 else 1.0
                    take_proj("ab", e, proj[:, e, :], scale)
                else:
                    take_value("ab", e)
                if e == 13:
                    act.wait_ge(misc_taken, misc["gatesT"] + 1)
                    nc.scalar.activation(small[:, 0:48], gt[:, :, :].rearrange("p q n -> p (q n)"), ACT.Exp,
                                         scale=-1.0).then_inc(gate_exp, 1)
            for a in range(1, 24):
                if a >= 2:
                    act.wait_ge(pt_psum, a - 1)
                exp_rows(a, a % 2)
            act.wait_ge(sink_in, 1)
            nc.scalar.activation(sinkx[:, :, :], sinkx[:, :, :], ACT.Exp).then_inc(sink_exp, 1)
            oT_high(0)
            for e in range(16, 24):
                split_upto(min(e + 5, 27))
            norm_b(0, "ab")
            norm_a(1)
            ffn("f0", 1)
            norm_a(2)

            act.wait_ge(misc_psum, misc["mod2g"] + 1)
            base = BASE["cd"]
            end = base + CD_UNITS
            for e in range(18):
                split_upto(min(base + e + 5, end + 3))
                if e == 17:
                    act.wait_ge(pt_psum, 24)
                    exp_rows(24, 0)
                if e < 13:
                    scale = -0.125 if e < 4 else (0.125 if 5 <= e < 9 else 1.0)
                    take_proj("cd", e, proj[:, e, :], scale)
                else:
                    take_value("cd", e)
            for h in range(H + 1):
                if 1 <= h < H:
                    act.wait_ge(pt_psum, 24 + h)
                    exp_rows(24 + h, 0)
                if h < H:
                    act.wait_ge(zabs_ready, h + 1)
                    link(nc.scalar.activation(stick_sp[h % 2], stick_sp[h % 2], ACT.Exp, scale=-1.0))
                    nc.scalar.activation(stick_sp[h % 2], stick_sp[h % 2], ACT.Ln,
                                         bias=ones[:, 0:1]).then_inc(zlog_ready, 1)
                if h >= 1:
                    act.wait_ge(fw_ready, h)
                    nc.scalar.activation(stick_w[(h - 1) % 2], stick_w[(h - 1) % 2], ACT.Exp).then_inc(w_ready, 1)
            oT_high(4)
            for e in range(18, 27):
                split_upto(min(base + e + 5, end + 3))
            norm_b(2, "cd")
            norm_a(3)
            ffn("f1", 3)
            norm_a(4)

            act.wait_ge(misc_psum, misc["mod4g"] + 1)
            base = BASE["sb"]
            end = base + SB_UNITS
            for e in range(14):
                split_upto(min(base + e + 5, end + 3))
                if e < 5:
                    take_proj("sb", e, proj[:, e, :])
                    act.wait_ge(proj_done, PROJ0["sb"] + e + 1)
                    nc.scalar.activation(tt[:, e, :], proj[:, e, :], ACT.Square).then_inc(qk_sq, 1)
                elif e == 5:
                    take_value("sb", e)
                    act.wait_ge(qk_ms, 5)
                    for n, src in enumerate((bank[2][:, :], bank[3][:, :], bank[6][:, 0:S])):
                        dst = qk_rs[n]
                        link(nc.scalar.activation(dst, src, ACT.Ln, bias=epst[:, 0:1], scale=1.0 / HD))
                        nc.scalar.activation(dst, dst, ACT.Exp, scale=-0.5).then_inc(qk_rstd, 1)
                elif e < 10:
                    take_value("sb", e, func=ACT.Gelu_apprx_tanh)
                else:
                    take_proj("sb", e, proj[:, e - 5, :], func=ACT.Gelu_apprx_tanh)
            nc.scalar.preload_act_table_set("natural_log_exp_and_others")
            exp_rows(32, 0, bank[4])
            act.wait_ge(tokv_ms, 1)
            link(nc.scalar.activation(small[:, 16:32], small[:, 0:16], ACT.Ln, bias=epst[:, 0:1], scale=1.0 / HD))
            nc.scalar.activation(small[:, 32:48], small[:, 16:32], ACT.Exp, scale=-0.5).then_inc(tokv_rstd, 1)
            for a in range(33, 40):
                if a >= 34:
                    act.wait_ge(pt_psum, a - 1)
                exp_rows(a, a % 2, bank[4 + a % 2])
            act.wait_ge(tokms, 1)
            link(nc.scalar.activation(lnms[:, :], bank[2][:, 0:S], ACT.Ln, bias=epst[:, 0:1], scale=1.0 / 512))
            nc.scalar.activation(rstd[:, :], lnms[:, :], ACT.Exp, scale=-0.5).then_inc(tokrstd, 1)
            def mix_high(n):
                b = MIX_ORDER[n]
                act.wait_ge(mixf_ready, n + 1)
                nc.scalar.activation(hHf[:, b * 512:(b + 1) * 512], mix_src(b), ACT.Copy).then_inc(mixH_ready, 1)

            mix_high(0)
            mix_high(1)
            act.wait_ge(otok_ready, 3)
            for q in range(QT):
                link(nc.scalar.activation(sn[:, q, :], otok[:, q, 0:512], ACT.Square,
                                          accum_out=small[:, 48 + q:49 + q]))
            link(nc.scalar.activation(small[:, 50:52], small[:, 48:50], ACT.Ln, bias=epst[:, 0:1], scale=1.0 / 512))
            nc.scalar.activation(small[:, 52:54], small[:, 50:52], ACT.Exp, scale=-0.5).then_inc(an_in, 1)
            mix_high(2)
            mix_high(3)
            for e in range(14, 24):
                split_upto(min(base + e + 5, end + 3))
            norm_a(5)
            ffn("f2", None)
            norm_a(6)

        @block.vector
        def _(dve):
            chain = Count(dve_done)

            def link(ins):
                chain.inc(ins)
                dve.wait_ge(chain.sem, chain.now())

            class Cursor:
                at = 0
                job = 0
            lo = Cursor()
            V = nc.vector

            def split_low(p, i=None):
                c, n = cls(p)
                slot = p % RING
                dve.wait_ge(hi_ready[c], n if i is None else i * 2 + n)
                V.tensor_tensor(wL[:, slot, :], raw[:, slot, :], wH[:, slot, :].bitcast(F32),
                                ALU.subtract).then_inc(lo_ready[c], 1)

            def split_upto(n):
                while lo.at < min(n, N_UNITS):
                    if lo.at % 3 != 2:
                        split_low(lo.at)
                    lo.at += 1

            def job(q):
                m, k, col, width = JOBS[q]
                src, landed, value = job_buffer(q)
                dve.wait_ge(landed, value)
                dst = acc0[:, col:col + width]
                cc = cvec[:, 0, :] if m < 4 else csil[:, :]
                if q >= 1:
                    dve.wait_ge(mod_used, q)
                if k == 0:
                    V.tensor_scalar(dst, src, cc[:, 0:1], None, ALU.mult).then_inc(mod_used, 1)
                else:
                    V.scalar_tensor_tensor(out=dst, in0=src, scalar=cc[:, k:k + 1], in1=dst,
                                           op0=ALU.mult, op1=ALU.add).then_inc(mod_used, 1)

            def jobs_upto(n):
                while lo.job < n:
                    job(lo.job)
                    lo.job += 1

            def take(name):
                dve.wait_ge(misc_psum, misc[name] + 1)

            def taken(ins):
                ins.then_inc(misc_taken, 1)

            def mod_vector(m, name, lo_=0, up=24):
                take(name)
                taken(V.tensor_tensor(mv[:, m, lo_:up], bank[7][:, lo_:up], modb[:, m, lo_:up], ALU.add))
                dve.wait_ge(misc_taken, misc[name] + 1)
                if lo_ == 0:
                    w = normw[:, 2 * m if m < 4 else 8 + (m - 4), :]
                    link(V.scalar_tensor_tensor(out=sc1[:, m, :], in0=mv[:, m, KT:2 * KT], scalar=1.0, in1=w,
                                                op0=ALU.add, op1=ALU.mult))
                if up == 24:
                    if m < 4:
                        link(V.tensor_tensor(gw1[:, m, :], mv[:, m, 2 * KT:24], normw[:, 2 * m + 1, :], ALU.mult))
                    else:
                        link(V.tensor_copy(gw1[:, m, :], mv[:, m, 2 * KT:24]))

            def norm_a(a):
                n = NORMS.index(f"A{a}")
                scale = sc1[:, a, :] if a < 6 else normw[:, 10, :]
                if 1 <= a < 6:
                    mod_vector(a, f"mod{a}a", 0, 16)
                dve.wait_ge(rstd_ready, n + 1)

                def lower(b):
                    dve.wait_ge(hH_ready, 4 * a + b + 1)
                    for k in range(2 * b, 2 * b + 2):
                        last = V.scalar_tensor_tensor(out=hL[:, k, :], in0=tt[:, k, :], scalar=mv[:, a, k:k + 1],
                                                      in1=hH[:, k, :].bitcast(F32), op0=ALU.add, op1=ALU.subtract)
                    last.then_inc(h_ready, 1)

                for b in range(4):
                    for k in range(2 * b, 2 * b + 2):
                        last = V.scalar_tensor_tensor(out=tt[:, k, :], in0=x[:, k, :], scalar=scale[:, k:k + 1],
                                                      in1=rstd[:, :], op0=ALU.mult, op1=ALU.mult)
                    last.then_inc(hf_ready if a < 6 else out_ready, 1)
                    if a < 6 and b >= 1:
                        lower(b - 1)
                if a < 6:
                    lower(3)
                if 1 <= a < 6:
                    mod_vector(a, f"mod{a}g", 16, 24)

            def norm_b(i, m):
                add_pairs(dve, V.tensor_tensor, f"B{i}")
                dve.wait_ge(rstd_ready, NORMS.index(f"B{i}") + 1)
                for b in range(4):
                    link(V.tensor_tensor(tt[:, 2 * b:2 * b + 2, :],
                                         bank[b][:, :].rearrange("p (k s) -> p k s", k=2),
                                         bcast(rstd[:, :].unsqueeze(1), [P, 2, S]), ALU.mult))
                    for k in range(2 * b, 2 * b + 2):
                        last = V.scalar_tensor_tensor(out=x[:, k, :], in0=tt[:, k, :], scalar=gw1[:, m, k:k + 1],
                                                      in1=x[:, k, :], op0=ALU.mult, op1=ALU.add)
                    last.then_inc(x_ready, 1)

            def residual(phase, m):
                for b in range(4):
                    wait_y(dve, phase, b)
                    for k in range(2 * b, 2 * b + 2):
                        last = V.scalar_tensor_tensor(out=x[:, k, :], in0=bank[b][:, (k % 2) * S:(k % 2 + 1) * S],
                                                      scalar=gw1[:, m, k:k + 1], in1=x[:, k, :],
                                                      op0=ALU.mult, op1=ALU.add)
                    last.then_inc(x_ready, 1)

            def values(phase, e):
                tiles, first = VALUES[phase]
                if e - 1 in tiles:
                    col = e - 1 - tiles[0]
                    n = first + col
                    dve.wait_ge(v_turned, n + 1)
                    V.tensor_copy(vt[:, :, col, :], bank[n % 2][:, 0:S].rearrange("p (q n) -> p q n", q=QT)
                                  ).then_inc(v_ready, 1)

            def neg_scores(a, strip, first=3e38):
                dve.wait_ge(scores_psum, a + 1)
                if a >= 2:
                    dve.wait_ge(prob_ready, slot_freed(a))
                bk = bank[4 + slot_of(a)]
                V.tensor_tensor_reduce(sn[:, slot_of(a), 0:P], bk[:, 0:P], strips[:, strip, P:S], 1.0, first,
                                       ALU.add, ALU.min, nm[:, a, 0:1])
                V.tensor_tensor_reduce(sn[:, slot_of(a), P:3 * P], bk[:, P:3 * P], strips[:, strip, :], 1.0, first,
                                       ALU.add, ALU.min, nm[:, a, 1:2]).then_inc(neg_ready, 1)

            def take_pt(a, width=384):
                dve.wait_ge(pt_psum, a + 1)
                if a >= 2:
                    dve.wait_ge(pv_done, slot_freed(a))
                V.tensor_copy(pt[:, slot_of(a), 0:width], bank[6 + slot_of(a)][:, 0:width]).then_inc(pt_ready, 1)

            def row_factor(a0, gate):
                link(V.reciprocal(rg[:, :, :], sm[:, a0:a0 + H, :]))
                if gate is not None:
                    gates = gt[:, :, :].rearrange("p q (h j) -> p j h q", j=3)[:, gate]
                    link(V.tensor_tensor(rg[:, :, :], rg[:, :, :], gates, ALU.mult))

            def take_o(j, a0, col, add, signal=None):
                dve.wait_ge(pv_done, a0 + H)
                for q in range(QT):
                    dst = otok[:, q, col:col + 512].rearrange("p (h d) -> p h d", d=HD)
                    src = bank[2 * (j % 2) + q][:, :].rearrange("p (h d) -> p h d", d=HD)
                    f = bcast(rg[:, :, q:q + 1], [P, H, HD])
                    if add:
                        tmp = sq[:, q, :].rearrange("p (h d) -> p h d", d=HD)
                        link(V.tensor_tensor(tmp, src, f, ALU.mult))
                        ins = V.tensor_tensor(dst, dst, tmp, ALU.add)
                    else:
                        ins = V.tensor_tensor(dst, src, f, ALU.mult)
                    if q == QT - 1 and signal is not None:
                        ins.then_inc(signal, 1)
                    else:
                        link(ins)

            def oT_low(o0):
                for b in range(4):
                    dve.wait_ge(oTH_ready, o0 + b + 1)
                    V.tensor_tensor(hLf[:, b * 512:(b + 1) * 512], bank[4 + b % 2][:, :],
                                    hHf[:, b * 512:(b + 1) * 512].bitcast(F32), ALU.subtract).then_inc(oT_ready, 1)

            def ffn(phase, m):
                base = BASE[phase]
                g0 = TILE0[phase]

                def step(t, i=None, jobs=False):
                    def at(n, per):
                        return n if i is None else i * per + n

                    b = base + 3 * (t + 1)
                    split = t < FT - 1 or base + 3 * FT < N_UNITS
                    for c in range(2):
                        if split:
                            split_low(b + c, i)
                    up = bank[4 + t % 2][:, S:2 * S]
                    if phase == "f2":
                        row = conv[:, t] if i is None else conv[:, bass.ds(i * 2 + t, 1)].rearrange("p o c -> p (o c)")
                        dve.wait_ge(zc_ready, at(t + 1, 2))
                        for n in range(2):
                            z = bank[4 + t % 2][:, n * S:(n + 1) * S]
                            dst = pr[:, t % 2, n * S:(n + 1) * S]
                            link(V.scalar_tensor_tensor(out=dst[:, 1:S], in0=z[:, 0:S - 1],
                                                        scalar=row[:, 4 * n:4 * n + 1], in1=dst[:, 1:S],
                                                        op0=ALU.mult, op1=ALU.add))
                            ins = V.scalar_tensor_tensor(out=dst[:, 0:S - 1], in0=z[:, 1:S],
                                                         scalar=row[:, 4 * n + 2:4 * n + 3], in1=dst[:, 0:S - 1],
                                                         op0=ALU.mult, op1=ALU.add)
                        ins.then_inc(conv_ready, 1)
                        up = pr[:, t % 2, S:2 * S]
                    dve.wait_ge(silu_ready, at(g0 + t + 1, 2))
                    V.tensor_tensor(sn[:, t % 2, S:2 * S], sn[:, t % 2, 0:S], up, ALU.mult).then_inc(af_ready, 1)
                    dve.wait_ge(aH_ready, at(g0 + t + 1, 2))
                    V.tensor_tensor(aL[:, t % 2, :], sn[:, t % 2, S:2 * S], aH[:, t % 2, :].bitcast(F32),
                                    ALU.subtract).then_inc(aL_ready, 1)
                    if jobs:
                        n = t % 2
                        q = JOBS_END[m - 1] + n
                        cc = cvec[:, 0] if m < 4 else csil[:, :]
                        half = acc1[:, n * MC:(n + 1) * MC]
                        dve.wait_ge(mod_full[q % 2], i * 16 + job_value(q))
                        dve.wait_ge(mod_used, i * 2 + q)
                        V.scalar_tensor_tensor(out=half, in0=modbuf[:, q % 2, :], scalar=cc[:, bass.ds(i, 1)],
                                               in1=half, op0=ALU.mult, op1=ALU.add).then_inc(mod_used, 1)

                step(0)
                step(1)
                if m is not None:
                    dve.wait_ge(acc_zero, 1 if phase == "f0" else 2)
                    dve.wait_ge(csil_ready, 1)
                per = 4 if phase == "f2" else 0
                with dve.Fori(0, 8) as i:
                    chain.enter(i, per)
                    step(2, i, m is not None)
                    step(3, i, m is not None)
                chain.leave(8)
                for t in range(18, FT):
                    step(t)
                lo.at = base + 3 * FT + 3
                if m is not None:
                    lo.job = JOBS_END[m]

            dve.wait_ge(small_landed, 32)
            link(V.tensor_scalar(nsink[:, :], param("sinks"), -1.0, None, ALU.mult))
            dve.wait_ge(gw_ready, 1)
            V.tensor_tensor(gwL[:, :, :].rearrange("p k n -> p (k n)"), param("wga"),
                            gwH[:, :, :].rearrange("p k n -> p (k n)").bitcast(F32), ALU.subtract).then_inc(gw_ready, 1)
            jobs_upto(KT)
            dve.wait_ge(early_landed, 16)
            take("table")
            taken(V.scalar_tensor_tensor(out=pt[0:16, 1, :], in0=bank[7][0:16, :], scalar=-1.0,
                                         in1=early_const("negmask", 16), op0=ALU.mult, op1=ALU.add))
            take("bc")
            link(V.tensor_scalar(bc[:, :, :, :].rearrange("p q n h -> p (q n h)"), bank[7][:, 0:S], -1.0, None,
                                 ALU.mult))
            cmask = bcast(const("cmpmask").rearrange("p (q n) -> p q n", q=QT).unsqueeze(3), [P, QT, 16, H])
            taken(V.tensor_tensor(bc[:, :, :, :], bc[:, :, :, :], cmask, ALU.add))
            jobs_upto(JOBS_AT_START)
            split_upto(3)
            mod_vector(0, "mod0a", 0, 16)

            norm_a(0)

            def compressed_input(e, n):
                dve.wait_ge(proj_done, e + 1)
                base_ap = proj[:, e, :]
                win = bass.AP(base_ap.tensor, base_ap.offset, [list(base_ap.ap[0]), [1, CLEN], [CSTR, NCMP]])
                V.tensor_tensor(sn[:, n, :].rearrange("p (l n) -> p l n", n=16)[:, :, 0:NCMP], win,
                                bcast(param("pe").unsqueeze(2), [P, CLEN, NCMP]), ALU.add).then_inc(kpe_ready, 1)

            for e in range(16):
                split_upto(min(e + 5, 27))
                if e == 1:
                    compressed_input(0, 0)
                if e == 2:
                    compressed_input(1, 1)
                if e == 4:
                    take("cmpk")
                    taken(V.tensor_copy(kcs[0:NCMP, :], bank[7][0:NCMP, 0:P]))
                if e == 6:
                    take("kcT")
                    taken(V.tensor_copy(kc[:, 0:NCMP], bank[7][:, 0:NCMP]))
                if e == 8:
                    take("cmpv")
                    taken(V.tensor_copy(vcs[0:NCMP, :], bank[7][0:NCMP, 0:P]))
                if e == 10:
                    take("vrep")
                    vcb = pt[:, 0, :].rearrange("p (h d) -> p h d", d=HD)
                    for g in range(G):
                        rep = bcast(bank[7][:, g * HD:(g + 1) * HD].unsqueeze(1), [P, H // G, HD])
                        hm = bcast(const("headmask")[:, g * 4:(g + 1) * 4].unsqueeze(2), [P, H // G, HD])
                        ins = V.tensor_tensor(vcb[:, g * 4:(g + 1) * 4, :], rep, hm, ALU.mult)
                    taken(ins)
                    mod_vector(0, "mod0g", 16, 24)
                if e == 11:
                    take("cscore")
                    s3 = sn[:, 0, 0:S].rearrange("p (r n) -> p r n", n=16)
                    for q in range(QT):
                        for g in range(G):
                            heads = slice(g * (H // G), (g + 1) * (H // G))
                            s4 = sn[:, 0, q * P:(q + 1) * P].rearrange("p (h n) -> p h n", n=16)[:, heads]
                            scores_ = bank[7 - g][:, q * HD:(q + 1) * HD].rearrange("p (h n) -> p h n", n=16)
                            ins = V.tensor_tensor(s4, scores_, bc[:, q, :, heads].rearrange("p n h -> p h n"), ALU.add)
                            taken(ins) if q == QT - 1 and g == G - 1 else link(ins)
                    dve.wait_ge(misc_taken, misc["cscore"] + 1)
                    link(V.tensor_reduce(cm[:, 0, :], s3, AX, ALU.min))
                    V.tensor_tensor(s3, s3, bcast(cm[:, 0, :].unsqueeze(2), [P, 16, 16]),
                                    ALU.subtract).then_inc(cmp_sub, 1)
                if e == 12:
                    take("gates")
                    taken(V.tensor_copy(gates_f, bank[7][0:24, 0:S]))
                    take("gatesT")
                    taken(V.tensor_copy(gt[:, :, :].rearrange("p q n -> p (q n)"), bank[7][:, 0:48]))
                if e == 13:
                    dve.wait_ge(cmp_exp, 1)
                    p3 = pr[:, 0, 0:S].rearrange("p (r n) -> p r n", n=16)
                    link(V.tensor_reduce(cm[:, 1, :], p3, AX, ALU.add))
                    link(V.reciprocal(cm[:, 2, :], cm[:, 1, :]))
                    link(V.tensor_tensor(rg[:, :, :], cm[:, 2, :].rearrange("p (q h) -> p h q", q=QT),
                                         bcast(const("rowvalid").unsqueeze(1), [P, H, QT]), ALU.mult))
                    for q in range(QT):
                        take(f"cpt{q}")
                        taken(V.tensor_copy(sn[:, 1, q * P:(q + 1) * P], bank[7][:, 0:P]))
                if e == 14:
                    dve.wait_ge(gate_exp, 1)
                    link(V.tensor_scalar(small[:, 0:48], small[:, 0:48], 1.0, None, ALU.add))
                    link(V.reciprocal(gt[:, :, :].rearrange("p q n -> p (q n)"), small[:, 0:48]))
                    link(V.tensor_tensor(rg[:, :, :], rg[:, :, :],
                                         gt[:, :, :].rearrange("p q (h j) -> p j h q", j=3)[:, 0], ALU.mult))
                if e == 15:
                    dve.wait_ge(strips_landed, 16 * (P // COPIES))
                    neg_scores(0, 0)
                if e >= 14:
                    q = e - 14
                    take(f"cpv{q}")
                    taken(V.tensor_tensor(otok[:, q, 0:512].rearrange("p (h d) -> p h d", d=HD),
                                          bank[7][:, :].rearrange("p (h d) -> p h d", d=HD),
                                          bcast(rg[:, :, q:q + 1], [P, H, HD]), ALU.mult))
                if e == 15:
                    dve.wait_ge(misc_taken, misc["cpv1"] + 1)
                values("ab", e)
                jobs_upto(jobs_done("ab", e))
            for s in range(24 + 4):
                if s == 2:
                    values("ab", 16)
                if 1 <= s < 24:
                    j = s // 8
                    strip = s % 8 + (8 if j == 2 else 0)
                    neg_scores(s, strip, nsink[:, s % 8:s % 8 + 1] if j == 2 else 3e38)
                if 1 <= s <= 24:
                    take_pt(s - 1)
                jobs_upto(jobs_done("ab", 100 + s))
                if s >= 10 and (s - 10) % 8 == 0 and s < 28:
                    j = (s - 10) // 8
                    if j < 2:
                        row_factor(8 * j, j + 1)
                        take_o(j, 8 * j, 0, True, o_taken)
                        dve.wait_ge(o_taken, j + 1)
            dve.wait_ge(neg_ready, 24)
            V.tensor_tensor(sinkx[:, :, :], nm[:, 16:24, :], bcast(param("sinks").unsqueeze(2), [P, H, QT]),
                            ALU.add).then_inc(sink_in, 1)
            dve.wait_ge(sink_exp, 1)
            dve.wait_ge(prob_ready, 24)
            link(V.tensor_tensor(sm[:, 16:24, :], sm[:, 16:24, :], sinkx[:, :, :], ALU.add))
            row_factor(16, None)
            take_o(2, 16, 512, False, otok_ready)
            oT_low(0)
            for e in range(16, 24):
                split_upto(min(e + 5, 27))
            norm_b(0, 0)
            norm_a(1)
            ffn("f0", 2)
            norm_b(1, 1)
            norm_a(2)

            base = BASE["cd"]
            end = base + CD_UNITS
            for e in range(18):
                split_upto(min(base + e + 5, end + 3))
                if e == 17:
                    neg_scores(24, 0)
                values("cd", e)
                jobs_upto(jobs_done("cd", e))
            mask = const("stickmask")

            def stick_in(h):
                dve.wait_ge(z_psum, h + 1)
                if h >= 2:
                    dve.wait_ge(fw_ready, h - 1)
                link(V.tensor_tensor(stick_z_buf[h % 2], bank[5][:, 0:384], mask, ALU.add))
                if h >= 2:
                    dve.wait_ge(suf_psum, h - 1)
                V.scalar_tensor_tensor(out=stick_sp[h % 2], in0=stick_z_buf[h % 2], scalar=-1.0,
                                       in1=stick_z_buf[h % 2], op0=ALU.mult, op1=ALU.max).then_inc(zabs_ready, 1)

            values("cd", 18)
            for s in range(H + 1):
                if 1 <= s < H:
                    neg_scores(24 + s, s)
                if s < H:
                    stick_in(s)
                if s >= 1:
                    h = s - 1
                    dve.wait_ge(suf_psum, h + 1)
                    if h >= 2:
                        dve.wait_ge(stick_pv, h - 1)
                    V.tensor_tensor(stick_w[h % 2], bank[7][:, 0:384], stick_z_buf[h % 2],
                                    ALU.add).then_inc(fw_ready, 1)
                    take_pt(24 + h)
                if s < H:
                    dve.wait_ge(zlog_ready, s + 1)
                    V.scalar_tensor_tensor(out=stick_sp[s % 2], in0=stick_z_buf[s % 2], scalar=0.0,
                                           in1=stick_sp[s % 2], op0=ALU.max, op1=ALU.add).then_inc(sp_ready, 1)
            dve.wait_ge(prob_ready, 32)
            row_factor(24, None)
            take_o(0, 24, 0, False)
            dve.wait_ge(stick_pv, H)
            V.tensor_copy(otok[:, 0, 512:1024], bank[2][:, :])
            V.tensor_copy(otok[:, 1, 512:1024], bank[3][:, :]).then_inc(otok_ready, 1)
            oT_low(4)
            for e in range(18, 27):
                split_upto(min(base + e + 5, end + 3))
                jobs_upto(min(lo.job + 1, JOBS_END[3]))
            norm_b(2, 2)
            norm_a(3)
            ffn("f1", 4)
            norm_b(3, 3)
            norm_a(4)

            base = BASE["sb"]
            end = base + SB_UNITS
            link(V.tensor_scalar(qgain[:, 0:1], param("gqk")[:, 0:1], -0.125, None, ALU.mult))
            for e in range(14):
                split_upto(min(base + e + 5, end + 3))
                values("sb", e)
                if e == 7:
                    for n, tiles in enumerate(qk_tiles):
                        flat = tiles.rearrange("p a s -> p (a s)")
                        dve.wait_ge(qk_rstd, n + 1)
                        V.scalar_tensor_tensor(out=flat, in0=flat,
                                               scalar=qgain[:, 0:1] if n < 2 else param("gqk")[:, 1:2],
                                               in1=qk_rs[n], op0=ALU.mult, op1=ALU.mult).then_inc(qk_n, 1)
                if e == 9:
                    for n, tiles in enumerate(qk_tiles):
                        w = 2 if n < 2 else 1
                        cos, sin = (bcast(const(c).unsqueeze(1), [P, w, S]) for c in ("cos", "sin"))
                        rot = pr[:, n % 2, 0:w * S].rearrange("p (a s) -> p a s", a=w)
                        src = bank[(2, 3, 6)[n]][:, 0:w * S].rearrange("p (a s) -> p a s", a=w)
                        dve.wait_ge(qk_rot, n + 1)
                        link(V.tensor_tensor(rot, src, sin, ALU.mult))
                        link(V.tensor_tensor(tiles, tiles, cos, ALU.mult))
                        V.tensor_tensor(tiles, tiles, rot, ALU.add).then_inc(qk_done, 1)
                if e == 11:
                    dve.wait_ge(v_ready, 13)
                    for q in range(QT):
                        v2 = vt[:, q, 1:5, :].rearrange("p a b -> p (a b)")
                        link(V.tensor_tensor(sn[:, q, :], v2, v2, ALU.mult))
                    V.tensor_reduce(small[:, 0:16], sn[:, :, :].rearrange("p q (h d) -> p (q h) d", d=HD), AX,
                                    ALU.add).then_inc(tokv_ms, 1)
                jobs_upto(jobs_done("sb", e))

            def token_values():
                dve.wait_ge(tokv_rstd, 1)
                for q in range(QT):
                    v3 = vt[:, q, 1:5, :].rearrange("p a b -> p (a b)").rearrange("p (h d) -> p h d", d=HD)
                    link(V.tensor_tensor(v3, v3, bcast(small[:, 32 + 8 * q:40 + 8 * q].unsqueeze(2), [P, H, HD]),
                                         ALU.mult))
                    V.tensor_tensor(v3, v3, bcast(param("gtokv").unsqueeze(1), [P, H, HD]),
                                    ALU.mult).then_inc(tokv_ready, 1)

            def token_mixed(t):
                dve.wait_ge(tok_psum, t + 1)
                u = proj[:, 5 + t, :]
                if t == 0:
                    dve.wait_ge(proj_done, PROJ0["sb"] + 14)
                bs = bcast(param("bs")[:, t * P:(t + 1) * P].unsqueeze(1), [P, QT, P])
                dst = sn[:, t % 2, 0:S]
                link(V.tensor_tensor(dst.rearrange("p (c n) -> p c n", c=QT),
                                     bank[2 + t % 2][:, 0:S].rearrange("p (c n) -> p c n", c=QT), bs, ALU.add))
                link(V.tensor_tensor(u, dst, u, ALU.mult))
                V.tensor_tensor(sq[:, t // 2, (t % 2) * S:(t % 2 + 1) * S], u, u, ALU.mult).then_inc(tok_ready, 1)

            for a in range(32, 40 + 1):
                if a < 40:
                    dve.wait_ge(scores_psum, a + 1)
                    V.tensor_reduce(nm[:, a, :], bank[4 + a % 2][:, :].rearrange("p (q n) -> p q n", q=QT), AX,
                                    ALU.min).then_inc(neg_ready, 1)
                if a >= 33:
                    take_pt(a - 1, 512)
                if a == 32:
                    token_values()
                if 33 <= a <= 36:
                    token_mixed(a - 33)
                jobs_upto(jobs_done("sb", 99 + max(0, min(a, 38) - 33)))
            gout = param("gout")
            dve.wait_ge(tokrstd, 1)
            for b in range(2):
                for k in range(2):
                    t = 2 * b + k
                    last = V.scalar_tensor_tensor(out=proj[:, 5 + t, :], in0=proj[:, 5 + t, :],
                                                  scalar=gout[:, 4 + t:5 + t], in1=rstd[:, :],
                                                  op0=ALU.mult, op1=ALU.mult)
                last.then_inc(mixf_ready, 1)

            def mix_low(n):
                b = MIX_ORDER[n]
                dve.wait_ge(mixH_ready, n + 1)
                V.tensor_tensor(hLf[:, b * 512:(b + 1) * 512], mix_src(b),
                                hHf[:, b * 512:(b + 1) * 512].bitcast(F32), ALU.subtract).then_inc(oT_ready, 1)

            dve.wait_ge(prob_ready, 40)
            row_factor(32, None)
            take_o(0, 32, 0, False, otok_ready)
            mix_low(0)
            mix_low(1)
            dve.wait_ge(an_in, 1)
            for q in range(QT):
                V.tensor_scalar(otok[:, q, 0:512], otok[:, q, 0:512], small[:, 52 + q:53 + q], None,
                                ALU.mult).then_inc(an_out, 1)
            for b in range(2):
                dve.wait_ge(oT_psum, 8 + b + 1)
                for k in range(2):
                    last = V.tensor_scalar(sn[:, b, k * S:(k + 1) * S], bank[4 + b][:, k * S:(k + 1) * S],
                                           gout[:, 2 * b + k:2 * b + k + 1], None, ALU.mult)
                last.then_inc(mixf_ready, 1)
            mix_low(2)
            mix_low(3)
            for e in range(14, 24):
                split_upto(min(base + e + 5, end + 3))
                jobs_upto(min(lo.job + 2, JOBS_END[5]))
            residual("sb", 4)
            norm_a(5)
            ffn("f2", None)
            residual("f2", 5)
            norm_a(6)

        @block.tensor
        def _(pe):
            mm = nc.tensor.matmul

            def unit_ready(p, i=None):
                c, n = cls(p)
                pe.wait_ge(lo_ready[c], n if i is None else i * 2 + n)

            def three(out, lhs_h, lhs_l, rhs_h, rhs_l, start, stop):
                mm(out, lhs_h, rhs_h, start=start, stop=False, skip_group_check=True)
                mm(out, lhs_h, rhs_l, start=False, stop=False, skip_group_check=True)
                return mm(out, lhs_l, rhs_h, start=False, stop=stop, skip_group_check=True)

            def misc_free(name):
                if misc[name] > 0:
                    pe.wait_ge(misc_taken, misc[name])

            def sum_squares(n, fill=None):
                if n >= 1:
                    pe.wait_ge(rstd_ready, n)
                for b in range(4):
                    if b >= 1 and fill is not None:
                        fill(b)
                    pe.wait_ge(pair_ready, 4 * n + b + 1)
                    mm(bank[6][:, 0:S], ones, sq[:, b % 2, 0:S], start=(b == 0), stop=(b == 3),
                       skip_group_check=True).then_inc(sq_used, 1)

            def mod_columns(cols, acc):
                for j in cols:
                    last = mm(bank[7][:, j:j + P], acc[:, j * P:(j + 1) * P], ones, start=True, stop=True,
                              skip_group_check=True)
                return last

            def mod_sum(name, cols, acc):
                misc_free(name)
                mod_columns(cols, acc).then_inc(misc_psum, 1)

            def project(phase, e, first_h=None):
                p = BASE[phase] + e
                if e >= 2:
                    pe.wait_ge(proj_done, PROJ0[phase] + e - 1)
                unit_ready(p)
                slot = p % RING
                H3 = wH[:, slot, :].rearrange("p (k n) -> p k n", k=KT)
                L3 = wL[:, slot, :].rearrange("p (k n) -> p k n", k=KT)
                out = proj_bank(phase, e)[:, 0:S]
                for k in range(KT):
                    if first_h is not None and k % 2 == 0:
                        pe.wait_ge(h_ready, first_h + k // 2 + 1)
                    last = three(out, H3[:, k], L3[:, k], hH[:, k], hL[:, k], k == 0, k == KT - 1)
                last.then_inc(unit_used[p % 3], 1)

            def turn_values(phase, e):
                tiles, first = VALUES[phase]
                if e - 1 in tiles:
                    n = first + e - 1 - tiles[0]
                    pe.wait_ge(proj_done, PROJ0[phase] + e)
                    if n - first >= 2:
                        pe.wait_ge(v_ready, n - 1)
                    for q in range(QT):
                        last = nc.tensor.transpose(bank[n % 2][:, q * P:(q + 1) * P],
                                                   sq[:, n % 2, q * P:(q + 1) * P], ident)
                    last.then_inc(v_turned, 1)

            def y_unit(phase, m, p, extra=()):
                unit_ready(p)
                slot = p % RING
                H3 = wH[:, slot, :].rearrange("p (k n) -> p k n", k=KT)
                L3 = wL[:, slot, :].rearrange("p (k n) -> p k n", k=KT)
                out = bank[m // 2][:, (m % 2) * S:(m % 2 + 1) * S]
                chunks = MIX_ORDER if phase == "sb" else range(4)
                for n, k in enumerate([2 * b + half for b in chunks for half in range(2)]):
                    if m == 0 and n % 2 == 0:
                        pe.wait_ge(oT_ready, OT0[phase] + n // 2 + 1)
                    last = three(out, H3[:, k], L3[:, k], hH[:, k], hL[:, k], n == 0, n == KT - 1)
                    if n < len(extra):
                        last.then_inc(extra[n], 1)
                last.then_inc(unit_used[p % 3], 1)

            OT0 = {"ab": 0, "cd": 4, "sb": 8}

            def transposes(a, cuts):
                pe.wait_ge(prob_ready, a + 1)
                if a >= 2:
                    pe.wait_ge(pt_ready, slot_freed(a))
                for n in range(cuts):
                    last = nc.tensor.transpose(bank[6 + slot_of(a)][:, n * P:(n + 1) * P], pr[:, slot_of(a), n * P:(n + 1) * P],
                                               ident)
                last.then_inc(pt_psum, 1)

            def pv(a, h, j, vcol):
                pe.wait_ge(pt_ready, a + 1)
                g = h // 4
                v = [vt[:, kt, vcol, g * HD:(g + 1) * HD] for kt in range(QT)]
                o = [bank[2 * (j % 2) + q][:, h * HD:(h + 1) * HD] for q in range(QT)]
                w = pt[:, slot_of(a), :]
                mm(o[0], w[:, 0:P], v[0], start=True, stop=True, skip_group_check=True)
                mm(o[1], w[:, P:2 * P], v[0], start=True, stop=False, skip_group_check=True)
                mm(o[1], w[:, 2 * P:3 * P], v[1], start=False, stop=True, skip_group_check=True).then_inc(pv_done, 1)

            def turn_otok(o0, phase_n, tiles=8):
                pe.wait_ge(otok_ready, phase_n)
                for b in range(tiles // 2):
                    if b >= 2:
                        pe.wait_ge(oT_ready, o0 + b - 1)
                    for n in range(2):
                        for q in range(QT):
                            f = 2 * b + n
                            last = nc.tensor.transpose(bank[4 + b % 2][:, n * S + q * P:n * S + (q + 1) * P],
                                                       otok[:, q, f * P:(f + 1) * P], ident)
                    last.then_inc(oT_psum, 1)

            def norm_sums(name):
                sum_squares(NORMS.index(name))

            def norm_sums_with(name, m, acc):
                pe.wait_ge(mod_used, JOBS_END[m])
                misc_free(f"mod{m}a")
                mod_columns(range(10), acc)

                def between(b):
                    last = mod_columns(range(8 + 2 * b, 10 + 2 * b), acc)
                    if b == 3:
                        last.then_inc(misc_psum, 1)

                sum_squares(NORMS.index(name), between)
                mod_sum(f"mod{m}g", range(16, 24), acc)

            def ffn(phase, a):
                base = BASE[phase]
                g0 = TILE0[phase]

                def gate_up(t, i=None, first=False):
                    def at(n, per):
                        return n if i is None else i * per + n

                    bk = bank[4 + t % 2]
                    if t >= 2:
                        if phase == "f2":
                            pe.wait_ge(conv_ready, at(t - 1, 2))
                        else:
                            pe.wait_ge(af_ready, at(g0 + t - 1, 2))
                    order = ([(n, k) for b in range(4) for n in range(2) for k in (2 * b, 2 * b + 1)] if first
                             else [(n, k) for n in range(2) for k in range(KT)])
                    for n, k in order:
                        p = base + 3 * t + n
                        if k == 0:
                            unit_ready(p, i)
                        slot = p % RING
                        H3 = wH[:, slot, :].rearrange("p (k n) -> p k n", k=KT)
                        L3 = wL[:, slot, :].rearrange("p (k n) -> p k n", k=KT)
                        if first and n == 0 and k % 2 == 0:
                            pe.wait_ge(h_ready, 4 * a + k // 2 + 1)
                        last = three(bk[:, n * S:(n + 1) * S], H3[:, k], L3[:, k], hH[:, k], hL[:, k],
                                     k == 0 and not (first and n == 1), k == KT - 1)
                        if k == KT - 1:
                            last.then_inc(unit_used[p % 3], 1)

                def down(t, i=None):
                    p = base + 3 * t + 2
                    unit_ready(p, i)
                    pe.wait_ge(aL_ready, g0 + t + 1 if i is None else i * 2 + (g0 + t + 1))
                    slot = p % RING
                    for m in range(KT):
                        out = bank[m // 2][:, (m % 2) * S:(m % 2 + 1) * S]
                        last = three(out, wH[:, slot, m * P:(m + 1) * P], wL[:, slot, m * P:(m + 1) * P],
                                     aH[:, t % 2, :], aL[:, t % 2, :], t == 0 and m % 2 == 0, t == FT - 1)
                        if t == FT - 1 and m in (1, 3, 5):
                            last.then_inc(y_ready, 1)
                    last.then_inc(unit_used[2], 1)

                gate_up(0, first=True)
                gate_up(1)
                down(0)
                with pe.Fori(0, 8) as i:
                    gate_up(2, i)
                    down(1, i)
                    gate_up(3, i)
                    down(2, i)
                for t in range(18, FT):
                    gate_up(t)
                    down(t - 1)
                down(FT - 1)

            def scores(a, h, qtile, ktile):
                r = slice((h // 4) * HD, (h // 4 + 1) * HD)
                q, k = proj[r, qtile + h % 4, :], proj[r, ktile, :]
                bk = bank[4 + slot_of(a)]
                mm(bk[:, 0:P], q[:, 0:P], k[:, 0:P], start=True, stop=True, skip_group_check=True)
                mm(bk[:, P:3 * P], q[:, P:2 * P], k, start=True, stop=True,
                   skip_group_check=True).then_inc(scores_psum, 1)

            pe.wait_ge(small_landed, 32)
            pe.wait_ge(early_landed, 16)
            mm(bank[7][0:16, :], param("reltab", REL), early_const("onehot_rel", REL), start=True,
               stop=True).then_inc(misc_psum, 1)
            misc_free("bc")
            hot = early_const("onehot_cmp").rearrange("p (g q) -> p g q", g=4)
            for q in range(QT):
                for g in range(4):
                    last = mm(bank[7][:, q * P + g * 32:q * P + (g + 1) * 32], hot[:, g, q * P:(q + 1) * P],
                              param("relblock"), start=True, stop=True, skip_group_check=True)
            last.then_inc(misc_psum, 1)
            norm_sums("A0")
            misc_free("mod0a")
            for half in range(2):
                pe.wait_ge(mod_used, KT * (half + 1))
                last = mod_columns(range(KT * half, KT * (half + 1)), acc0)
            last.then_inc(misc_psum, 1)

            def compress(name, n):
                pe.wait_ge(cw_landed, 32 * (n + 1))
                pe.wait_ge(kpe_ready, n + 1)
                misc_free(name)
                win = sn[:, n, :].rearrange("p (l n) -> p l n", n=16)
                for l in range(CLEN):
                    last = mm(bank[7][0:NCMP, 0:P], win[:, l, 0:NCMP], cw[:, :, l, :], start=(l == 0),
                              stop=(l == CLEN - 1))
                last.then_inc(misc_psum, 1)

            for e in range(16):
                if e == 15:
                    pe.wait_ge(proj_done, PROJ0["ab"] + 13)
                    scores(0, 0, ATT["ab"][0][1], ATT["ab"][0][2])
                project("ab", e, 0 if e == 0 else None)
                turn_values("ab", e)
                if e == 3:
                    compress("cmpk", 0)
                if e == 7:
                    compress("cmpv", 1)
                if e == 5:
                    misc_free("kcT")
                    nc.tensor.transpose(bank[7][:, 0:NCMP], kcs[0:NCMP, :],
                                        const("ident", NCMP)[:, 0:NCMP]).then_inc(misc_psum, 1)
                if e == 9:
                    misc_free("vrep")
                    mm(bank[7][:, 0:P], const("select", NCMP), vcs[0:NCMP, :], start=True,
                       stop=True).then_inc(misc_psum, 1)
                    pe.wait_ge(mod_used, JOBS_AT_START + KT)
                    mod_sum("mod0g", range(16, 24), acc0)
                if e == 10:
                    misc_free("cscore")
                    pe.wait_ge(proj_done, 9)
                    for g in range(G):
                        mm(bank[7 - g][:, 0:P], ident, const("stickmask")[:, P:S],
                           start=True, stop=False, skip_group_check=True)
                        r = slice(g * HD, (g + 1) * HD)
                        for q in range(QT):
                            for h in range(H // G):
                                c0 = (q * (H // G) + h) * 16
                                last = mm(bank[7 - g][:, c0:c0 + NCMP], proj[r, 5 + h, q * P:(q + 1) * P],
                                          kc[r, 0:NCMP], start=False, stop=True, skip_group_check=True)
                    last.then_inc(misc_psum, 1)
                if e == 11:
                    misc_free("gates")
                    pe.wait_ge(gw_ready, 2)
                    for k in range(KT):
                        last = three(bank[7][0:24, 0:S], gwH[:, k], gwL[:, k], hH[:, k], hL[:, k],
                                     k == 0, k == KT - 1)
                    last.then_inc(misc_psum, 1)
                if e == 12:
                    misc_free("gatesT")
                    for q in range(QT):
                        last = nc.tensor.transpose(bank[7][:, q * 24:(q + 1) * 24], gates_f[:, q * P:(q + 1) * P],
                                                   const("ident", 24)[:, 0:24])
                    last.then_inc(misc_psum, 1)
                    for q in range(QT):
                        misc_free(f"cpt{q}")
                        pe.wait_ge(cmp_exp, 1)
                        nc.tensor.transpose(bank[7][:, 0:P], pr[:, 0, q * P:(q + 1) * P],
                                            ident).then_inc(misc_psum, 1)
                if e >= 14:
                    q = e - 14
                    if e == 15:
                        pe.wait_ge(proj_done, PROJ0["ab"] + 14)
                        scores(1, 1, ATT["ab"][0][1], ATT["ab"][0][2])
                    misc_free(f"cpv{q}")
                    mm(bank[7][:, :], sn[:, 1, q * P:(q + 1) * P], pt[:, 0, :], start=True,
                       stop=True).then_inc(misc_psum, 1)
            turn_values("ab", 16)

            def attention(phase):
                atts = ATT[phase]
                a0 = atts[0][0]
                n = 8 * len(atts)
                for s in range(n + 2):
                    if s < n:
                        j, h = s // 8, s % 8
                        if s == 0:
                            pe.wait_ge(proj_done, PROJ0[phase] + NPROJ[phase])
                        if s >= 2:
                            pe.wait_ge(neg_ready, a0 + s - 1)
                        if s >= 2:
                            scores(a0 + s, h, atts[j][1], atts[j][2])
                    if 1 <= s <= n:
                        if s == 2 and phase == "ab":
                            pe.wait_ge(misc_taken, misc["cpv1"] + 1)
                        transposes(a0 + s - 1, 3)
                    if s == 2:
                        pe.wait_ge(v_ready, VALUES[phase][1] + len(VALUES[phase][0]))
                    if s >= 2:
                        a = s - 2
                        j, h = a // 8, a % 8
                        if j == 2 and h == 0:
                            pe.wait_ge(o_taken, 1)
                        pv(a0 + a, h, j, atts[j][3])

            attention("ab")
            turn_otok(0, 1)
            for m in range(KT):
                y_unit("ab", m, 16 + m)
            norm_sums("B0")
            norm_sums_with("A1", 1, acc0)
            ffn("f0", 1)
            norm_sums("B1")
            norm_sums_with("A2", 2, acc1)

            base = BASE["cd"]
            for e in range(18):
                if e == 17:
                    pe.wait_ge(proj_done, PROJ0["cd"] + 15)
                    scores(24, 0, 0, 4)
                project("cd", e, 8 if e == 0 else None)
                turn_values("cd", e)

            def stick_z(h):
                r = slice((h % 2) * HD, (h % 2 + 1) * HD)
                q, k = proj[r, 5 + h // 2, :], proj[r, 9 + h // 2, :]
                bk = bank[5]
                if h >= 1:
                    pe.wait_ge(zabs_ready, h)
                mm(bk[:, 0:S], k[:, 0:P], q, start=True, stop=True, skip_group_check=True)
                mm(bk[:, S:3 * P], k[:, P:S], q[:, P:S], start=True, stop=True,
                   skip_group_check=True).then_inc(z_psum, 1)

            def stick_suffix(h):
                pe.wait_ge(sp_ready, h + 1)
                if h >= 1:
                    pe.wait_ge(fw_ready, h)
                bk, w = bank[7], stick_sp[h % 2]
                mm(bk[:, S:3 * P], const("tri"), w[:, S:3 * P], start=True, stop=True, skip_group_check=True)
                mm(bk[:, 0:S], const("tri"), w[:, 0:S], start=True, stop=False, skip_group_check=True)
                mm(bk[:, P:S], const("neg1"), w[:, S:3 * P], start=False, stop=True,
                   skip_group_check=True).then_inc(suf_psum, 1)

            def stick_out(h):
                pe.wait_ge(w_ready, h + 1)
                v = [vt[:, kt, 1 + h // 2, (h % 2) * HD:(h % 2 + 1) * HD] for kt in range(QT)]
                o = [bank[2 + q][:, h * HD:(h + 1) * HD] for q in range(QT)]
                w = stick_w[h % 2]
                mm(o[0], w[:, 0:P], v[0], start=True, stop=True, skip_group_check=True)
                mm(o[1], w[:, P:S], v[0], start=True, stop=False, skip_group_check=True)
                mm(o[1], w[:, S:3 * P], v[1], start=False, stop=True, skip_group_check=True).then_inc(stick_pv, 1)

            pe.wait_ge(proj_done, PROJ0["cd"] + 16)
            stick_z(0)
            turn_values("cd", 18)
            for s in range(H + 2):
                if 1 <= s < H:
                    pe.wait_ge(neg_ready, 24 + s)
                    scores(24 + s, s, 0, 4)
                    stick_z(s)
                if 1 <= s <= H:
                    if s == 1:
                        pe.wait_ge(misc_taken, misc["mod2g"] + 1)
                    transposes(24 + s - 1, 3)
                    stick_suffix(s - 1)
                if s == 2:
                    pe.wait_ge(v_ready, VALUES["cd"][1] + 5)
                if s >= 2:
                    pv(24 + s - 2, s - 2, 0, 0)
                    stick_out(s - 2)
            turn_otok(4, 2)
            for m in range(KT):
                y_unit("cd", m, base + 18 + m, (unit_used[2],) if m == 7 else ())
            norm_sums("B2")
            norm_sums_with("A3", 3, acc0)
            ffn("f1", 3)
            norm_sums("B3")
            norm_sums_with("A4", 4, acc1)

            base = BASE["sb"]
            for e in range(14):
                project("sb", e, 16 if e == 0 else None)
                turn_values("sb", e)
                if 1 <= e <= 5:
                    pe.wait_ge(qk_sq, e)
                    out = bank[(2, 2, 3, 3, 6)[e - 1]][:, ((e - 1) % 2) * S:((e - 1) % 2 + 1) * S]
                    mm(out, const("blockones"), tt[:, e - 1, :], start=True, stop=True,
                       skip_group_check=True).then_inc(qk_ms, 1)
                if e == 8:
                    for n, tiles in enumerate(qk_tiles):
                        w = 2 if n < 2 else 1
                        pe.wait_ge(qk_n, n + 1)
                        mm(bank[(2, 3, 6)[n]][:, 0:w * S], const("rot"), tiles.rearrange("p a s -> p (a s)"),
                           start=True, stop=True).then_inc(qk_rot, 1)
            turn_values("sb", 14)

            def token_mix(t):
                if t == 0:
                    pe.wait_ge(wst_landed, 16)
                    pe.wait_ge(tokv_ready, 2)
                if t >= 2:
                    pe.wait_ge(tok_ready, t - 1)
                for n in range(2):
                    h = 2 * t + n
                    for c in range(QT):
                        last = mm(bank[2 + t % 2][n * HD:(n + 1) * HD, c * P:(c + 1) * P],
                                  vt[:, c, 1 + t, n * HD:(n + 1) * HD], wst[:, h, :], start=True, stop=True,
                                  skip_group_check=True)
                last.then_inc(tok_psum, 1)

            a0 = 32
            for s in range(H + 2):
                if s < H:
                    a = a0 + s
                    r = slice((s // 4) * HD, (s // 4 + 1) * HD)
                    q, k = proj[r, s % 4, :], proj[r, 4, :]
                    if s == 0:
                        pe.wait_ge(qk_done, 3)
                        pe.wait_ge(proj_done, PROJ0["sb"] + 14)
                    if s >= 2:
                        pe.wait_ge(prob_ready, a - 1)
                    mm(bank[4 + a % 2][:, 0:S], q[:, 0:P], k, start=True, stop=True, skip_group_check=True)
                    mm(bank[4 + a % 2][:, S:2 * S], q[:, P:S], k, start=True, stop=True,
                       skip_group_check=True).then_inc(scores_psum, 1)
                if 1 <= s <= H:
                    transposes(a0 + s - 1, 4)
                if 1 <= s <= 4:
                    token_mix(s - 1)
                if s == 6:
                    pe.wait_ge(tok_ready, 4)
                    for t in range(4):
                        last = mm(bank[2][:, 0:S], ones, sq[:, t // 2, (t % 2) * S:(t % 2 + 1) * S], start=(t == 0),
                                  stop=(t == 3))
                    last.then_inc(tokms, 1)
                if s >= 2:
                    h = s - 2
                    a = a0 + h
                    pe.wait_ge(pt_ready, a + 1)
                    g = h // 4
                    for q in range(QT):
                        for kt in range(QT):
                            last = mm(bank[q][:, h * HD:(h + 1) * HD], pt[:, a % 2, (2 * q + kt) * P:(2 * q + kt + 1) * P],
                                      vt[:, kt, 0, g * HD:(g + 1) * HD], start=(kt == 0), stop=(kt == 1),
                                      skip_group_check=True)
                    last.then_inc(pv_done, 1)
            pe.wait_ge(an_out, 2)
            for b in range(2):
                for n in range(2):
                    for q in range(QT):
                        f = 2 * b + n
                        last = nc.tensor.transpose(bank[4 + b][:, n * S + q * P:n * S + (q + 1) * P],
                                                   otok[:, q, f * P:(f + 1) * P], ident)
                last.then_inc(oT_psum, 1)
            for m in range(KT):
                y_unit("sb", m, base + 14 + m, (unit_used[1], unit_used[2]) if m == 7 else ())
            norm_sums_with("A5", 5, acc0)
            ffn("f2", 5)
            norm_sums("A6")


def kernel(**inputs):
    import concourse.bacc as _bacc
    from concourse.bass_utils import run_bass_kernel_spmd as _run

    a = {k: np.asarray(v) for k, v in inputs.items()}
    heads = [n for t in range(4) for n in (t, t + 4)]
    paired = np.concatenate([np.arange(h * HD, (h + 1) * HD) for h in heads])

    units = np.zeros((N_UNITS, P, UW), np.float32)

    def columns(at, w, cols):
        for n in range(len(cols) // P):
            sel = w[:, cols[n * P:(n + 1) * P]]
            units[at + n] = sel.reshape(KT, P, P).transpose(1, 0, 2).reshape(P, UW)
        return at + len(cols) // P

    r = np.arange
    w = a["w_in_ab"][0]
    cuts = dict(zip(("qa", "kc", "vc", "ks", "vs", "kw", "vw", "ga", "qb", "kb", "vb"),
                    np.cumsum([0, 512, 128, 128, 128, 128, 128, 128, 24, 512, 128])))
    p = BASE["ab"]
    for name in ("kc", "vc", "ks", "kw", "kb"):
        p = columns(p, w, cuts[name] + r(P))
    for name in ("qa", "qb"):
        p = columns(p, w, cuts[name] + paired)
    for name in ("vs", "vw", "vb"):
        p = columns(p, w, cuts[name] + r(P))
    columns(p, a["w_out_ab"][0], r(D))
    wga = w[:, cuts["ga"]:cuts["ga"] + 24]
    w = a["w_in_cd"][0]
    p = columns(BASE["cd"], w, paired)
    p = columns(p, w, 512 + r(P))
    p = columns(p, w, 768 + r(1024))
    p = columns(p, w, 640 + r(P))
    p = columns(p, w, 1792 + r(512))
    columns(p, a["w_out_cd"][0], r(D))
    w = a["w_in_2"][0]
    p = columns(BASE["sb"], w, paired)
    p = columns(p, w, 512 + r(P))
    p = columns(p, w, 640 + r(P))
    p = columns(p, w, 1280 + r(512))
    p = columns(p, w, 768 + r(512))
    columns(p, a["w_out_2"][0], r(D))
    for name, wi, wo in (("f0", a["ffn_w_in"][0], a["ffn_w_out"][0]), ("f1", a["ffn_w_in"][1], a["ffn_w_out"][1]),
                         ("f2", a["w_up_2"][0], a["w_down_2"][0])):
        for t in range(FT):
            columns(BASE[name] + 3 * t, wi, t * P + r(P))
            columns(BASE[name] + 3 * t + 1, wi, FF + t * P + r(P))
            units[BASE[name] + 3 * t + 2] = wo[t * P:(t + 1) * P]

    def tiles(v):
        return v.reshape(-1, P).T

    params = np.zeros((P, PARAM_COLS), np.float32)

    def put(name, v, rows=P, at=0):
        c0 = PARAM[name][0] + at
        params[:rows, c0:c0 + v.shape[1]] = v

    put("c", tiles(a["c"][0]))
    put("c", tiles(a["c_2"][0]), at=KT)
    for m in range(4):
        put("modb", tiles(a["mod_b"][m // 2, m % 2]), at=24 * m)
    put("modb", tiles(a["b_ada_2"][0]), at=96)
    put("normw", tiles(a["norm_w"].reshape(-1)))
    put("normw", tiles(a["g_norm1_2"][0]), at=64)
    put("normw", tiles(a["g_norm2_2"][0]), at=72)
    put("normw", tiles(a["g_final_2"]), at=80)
    put("gout", tiles(a["g_attn_out_2"][0]))
    put("gout", tiles(a["g_tok_out_2"][0]), at=4)
    put("gqk", np.tile(a["g_q_2"][0], 2)[:, None])
    put("gqk", np.tile(a["g_k_2"][0], 2)[:, None], at=1)
    put("gtokv", np.tile(a["g_tok_v_2"], (P, 1)))
    put("sinks", np.tile(a["swa_sinks"], (P, 1)))
    put("pe", np.tile(a["nsa_cmp_pe"][0].T, (2, 1)))
    put("wga", wga.reshape(KT, P, 24).transpose(1, 0, 2).reshape(P, -1))
    cw = np.concatenate([a["w_conv_2"][0], a["b_conv_2"]], 0)
    cw = cw.reshape(4, 2, FT, P).transpose(3, 2, 1, 0)
    put("conv", cw.reshape(P, -1))
    bs = a["b_s_2"][0].reshape(4, 2, P)
    put("bs", np.repeat(bs.transpose(1, 0, 2), HD, 0).reshape(P, -1))
    put("reltab", a["rel_table"], REL)
    blk = np.zeros((4, REL, 4, H), np.float32)
    for n in range(4):
        blk[n, :, n, :] = a["rel_table"][:, :H]
    put("relblock", blk.reshape(P, 32))
    consts, early = shape_constants()
    arrays = {
        "weights": units,
        "mod_w": np.ascontiguousarray(a["mod_w"].reshape(4, D, MW)),
        "w_ada": np.ascontiguousarray(a["w_ada_2"][0]),
        "params": params,
        "consts": consts,
        "early": early,
        "xT": np.ascontiguousarray(a["x"][0].T.reshape(KT, P, S).transpose(1, 0, 2)),
        "cmp_w": np.ascontiguousarray(np.stack([a["nsa_cmp_wk"][0].transpose(1, 0, 2),
                                                a["nsa_cmp_wv"][0].transpose(1, 0, 2)])),
        "w_s": np.ascontiguousarray(a["w_s_2"][0].transpose(2, 0, 1)),
    }
    nc = _bacc.Bacc("TRN2", target_bir_lowering=False, num_devices=1)
    aps = {n: nc.dram_tensor(f"in_{n}", v.shape, F32, kind="ExternalInput").ap() for n, v in arrays.items()}
    aps["table"] = nc.dram_tensor("bias_table", (COPIES, 16, 512), F32, kind="Internal").ap()
    aps["out"] = nc.dram_tensor("out_dram", (P, KT, S), F32, kind="ExternalOutput").ap()
    build_program(nc, aps)
    res = _run(nc, [{f"in_{n}": v for n, v in arrays.items()}], core_ids=[0])
    y = res.results[0]["out_dram"]
    return np.ascontiguousarray(y.transpose(1, 0, 2).reshape(D, S).T)[None]
```
